# Optimizing a Trainium2 kernel written in Bass

```python
import jax, jax.numpy as jnp
from jax import lax
import numpy as np
import math
import jax
import jax.numpy as jnp

D_MODEL = 1024
BATCH = 1
SEQ = 256
DEPTH = 2

N_MIXERS = 2
N_HEADS = 16
HEAD_DIM = D_MODEL // N_HEADS
MOBA_BLOCK = 256
MOBA_TOPK = 3
Q_CHUNK = 32
ROPE_THETA = 10000.0
CONV_WIDTH = 3
D_FF = 2816
RMS_EPS = 1e-6
NEG_INF = -1e30
N_CONV_LAYERS = (DEPTH + 1) // 2
N_ATTN_LAYERS = DEPTH // 2


def rmsnorm(x, g):
    xf = x.astype(jnp.float32)
    var = jnp.mean(xf * xf, axis=-1, keepdims=True)
    return (xf * lax.rsqrt(var + RMS_EPS)).astype(x.dtype) * g

def causal_dwconv(x, w):
    S = x.shape[1]
    xp = jnp.pad(x, ((0, 0), (CONV_WIDTH - 1, 0), (0, 0)))
    y = xp[:, 0:S] * w[0]
    for j in range(1, CONV_WIDTH):
        y = y + xp[:, j:j + S] * w[j]
    return y

def short_conv_mixer(h, w_in, w_conv, w_out):
    bcv = h @ w_in
    b, c, v = jnp.split(bcv, 3, axis=-1)
    return (b * causal_dwconv(c * v, w_conv)) @ w_out

def rope(x, pos):
    half = HEAD_DIM // 2
    inv = ROPE_THETA ** (-jnp.arange(half, dtype=jnp.float32) / half)
    ang = pos.astype(jnp.float32)[:, None] * inv[None, :]
    cos = jnp.cos(ang).astype(x.dtype)
    sin = jnp.sin(ang).astype(x.dtype)
    x1, x2 = x[..., :half], x[..., half:]
    return jnp.concatenate([x1 * cos - x2 * sin, x2 * cos + x1 * sin], axis=-1)

def moba_attention(h, w_qkv, w_o):
    Bsz, S, _ = h.shape
    qkv = (h @ w_qkv).reshape(Bsz, S, 3, N_HEADS, HEAD_DIM)
    q = jnp.transpose(qkv[:, :, 0], (0, 2, 1, 3))
    k = jnp.transpose(qkv[:, :, 1], (0, 2, 1, 3))
    v = jnp.transpose(qkv[:, :, 2], (0, 2, 1, 3))
    pos = jnp.arange(S, dtype=jnp.int32)
    q = rope(q, pos) * (HEAD_DIM ** -0.5)
    k = rope(k, pos)

    n_blocks = -(-S // MOBA_BLOCK)
    pad = n_blocks * MOBA_BLOCK - S
    k = jnp.pad(k, ((0, 0), (0, 0), (0, pad), (0, 0)))
    v = jnp.pad(v, ((0, 0), (0, 0), (0, pad), (0, 0)))
    k_blocks = k.reshape(Bsz, N_HEADS, n_blocks, MOBA_BLOCK, HEAD_DIM)
    v_blocks = v.reshape(Bsz, N_HEADS, n_blocks, MOBA_BLOCK, HEAD_DIM)
    k_mean = jnp.mean(k_blocks.astype(jnp.float32), axis=3).astype(k.dtype)

    topk = min(MOBA_TOPK, n_blocks)
    b_idx = jnp.arange(Bsz)[:, None, None, None]
    h_idx = jnp.arange(N_HEADS)[None, :, None, None]
    block_ids = jnp.arange(n_blocks)
    key_off = jnp.arange(MOBA_BLOCK)
    q_off = jnp.arange(Q_CHUNK)

    def chunk(c):
        q0 = c * Q_CHUNK
        qc = lax.dynamic_slice_in_dim(q, q0, Q_CHUNK, axis=2)
        qpos = q0 + q_off
        own = q0 // MOBA_BLOCK
        gate = jnp.einsum('bhqd,bhnd->bhqn', qc, k_mean).astype(jnp.float32)
        gate = jnp.where((block_ids < own)[None, None, None, :], gate, NEG_INF)
        _, top_i = lax.top_k(gate, topk)
        rank_valid = jnp.arange(topk) < jnp.minimum(own, MOBA_TOPK)
        kg = k_blocks[b_idx, h_idx, top_i]
        vg = v_blocks[b_idx, h_idx, top_i]
        s_sel = jnp.einsum('bhqd,bhqnjd->bhqnj', qc, kg).astype(jnp.float32)
        s_sel = jnp.where(rank_valid[:, None], s_sel, NEG_INF)
        s_sel = s_sel.reshape(Bsz, N_HEADS, Q_CHUNK, topk * MOBA_BLOCK)
        ko = lax.dynamic_slice_in_dim(k, own * MOBA_BLOCK, MOBA_BLOCK, axis=2)
        vo = lax.dynamic_slice_in_dim(v, own * MOBA_BLOCK, MOBA_BLOCK, axis=2)
        s_own = jnp.einsum('bhqd,bhjd->bhqj', qc, ko).astype(jnp.float32)
        kpos = own * MOBA_BLOCK + key_off
        s_own = jnp.where(kpos[None, :] <= qpos[:, None], s_own, NEG_INF)
        p = jax.nn.softmax(jnp.concatenate([s_sel, s_own], axis=-1), axis=-1).astype(v.dtype)
        p_sel = p[..., :topk * MOBA_BLOCK].reshape(Bsz, N_HEADS, Q_CHUNK, topk, MOBA_BLOCK)
        p_own = p[..., topk * MOBA_BLOCK:]
        return (jnp.einsum('bhqnj,bhqnjd->bhqd', p_sel, vg)
                + jnp.einsum('bhqj,bhjd->bhqd', p_own, vo))

    o = lax.map(chunk, jnp.arange(S // Q_CHUNK))
    o = jnp.transpose(o, (1, 0, 3, 2, 4)).reshape(Bsz, S, N_HEADS * HEAD_DIM)
    return o @ w_o

def conv_ffn(h, w_up, w_conv, w_down):
    gu = causal_dwconv(h @ w_up, w_conv)
    g, u = jnp.split(gu, 2, axis=-1)
    return (jax.nn.silu(g) * u) @ w_down

def first_inputs(seed: int = 0) -> dict:
    key = jax.random.key(seed)
    ks = jax.random.split(key, 16)
    D = D_MODEL
    f32 = jnp.float32

    def nrm(k, shape, scale):
        return jax.random.normal(k, shape, dtype=f32) * scale

    return {
        "x": nrm(ks[0], (BATCH, SEQ, D), 1.0),
        "mix_norm": 1.0 + nrm(ks[1], (DEPTH, D), 0.02),
        "sc_w_in": nrm(ks[2], (N_CONV_LAYERS, D, 3 * D), D ** -0.5),
        "sc_w_conv": nrm(ks[3], (N_CONV_LAYERS, CONV_WIDTH, D), CONV_WIDTH ** -0.5),
        "sc_w_out": nrm(ks[4], (N_CONV_LAYERS, D, D), D ** -0.5),
        "moba_w_qkv": nrm(ks[5], (N_ATTN_LAYERS, D, 3 * D), D ** -0.5),
        "moba_w_o": nrm(ks[6], (N_ATTN_LAYERS, D, D), D ** -0.5),
        "ffn_norm": 1.0 + nrm(ks[7], (DEPTH, D), 0.02),
        "ffn_w_up": nrm(ks[8], (DEPTH, D, 2 * D_FF), D ** -0.5),
        "ffn_w_conv": nrm(ks[9], (DEPTH, CONV_WIDTH, 2 * D_FF), CONV_WIDTH ** -0.5),
        "ffn_w_down": nrm(ks[10], (DEPTH, D_FF, D), D_FF ** -0.5),
        "final_norm": 1.0 + nrm(ks[11], (D,), 0.02),
    }

def first_block(x, mix_norm, sc_w_in, sc_w_conv, sc_w_out, moba_w_qkv, moba_w_o,
              ffn_norm, ffn_w_up, ffn_w_conv, ffn_w_down, final_norm):
    for i in range(DEPTH):
        h = rmsnorm(x, mix_norm[i])
        j = i // N_MIXERS
        if i % N_MIXERS == 0:
            x = x + short_conv_mixer(h, sc_w_in[j], sc_w_conv[j], sc_w_out[j])
        else:
            x = x + moba_attention(h, moba_w_qkv[j], moba_w_o[j])
        x = x + conv_ffn(rmsnorm(x, ffn_norm[i]), ffn_w_up[i], ffn_w_conv[i], ffn_w_down[i])
    return rmsnorm(x, final_norm)


DEPTH_2 = 1

HEAD_DIM_2 = 64
Q_BLOCK = 128
EPS = 1e-6
NEG = -1e30
FORCE_SCORE = 1e4

SB_HEADS = 8
SB_W = SB_HEADS * HEAD_DIM_2
NSA_HEADS = 8
NSA_GROUPS = 2
NSA_HPG = NSA_HEADS // NSA_GROUPS
NSA_W = NSA_HEADS * HEAD_DIM_2
NSA_KV_W = NSA_GROUPS * HEAD_DIM_2
CMP_LEN = 32
CMP_STRIDE = 16
SEL_BLOCK = 64
SEL_TOPN = 4
WINDOW = 256
HGRN_HEADS = 4
HGRN_DK = 128
HGRN_DV = 128
HGRN_K_W = HGRN_HEADS * HGRN_DK
HGRN_V_W = HGRN_HEADS * HGRN_DV
HGRN_CHUNK = 64
N_BRANCH = 3
IN_SPLITS = (SB_W, SB_W, SB_W, NSA_W, 6 * NSA_KV_W, 3 * NSA_HEADS, HGRN_K_W, HGRN_K_W, HGRN_V_W, HGRN_V_W, N_BRANCH * D_MODEL)
IN_WIDTH = sum(IN_SPLITS)
PEER_HEADS = 8
PEER_NKEYS = 128
PEER_EXPERTS = PEER_NKEYS * PEER_NKEYS
PEER_TOPK = 16
PEER_QDIM = 128
PEER_TOK_CHUNK = 128


def rms_norm(x, g):
    xf = x.astype(jnp.float32)
    y = xf * lax.rsqrt(jnp.mean(xf * xf, axis=-1, keepdims=True) + EPS)
    return (y * g.astype(jnp.float32)).astype(x.dtype)

def alibi_slopes(n_heads):
    return jnp.exp2(-8.0 * (jnp.arange(n_heads, dtype=jnp.float32) + 1.0) / n_heads)

def stick_breaking_attention(q, k, v):
    B, H, T, dh = q.shape
    scale = dh ** -0.5
    outs = []
    for i in range(T // Q_BLOCK):
        q0 = i * Q_BLOCK
        kl = q0 + Q_BLOCK
        z = jnp.einsum("bhtd,bhsd->bhts", q[:, :, q0:kl], k[:, :, :kl]).astype(jnp.float32) * scale
        before = jnp.arange(kl)[None, :] < (q0 + jnp.arange(Q_BLOCK))[:, None]
        log_1m = jnp.where(before, jax.nn.log_sigmoid(-z), 0.0)
        after = lax.cumsum(log_1m, axis=3, reverse=True) - log_1m
        a = jnp.where(before, jnp.exp(jax.nn.log_sigmoid(z) + after), 0.0)
        outs.append(jnp.einsum("bhts,bhsd->bhtd", a.astype(v.dtype), v[:, :, :kl]))
    return jnp.concatenate(outs, axis=2)

def nsa_attention(q, k_cmp, v_cmp, k_sel, v_sel, k_win, v_win, gates, w_cmp_k, w_cmp_v, cmp_pe):
    B, G, P, T, dh = q.shape
    f32 = jnp.float32
    scale = dh ** -0.5
    slopes = alibi_slopes(G * P).reshape(G, P)
    t_pos = jnp.arange(T)

    n_piece = T // CMP_STRIDE
    per = CMP_LEN // CMP_STRIDE
    n_cmp = n_piece - per + 1

    def compress(x, w):
        pieces = x.reshape(B, G, n_piece, CMP_STRIDE, dh)
        blocks = jnp.concatenate([pieces[:, :, j:j + n_cmp] for j in range(per)], axis=3) + cmp_pe
        return blocks.reshape(B, G, n_cmp, CMP_LEN * dh) @ w

    kc = compress(k_cmp, w_cmp_k)
    vc = compress(v_cmp, w_cmp_v)
    c_start = jnp.arange(n_cmp) * CMP_STRIDE
    dist_c = t_pos[:, None] - (c_start + CMP_LEN - 1)[None, :]
    valid_c = dist_c >= 0
    s_c = jnp.einsum("bgptd,bgcd->bgptc", q, kc).astype(f32) * scale - slopes[:, :, None, None] * dist_c.astype(f32)
    p_c = jnp.where(valid_c, jax.nn.softmax(jnp.where(valid_c, s_c, NEG), axis=-1), 0.0)
    o_c = jnp.einsum("bgptc,bgcd->bgptd", p_c.astype(vc.dtype), vc)

    n_blk = T // SEL_BLOCK
    n_sel = min(SEL_TOPN, n_blk)
    b_start = jnp.arange(n_blk) * SEL_BLOCK
    overlap = ((c_start[:, None] < b_start[None, :] + SEL_BLOCK) & (c_start[:, None] + CMP_LEN > b_start[None, :])).astype(f32)
    imp = jnp.einsum("bgptc,cn->bgtn", p_c, overlap)
    bid = jnp.arange(n_blk)
    forced = (bid[None, :] == (t_pos // SEL_BLOCK)[:, None]) | (bid[None, :] == 0)
    causal_b = b_start[None, :] <= t_pos[:, None]
    imp = jnp.where(forced, FORCE_SCORE, jnp.where(causal_b, imp, NEG))
    _, sel_idx = lax.top_k(imp, n_sel)

    kblk = k_sel.reshape(B, G, n_blk, SEL_BLOCK, dh)
    vblk = v_sel.reshape(B, G, n_blk, SEL_BLOCK, dh)
    nq = T // Q_BLOCK
    q_chunks = jnp.moveaxis(q.reshape(B, G, P, nq, Q_BLOCK, dh), 3, 0)
    idx_chunks = jnp.moveaxis(sel_idx.reshape(B, G, nq, Q_BLOCK, n_sel), 2, 0)
    bi = jnp.arange(B)[:, None, None, None]
    gi = jnp.arange(G)[None, :, None, None]
    n_keys_sel = n_sel * SEL_BLOCK

    def sel_chunk(args):
        qc, ic, c = args
        kg = kblk[bi, gi, ic].reshape(B, G, Q_BLOCK, n_keys_sel, dh)
        vg = vblk[bi, gi, ic].reshape(B, G, Q_BLOCK, n_keys_sel, dh)
        pos = (ic[..., None] * SEL_BLOCK + jnp.arange(SEL_BLOCK)).reshape(B, G, Q_BLOCK, n_keys_sel)
        dist = (c * Q_BLOCK + jnp.arange(Q_BLOCK))[:, None] - pos
        sc = jnp.einsum("bgpqd,bgqsd->bgpqs", qc, kg).astype(f32) * scale - slopes[None, :, :, None, None] * dist[:, :, None].astype(f32)
        pr = jax.nn.softmax(jnp.where(dist[:, :, None] >= 0, sc, NEG), axis=-1)
        return jnp.einsum("bgpqs,bgqsd->bgpqd", pr.astype(vg.dtype), vg)

    o_s = lax.map(sel_chunk, (q_chunks, idx_chunks, jnp.arange(nq)))
    o_s = jnp.moveaxis(o_s, 0, 3).reshape(B, G, P, T, dh)

    nb = T // Q_BLOCK
    nwb = WINDOW // Q_BLOCK
    span = (nwb + 1) * Q_BLOCK

    def band(x):
        xb = jnp.pad(x.reshape(B, G, nb, Q_BLOCK, dh), ((0, 0), (0, 0), (nwb, 0), (0, 0), (0, 0)))
        return jnp.concatenate([xb[:, :, j:j + nb] for j in range(nwb + 1)], axis=3)

    kwb = band(k_win)
    vwb = band(v_win)
    tq = t_pos.reshape(nb, Q_BLOCK)
    sk = jnp.arange(nb)[:, None] * Q_BLOCK - nwb * Q_BLOCK + jnp.arange(span)[None, :]
    dist_w = tq[:, :, None] - sk[:, None, :]
    valid_w = (dist_w >= 0) & (dist_w < WINDOW) & (sk[:, None, :] >= 0)
    s_w = jnp.einsum("bgpnqd,bgnsd->bgpnqs", q.reshape(B, G, P, nb, Q_BLOCK, dh), kwb).astype(f32) * scale - slopes[:, :, None, None, None] * dist_w.astype(f32)
    p_w = jax.nn.softmax(jnp.where(valid_w, s_w, NEG), axis=-1)
    o_w = jnp.einsum("bgpnqs,bgnsd->bgpnqd", p_w.astype(vwb.dtype), vwb).reshape(B, G, P, T, dh)

    g = jax.nn.sigmoid(gates.astype(f32)).reshape(B, T, G, P, 3).transpose(4, 0, 2, 3, 1)
    o = g[0][..., None] * o_c + g[1][..., None] * o_s + g[2][..., None] * o_w
    return o.astype(q.dtype)

def hgrn2_recurrence(q, log_f, k, i):
    B, H, T, dk = q.shape
    dv = i.shape[-1]
    C = HGRN_CHUNK
    nc = T // C

    def to_chunks(x):
        return jnp.moveaxis(x.reshape(B, H, nc, C, x.shape[-1]), 2, 0)

    causal = jnp.tril(jnp.ones((C, C), dtype=bool))

    def step(S, inp):
        qc, gc, kc, ic = inp
        b = jnp.cumsum(gc, axis=2)
        o_inter = jnp.einsum("bhtk,bhkv->bhtv", qc * jnp.exp(b), S)
        rel = b[:, :, :, None, :] - b[:, :, None, :, :]
        decay = jnp.exp(jnp.where(causal[:, :, None], rel, -jnp.inf))
        att = jnp.einsum("bhtk,bhsk,bhtsk->bhts", qc, kc, decay)
        o = o_inter + jnp.einsum("bhts,bhsv->bhtv", att, ic)
        b_last = b[:, :, -1:, :]
        S_new = jnp.exp(b_last[:, :, 0, :, None]) * S + jnp.einsum("bhsk,bhsv->bhkv", kc * jnp.exp(b_last - b), ic)
        return S_new, o

    S0 = jnp.zeros((B, H, dk, dv), dtype=jnp.float32)
    _, o = lax.scan(step, S0, (to_chunks(q), to_chunks(log_f), to_chunks(k), to_chunks(i)))
    return jnp.moveaxis(o, 0, 2).reshape(B, H, T, dv)

def hybrid_mixer(h, w_in, w_cmp_k, w_cmp_v, cmp_pe, hgrn_norm, lower, w_sb, w_nsa, w_hg, w_out):
    B, T, _ = h.shape
    f32 = jnp.float32
    proj = h @ w_in
    offsets = np.cumsum(IN_SPLITS)[:-1].tolist()
    sb_q, sb_k, sb_v, nsa_q, nsa_kv, nsa_g, hg_q, hg_f, hg_i, hg_g, merge_g = jnp.split(proj, offsets, axis=-1)

    def heads(t, n):
        return t.reshape(B, T, n, -1).transpose(0, 2, 1, 3)

    o_sb = stick_breaking_attention(heads(sb_q, SB_HEADS), heads(sb_k, SB_HEADS), heads(sb_v, SB_HEADS))
    o_sb = o_sb.transpose(0, 2, 1, 3).reshape(B, T, SB_W)

    qn = heads(nsa_q, NSA_HEADS).reshape(B, NSA_GROUPS, NSA_HPG, T, HEAD_DIM_2)
    kv = nsa_kv.reshape(B, T, 6, NSA_GROUPS, HEAD_DIM_2).transpose(2, 0, 3, 1, 4)
    o_nsa = nsa_attention(qn, kv[0], kv[1], kv[2], kv[3], kv[4], kv[5], nsa_g.reshape(B, T, NSA_HEADS, 3), w_cmp_k, w_cmp_v, cmp_pe)
    o_nsa = o_nsa.reshape(B, NSA_HEADS, T, HEAD_DIM_2).transpose(0, 2, 1, 3).reshape(B, T, NSA_W)

    lb = lower.reshape(HGRN_HEADS, 1, HGRN_DK)
    f = lb + (1.0 - lb) * jax.nn.sigmoid(heads(hg_f, HGRN_HEADS).astype(f32))
    qh = jax.nn.silu(heads(hg_q, HGRN_HEADS).astype(f32))
    o_hg = hgrn2_recurrence(qh, jnp.log(f), 1.0 - f, heads(hg_i, HGRN_HEADS).astype(f32))
    o_hg = rms_norm(o_hg.transpose(0, 2, 1, 3), hgrn_norm.reshape(HGRN_HEADS, HGRN_DV))
    o_hg = (o_hg * jax.nn.silu(hg_g.astype(f32).reshape(B, T, HGRN_HEADS, HGRN_DV))).reshape(B, T, HGRN_V_W).astype(h.dtype)

    gm = jax.nn.sigmoid(merge_g.astype(f32)).reshape(B, T, N_BRANCH, D_MODEL)
    m = gm[:, :, 0] * (o_sb @ w_sb) + gm[:, :, 1] * (o_nsa @ w_nsa) + gm[:, :, 2] * (o_hg @ w_hg)
    return m.astype(h.dtype) @ w_out

def peer_ffn(x, w_q, sub_keys, u_tab, v_tab):
    B, T, D = x.shape
    f32 = jnp.float32
    Ct = PEER_TOK_CHUNK
    H, K = PEER_HEADS, PEER_TOPK
    xt = x.reshape((B * T) // Ct, Ct, D)

    def chunk(xc):
        qh = (xc @ w_q).reshape(Ct, H, 2, PEER_QDIM // 2)
        s = jnp.einsum("nhad,akd->nhak", qh, sub_keys).astype(f32)
        top_s, top_i = lax.top_k(s, K)
        cand = (top_s[:, :, 0, :, None] + top_s[:, :, 1, None, :]).reshape(Ct, H, K * K)
        cand_idx = (top_i[:, :, 0, :, None] * PEER_NKEYS + top_i[:, :, 1, None, :]).reshape(Ct, H, K * K)
        best_s, pos = lax.top_k(cand, K)
        eidx = jnp.take_along_axis(cand_idx, pos, axis=-1)
        gate = jax.nn.softmax(best_s, axis=-1)
        ug = u_tab[eidx]
        vg = v_tab[eidx]
        hpre = jnp.einsum("nd,nhkd->nhk", xc, ug).astype(f32)
        act = (gate * jax.nn.gelu(hpre, approximate=False)).astype(x.dtype)
        return jnp.einsum("nhk,nhkd->nd", act, vg)

    return lax.map(chunk, xt).reshape(B, T, D)

def second_inputs(seed: int = 0) -> dict:
    key = jax.random.key(seed)
    ks = jax.random.split(key, 20)
    f32 = jnp.float32
    nrm = lambda k, shape, s: jax.random.normal(k, shape, dtype=f32) * s
    L, D = DEPTH_2, D_MODEL
    return {
        "x": nrm(ks[0], (BATCH, SEQ, D), 1.0),
        "norm_mix": 1.0 + nrm(ks[1], (L, D), 0.02),
        "norm_ffn": 1.0 + nrm(ks[2], (L, D), 0.02),
        "w_in": nrm(ks[3], (L, D, IN_WIDTH), D ** -0.5),
        "nsa_w_cmp_k": nrm(ks[4], (L, CMP_LEN * HEAD_DIM_2, HEAD_DIM_2), (CMP_LEN * HEAD_DIM_2) ** -0.5),
        "nsa_w_cmp_v": nrm(ks[5], (L, CMP_LEN * HEAD_DIM_2, HEAD_DIM_2), (CMP_LEN * HEAD_DIM_2) ** -0.5),
        "nsa_cmp_pe": nrm(ks[6], (L, CMP_LEN, HEAD_DIM_2), 0.1),
        "hgrn_norm": 1.0 + nrm(ks[7], (L, HGRN_V_W), 0.02),
        "hgrn_lower_bounds": nrm(ks[8], (L, HGRN_K_W), 0.1),
        "w_branch_sb": nrm(ks[9], (L, SB_W, D), SB_W ** -0.5),
        "w_branch_nsa": nrm(ks[10], (L, NSA_W, D), NSA_W ** -0.5),
        "w_branch_hgrn": nrm(ks[11], (L, HGRN_V_W, D), HGRN_V_W ** -0.5),
        "w_out": nrm(ks[12], (L, D, D), 0.5 * D ** -0.5),
        "peer_w_q": nrm(ks[13], (L, D, PEER_HEADS * PEER_QDIM), D ** -0.5),
        "peer_sub_keys": nrm(ks[14], (L, 2, PEER_NKEYS, PEER_QDIM // 2), (PEER_QDIM // 2) ** -0.5),
        "peer_u": nrm(ks[15], (L, PEER_EXPERTS, D), D ** -0.5),
        "peer_v": nrm(ks[16], (L, PEER_EXPERTS, D), (PEER_HEADS * PEER_TOPK) ** -0.5),
        "norm_final": 1.0 + nrm(ks[17], (D,), 0.02),
    }

def second_block(x, norm_mix, norm_ffn, w_in, nsa_w_cmp_k, nsa_w_cmp_v, nsa_cmp_pe, hgrn_norm, hgrn_lower_bounds, w_branch_sb, w_branch_nsa, w_branch_hgrn, w_out, peer_w_q, peer_sub_keys, peer_u, peer_v, norm_final):
    lb_soft = jax.nn.softmax(hgrn_lower_bounds.astype(jnp.float32), axis=0)
    lower = jnp.cumsum(lb_soft, axis=0) - lb_soft[0]
    for l in range(DEPTH_2):
        h = rms_norm(x, norm_mix[l])
        x = x + hybrid_mixer(h, w_in[l], nsa_w_cmp_k[l], nsa_w_cmp_v[l], nsa_cmp_pe[l], hgrn_norm[l], lower[l], w_branch_sb[l], w_branch_nsa[l], w_branch_hgrn[l], w_out[l])
        h = rms_norm(x, norm_ffn[l])
        x = x + peer_ffn(h, peer_w_q[l], peer_sub_keys[l], peer_u[l], peer_v[l])
    return rms_norm(x, norm_final)


def setup_inputs(seed=0):
    out = dict(first_inputs(seed))
    for name, value in second_inputs(seed + 1).items():
        if name != "x":
            out[name + "_2"] = value
    return out


def reference(
    x, mix_norm, sc_w_in, sc_w_conv, sc_w_out, moba_w_qkv, moba_w_o, ffn_norm, ffn_w_up,
    ffn_w_conv, ffn_w_down, final_norm, norm_mix_2, norm_ffn_2, w_in_2, nsa_w_cmp_k_2,
    nsa_w_cmp_v_2, nsa_cmp_pe_2, hgrn_norm_2, hgrn_lower_bounds_2, w_branch_sb_2,
    w_branch_nsa_2, w_branch_hgrn_2, w_out_2, peer_w_q_2, peer_sub_keys_2, peer_u_2, peer_v_2,
    norm_final_2,
):
    x = first_block(
        x, mix_norm, sc_w_in, sc_w_conv, sc_w_out, moba_w_qkv, moba_w_o, ffn_norm, ffn_w_up,
        ffn_w_conv, ffn_w_down, final_norm,
    )
    return second_block(
        x, norm_mix_2, norm_ffn_2, w_in_2, nsa_w_cmp_k_2, nsa_w_cmp_v_2, nsa_cmp_pe_2,
        hgrn_norm_2, hgrn_lower_bounds_2, w_branch_sb_2, w_branch_nsa_2, w_branch_hgrn_2,
        w_out_2, peer_w_q_2, peer_sub_keys_2, peer_u_2, peer_v_2, norm_final_2,
    )


_drawn_inputs = setup_inputs


def setup_inputs(seed=0):
    import zlib

    import numpy as np

    out = dict(_drawn_inputs(seed))
    spreads = {}
    factors = {'ffn_norm': 3.174,
     'norm_mix_2': 6.92,
     'norm_ffn_2': 64.0,
     'nsa_cmp_pe_2': 31.928,
     'hgrn_norm_2': 24.224,
     'norm_final_2': 8.1}
    for name, (base, spread) in spreads.items():
        noise = np.random.default_rng([zlib.crc32(name.encode()), seed]).standard_normal(out[name].shape)
        drawn = base * np.exp(spread * noise) if base else spread * noise
        out[name] = jnp.asarray(drawn.astype(out[name].dtype))
    for name, factor in factors.items():
        out[name] = (out[name] * factor).astype(out[name].dtype)
    return out
```

```python
import numpy as np
import concourse.bass as bass
from concourse import mybir

F32 = mybir.dt.float32
U32 = mybir.dt.uint32
ALU = mybir.AluOpType
ACT = mybir.ActivationFunctionType
AX = mybir.AxisListType

P = 128
T = 256
D = 1024
KD = D // P
FF = 2816
NF = FF // P
HD = 64
EPS = 1e-6
NEG = -1e30
SCALE = HD ** -0.5
RING = 6
BLK = 8
NBLK = T // BLK
NKEY = 128
TOPK = 16
PH = 8
CMP = 16
SC3 = 384

PARTS = [("mix0", KD), ("mix1", KD), ("ffn0", KD), ("ffn1", KD), ("fin1", KD), ("mix2", KD),
         ("ffn2", KD), ("fin2", KD), ("sconv", KD * 3), ("fconv0", 2 * NF * 3), ("fconv1", 2 * NF * 3),
         ("hnorm", 4)]
POFF = {}
_o = 0
for _n, _w in PARTS:
    POFF[_n] = _o
    _o += _w
NPAR = _o
CPARTS = [("ident", P), ("swap", P), ("cos", T), ("sin", T), ("causal", SC3), ("strict", SC3),
          ("alibi", 8 * SC3), ("cmpbias", 8 * 2 * CMP), ("rowok", 2), ("blkmask", T), ("iota", P),
          ("iota16", TOPK)]
COFF = {}
_o = 0
for _n, _w in CPARTS:
    COFF[_n] = _o
    _o += _w
NCON = _o


class Step:

    def __init__(self, s, stride=0, i=None):
        self.s, self.stride, self.i = s, stride, i

    def lin(self, a, b=0):
        v = a * self.s + b
        return v if self.i is None else self.i * (a * self.stride) + v

    def mod(self, n, a=1, b=0):
        assert self.i is None or (a * self.stride) % n == 0
        return (a * self.s + b) % n

    def div(self, n, a=1, b=0):
        assert self.i is None or (a * self.stride) % n == 0
        v = (a * self.s + b) // n
        return v if self.i is None else self.i * (a * self.stride // n) + v


class Chain:

    def __init__(self, eng, sem):
        self.eng, self.sem, self.n, self.per, self.i = eng, sem, 0, 0, None

    def mark(self, ins):
        ins.then_inc(self.sem, 1)
        self.n += 1
        return self.n

    def need(self, k=None):
        k = self.n if k is None else k
        self.eng.wait_ge(self.sem, k if self.i is None else self.i * self.per + k)

    def link(self, ins):
        self.mark(ins)
        self.need()


def steps(eng, chain, lo, hi, body, fn, first=0, per=0):
    n = lo
    while n < min(first, hi):
        fn(Step(n))
        n += 1
    turns = (hi - n) // body
    if turns > 1:
        with eng.Fori(0, turns) as i:
            if chain is not None:
                at = chain.n
                chain.i, chain.per = i, per * body
            for u in range(body):
                fn(Step(n + u, body, i))
            if chain is not None:
                assert chain.n - at == per * body, (chain.n - at, per, body)
                chain.n = at + per * body * turns
                chain.i = None
        n += body * turns
    while n < hi:
        fn(Step(n))
        n += 1


def chunk_plan():
    at, out = 0, {}
    for name, n in [("sc", 4 * KD), ("ffn0", 3 * NF), ("qkv", 24), ("wo", KD), ("ffn1", 3 * NF),
                    ("p_split", 16), ("p_tok", 6), ("p_feat", 16), ("merge", 6 * KD),
                    ("pq", KD), ("peer", 2 * NKEY)]:
        out[name] = at
        at += n
    out["end"] = at
    return out


CH = chunk_plan()


def build(nc, stream, xT, par, con, wg, wcmpk, wcmpv, peT, subk, y):
    def sem(name):
        return nc.alloc_semaphore(name)

    def sb(name, shape, dt=F32):
        return nc.alloc_sbuf_tensor(name, shape, dt)

    ring = sb("ring", [P, RING, D])
    x = sb("x", [P, KD, T])
    h = sb("h", [P, KD, T])
    sq = sb("sq", [P, KD, T])
    tabs = sb("tabs", [P, NPAR])
    cons = sb("cons", [P, NCON])
    ones = sb("ones", [P, T])
    norm_t = sb("norm_t", [P, T])
    rstd = sb("rstd", [P, T])
    ARENA = 34512
    arena = sb("arena", [P, ARENA])
    ps = nc.alloc_psum_tensor("ps", [P, 8, 512], F32)

    def con_(name, n=None):
        o = COFF[name]
        return cons[:, o:o + (n or dict(CPARTS)[name])]

    def par_(name, a, n=1):
        return tabs[:, bass.ds(a + POFF[name], n)]

    ident = con_("ident")
    acc = ps[:, 0:4, :]

    class Area:

        def __init__(self, at=0):
            self.at = at

        def take(self, *dims, parts=P):
            n = int(np.prod(dims))
            v = arena[0:parts, self.at:self.at + n]
            self.at += n
            assert self.at <= ARENA, self.at
            if len(dims) == 2:
                v = v.rearrange("p (a b) -> p a b", a=dims[0])
            elif len(dims) == 3:
                v = v.rearrange("p (a b c) -> p a b c", a=dims[0], b=dims[1])
            elif len(dims) == 4:
                v = v.rearrange("p (a b c d) -> p a b c d", a=dims[0], b=dims[1], c=dims[2])
            return v

    f_ = Area(ARENA - 8 * T)
    conv_g, conv_u, silu_o, z = f_.take(T), f_.take(T), f_.take(T), f_.take(T)
    copied = f_.take(2, T)
    rope_a, rope_b = f_.take(T), f_.take(T)
    m_ = Area()
    heads = m_.take(32, T, parts=HD)
    vtok = m_.take(2, D)
    otok = m_.take(2, D)
    a_q = m_.take(2, T, parts=HD)
    a_s = m_.take(2, SC3)
    a_e = m_.take(2, SC3)
    a_t = m_.take(2, SC3)
    a_max = m_.take(2, 2)
    a_sum = m_.take(64, 2)
    a_r = m_.take(1, 2)
    a_l = m_.take(2, SC3)
    a_c = m_.take(SC3)
    m_oT = m_.at
    oT = m_.take(12, T)
    hfeat = m_.take(16, T)
    gates = m_.take(2, 24)
    wg_s = m_.take(KD, 24)
    scratch0 = m_.at

    c_ = Area(scratch0)
    wk_s, wv_s = c_.take(32, HD, parts=HD), c_.take(32, HD, parts=HD)
    pe_s = c_.take(32, parts=HD)
    blk_k, blk_v = c_.take(32, 2, CMP, parts=HD), c_.take(32, 2, CMP, parts=HD)
    kc, vc = c_.take(2, CMP, parts=HD), c_.take(2, HD, parts=CMP)
    ce, cm = c_.take(16 * CMP), c_.take(16)
    ceT = Area(m_oT).take(16, P, parts=CMP)
    hq, hf, hi, hg = (hfeat[:, 4 * i:4 * i + 4, :] for i in range(4))
    g_ = Area(scratch0)
    h_tmp, h_lf, h_k, h_lb, h_q, h_kn = (g_.take(4, T) for _ in range(6))
    h_e = g_.take(4, NBLK)
    h_o = g_.take(4, T)
    keys_s = Area(max(g_.at, c_.at)).take(2 * NKEY)
    g2_ = Area()
    h_w = g2_.take(2, 4, T)
    h_att = g2_.take(4, SC3)
    h_x = g2_.take(NBLK * BLK * BLK)
    h_x4 = h_x.rearrange("p (b t s) -> p b t s", b=NBLK, t=BLK)
    h_p = g2_.take(NBLK * BLK * BLK)
    h_od = g2_.take(4, T)
    h_itok = g2_.take(2, 4 * P)
    sg = arena[:, ARENA - 4 * T:ARENA - T].rearrange("p (a t) -> p a t", a=3)
    gmap = arena[:, 0:T * NKEY]
    t_ = Area()
    t_q, t_s = t_.take(PH, T), t_.take(32, NKEY)
    t_b, t_if = t_.take(32, TOPK), t_.take(32, TOPK)
    t_i = t_.take(32, TOPK).bitcast(U32)
    t_c = t_.take(16, TOPK * TOPK)
    t_g = t_.take(16, TOPK)
    t_w, t_wi, t_wj = (t_.take(16, TOPK).bitcast(U32) for _ in range(3))
    t_wf = t_.take(2, 16, TOPK)
    t_m = t_.take(16, 1)
    t_1 = t_.take(P, TOPK)
    t_key = t_.take(3, 2, P)
    assert t_.at <= g_.at
    idx = sg
    hot = sq[:, :, :].rearrange("p a t -> p (a t)").rearrange("p (h r k) -> p h r k", h=2, r=8)
    hot_a, hot_b = hot[:, 0], hot[:, 1]

    s_x = sem("x_loaded")
    s_par = sem("params_loaded")
    s_small = sem("block2_params_loaded")
    ring_full = [sem(f"ring_full{r}") for r in range(RING)]
    chunk_done = sem("chunk_multiplied")
    s_ones = sem("ones_written")
    x_part = sem("x_part_updated")
    sq_part = sem("square_ready")
    sum_ready = sem("square_sum_ready")
    recip_ready = sem("recip_ready")
    rstd_ready = sem("rstd_ready")
    h_ready = sem("h_ready")
    tile_copied = sem("tile_copied")
    conv_g_done = sem("conv_g_done")
    conv_u_done = sem("conv_u_done")
    c_copied = sem("c_copied")
    silu_done = sem("silu_done")
    z_ready = sem("z_ready")
    rot_ready = sem("rotated_ready")
    rope_done = sem("rope_done")
    dve_c, act_c, pool_c, pe_c = sem("dve_chain"), sem("act_chain"), sem("pool_chain"), sem("pe_chain")
    q_staged = sem("q_staged")
    s_ready = sem("scores_ready")
    s_read = sem("scores_read")
    max_ready = sem("max_ready")
    soft_ready = sem("softplus_ready")
    logit_ready = sem("log_weight_ready")
    e_ready = sem("weights_ready")
    et_ready = sem("weights_transposed")
    et_copied = sem("weights_transposed_copied")
    pv_ready = sem("pv_ready")
    o_read = sem("o_read")
    ot_ready = sem("o_transposed")
    ot_copied = sem("o_transposed_copied")
    gate_ready, gate_copied = sem("gate_ready"), sem("gate_copied")
    cmp_dve_s, cmp_pe_s, cmp_act_s = sem("cmp_vector_stage"), sem("cmp_tensor_stage"), sem("cmp_scalar_stage")
    hg_dve_s, hg_pe_s, hg_act_s = sem("hgrn_vector_stage"), sem("hgrn_tensor_stage"), sem("hgrn_scalar_stage")
    w_zeroed, w_ready, w_used = sem("decayed_keys_zeroed"), sem("decayed_keys_ready"), sem("decayed_keys_used")
    hd_sub, hd_masked, hd_exp = sem("pair_exponent_ready"), sem("pair_exponent_masked"), sem("pair_decay_ready")
    hd_x, hd_sum, hd_red = sem("pair_product_ready"), sem("pair_sum_ready"), sem("pair_output_ready")
    sg_ready, branch_taken = sem("merge_gate_ready"), sem("branch_taken")
    tk_pe, tk_act, tk_dve = sem("topk_tensor_stage"), sem("topk_scalar_stage"), sem("topk_vector_stage")
    hot_ready, gm_done, gm_copied = sem("one_hots_ready"), sem("gate_map_ready"), sem("gate_map_copied")
    gelu_done = sem("gelu_done")
    s_y = sem("y_stored")

    NCH = CH["end"]

    ZB = {"sc": 0, "ffn0": KD, "ffn1": KD + NF, "merge": KD + 2 * NF, "peer": 2 * KD + 2 * NF}
    HB = {"moba": 0, "sb": 16, "nsa0w": 24, "nsa0s": 28, "nsa1w": 32, "nsa1s": 36, "end": 40}
    MB = {b: b - 8 * (b > HB["sb"]) for b in HB.values()}
    TC = {"qkv": 0, "p_split": 24, "p_tok": 40, "p_feat": 46, "pq": 62}

    def bank(par, sub):
        return ps[:, 4 + 2 * par + sub // 2, (sub % 2) * T:(sub % 2) * T + T]

    def stream_all(sp):
        def load(st):
            r = st.mod(RING)
            sp.dma_start(ring[:, r, :], stream[st.lin(1), :, :]).then_inc(ring_full[r], 16)

        def one(st):
            sp.wait_ge(chunk_done, st.lin(1, 1 - RING))
            load(st)

        for c in range(RING):
            load(Step(c))
        steps(sp, None, RING, NCH, RING, one)

    def arrived(pe, st, a, b):
        r = st.mod(RING, a, b)
        v = (a * st.s + b) // RING + 1
        pe.wait_ge(ring_full[r], 16 * v if st.i is None else st.i * (16 * (a * st.stride // RING)) + 16 * v)
        return r

    def up(pe, slot, out, k0=0, nk=KD, rhs=None, inc=True):
        for k in range(nk):
            ins = nc.tensor.matmul(out, ring[:, slot, (k0 + k) * P:(k0 + k) * P + P],
                                   h[:, k, :] if rhs is None else rhs[:, k, :], start=(k == 0), stop=(k == nk - 1))
        if inc:
            ins.then_inc(chunk_done, 1)

    def down(pe, slot, src, first, final):
        for o in range(KD):
            ins = nc.tensor.matmul(acc[:, o // 2, (o % 2) * T:(o % 2) * T + T], ring[:, slot, o * P:o * P + P],
                                   src, start=(first and o % 2 == 0), stop=final, skip_group_check=True)
        ins.then_inc(chunk_done, 1)

    def up_at(name, per, j, u):
        return per, CH[name] + u - (1 if j > 0 else 0)

    def down_at(name, per, n, j):
        return per, CH[name] + (per - 2 if j < n else -1)

    def norm_pe(pe, parts):
        for k in range(4):
            pe.wait_ge(sq_part, parts + k + 1)
            for j in (2 * k, 2 * k + 1):
                ins = nc.tensor.matmul(ps[:, 7, 0:T], ones[:, 0:P], sq[:, j, :], start=(j == 0), stop=(j == 7))
        ins.then_inc(sum_ready, 1)

    def gated_pe(pe, name, n, ups, body, free, free_base, hn):
        pe.wait_ge(h_ready, hn)

        def one(st):
            if st.s < n:
                if st.s >= 2:
                    pe.wait_ge(free, st.lin(1, free_base - 1))
                for u in range(ups):
                    up(pe, arrived(pe, st, *up_at(name, ups + 1, st.s, u)), bank(st.mod(2), u))
            if st.s >= 1:
                pe.wait_ge(z_ready, st.lin(1, ZB[name]))
                r = arrived(pe, st, *down_at(name, ups + 1, n, st.s))
                down(pe, r, z, st.s == 1, st.s == n)

        steps(pe, None, 0, n, body, one, first=2)
        one(Step(n))

    def residual_dve(dve, dc):
        for k in range(4):
            nc.vector.tensor_tensor(x[:, 2 * k:2 * k + 2, :], x[:, 2 * k:2 * k + 2, :],
                                    acc[:, k, :].rearrange("p (a t) -> p a t", a=2), ALU.add).then_inc(x_part, 1)

    def norm_act(act, n, source, base):
        for k in range(4):
            act.wait_ge(source, base + (k + 1 if source is x_part else 0))
            nc.scalar.activation(sq[:, 2 * k:2 * k + 2, :], x[:, 2 * k:2 * k + 2, :], ACT.Square).then_inc(sq_part, 1)
        act.wait_ge(recip_ready, n + 1)
        nc.scalar.activation(rstd[:, :], norm_t[:, :], ACT.Sqrt).then_inc(rstd_ready, 1)

    def norm_dve(dve, dc, n, weight, dst):
        dve.wait_ge(sum_ready, n + 1)
        dc.link(nc.vector.tensor_scalar(norm_t[:, :], ps[:, 7, 0:T], 1.0 / D, EPS, ALU.mult, ALU.add))
        nc.vector.reciprocal(norm_t[:, :], norm_t[:, :]).then_inc(recip_ready, 1)
        dve.wait_ge(rstd_ready, n + 1)
        for k in range(KD):
            ins = nc.vector.scalar_tensor_tensor(dst[:, k, :], x[:, k, :], par_(weight, k), rstd[:, :],
                                                 ALU.mult, ALU.mult)
        ins.then_inc(h_ready, 1)
        dve.wait_ge(h_ready, n + 1)

    def conv(dve, dc, dst, src, wname, tap0):
        yield nc.vector.tensor_scalar(dst, src, par_(wname, tap0 + 2), None, ALU.mult)
        yield nc.vector.scalar_tensor_tensor(dst[:, 1:T], src[:, 0:T - 1], par_(wname, tap0 + 1), dst[:, 1:T],
                                             ALU.mult, ALU.add)
        yield nc.vector.scalar_tensor_tensor(dst[:, 2:T], src[:, 0:T - 2], par_(wname, tap0), dst[:, 2:T],
                                             ALU.mult, ALU.add)

    def ffn_dve(dve, dc, name, wname, sems0):
        n = NF

        def one(st):
            a, b = up_at(name, 3, st.s, 1)
            dve.wait_ge(chunk_done, st.lin(a, b + 1))
            if st.s >= 1:
                dve.wait_ge(z_ready, st.lin(1, ZB[name]))
            par = st.mod(2)
            cg = conv(dve, dc, conv_g, bank(par, 0), wname, st.lin(3, 0))
            cu = conv(dve, dc, conv_u, bank(par, 1), wname, st.lin(3, NF * 3))
            g1, u1 = dc.mark(next(cg)), dc.mark(next(cu))
            dc.need(g1)
            g2 = dc.mark(next(cg))
            dc.need(u1)
            u2 = dc.mark(next(cu))
            dc.need(g2)
            next(cg).then_inc(conv_g_done, 1)
            dc.need(u2)
            next(cu).then_inc(conv_u_done, 1)
            dve.wait_ge(conv_u_done, st.lin(1, sems0 + 1))
            dve.wait_ge(silu_done, st.lin(1, sems0 + 1))
            if st.s >= 1:
                a, b = down_at(name, 3, n, st.s)
                dve.wait_ge(chunk_done, st.lin(a, b + 1))
            nc.vector.tensor_tensor(z, silu_o, conv_u, ALU.mult).then_inc(z_ready, 1)

        steps(dve, dc, 0, n, 2, one, first=2, per=4)
        dve.wait_ge(chunk_done, CH[name] + 3 * n)

    def ffn_act(act, name, sems0):
        def one(st):
            act.wait_ge(conv_g_done, st.lin(1, sems0 + 1))
            nc.scalar.activation(silu_o, conv_g, ACT.Silu).then_inc(silu_done, 1)

        steps(act, None, 0, NF, 2, one, first=2)

    def sc_dve(dve, dc):
        def one(st):
            par = st.mod(2)
            a, b = up_at("sc", 4, st.s, 2)
            dve.wait_ge(chunk_done, st.lin(a, b + 1))
            dve.wait_ge(c_copied, st.lin(1, 1))
            if st.s >= 1:
                dve.wait_ge(z_ready, st.lin(1))
            dc.link(nc.vector.tensor_tensor(conv_u, silu_o, bank(par, 2), ALU.mult))
            for ins in conv(dve, dc, conv_g, conv_u, "sconv", st.lin(3)):
                dc.link(ins)
            if st.s >= 1:
                a, b = down_at("sc", 4, KD, st.s)
                dve.wait_ge(chunk_done, st.lin(a, b + 1))
            nc.vector.tensor_tensor(z, conv_g, bank(par, 0), ALU.mult).then_inc(z_ready, 1)

        steps(dve, dc, 0, KD, 6, one)
        dve.wait_ge(chunk_done, CH["sc"] + 4 * KD)

    def sc_act(act):
        def one(st):
            a, b = up_at("sc", 4, st.s, 1)
            act.wait_ge(chunk_done, st.lin(a, b + 1))
            if st.s >= 1:
                act.wait_ge(z_ready, st.lin(1))
            nc.scalar.activation(silu_o, bank(st.mod(2), 1), ACT.Copy).then_inc(c_copied, 1)

        steps(act, None, 0, KD, 6, one)

    def project_pe(pe, name, n, tokens_out=False, skip=0):
        def one(st):
            g = TC[name]
            if g + st.s >= 2:
                pe.wait_ge(tile_copied, st.lin(1, g - 1))
            r = arrived(pe, st, 1, CH[name])
            par = st.mod(2, 1, g)
            if not tokens_out:
                up(pe, r, bank(par, 0))
                return
            for c in range(2):
                for k in range(KD):
                    ins = nc.tensor.matmul(ps[:, 4 + 2 * par, c * P:c * P + P], h[:, k, c * P:c * P + P],
                                           ring[:, r, k * P:k * P + P], start=(k == 0), stop=(k == KD - 1))
            ins.then_inc(chunk_done, 1)

        steps(pe, None, skip, skip + n, RING, one)

    def copy_heads(act, ac, st, g, dst):
        src = bank(st.mod(2, 1, g), 0)
        nc.scalar.activation(dst[:, st.lin(2), :], src[0:HD, :], ACT.Copy)
        return nc.scalar.activation(dst[:, st.lin(2, 1), :], src[HD:P, :], ACT.Copy)

    def copy_tokens(act, ac, st, g, dst, skip):
        src = bank(st.mod(2, 1, g), 0).rearrange("p (c f) -> p c f", c=2)
        return nc.scalar.activation(dst[:, :, bass.ds(st.lin(P, -P * skip), P)], src, ACT.Copy)

    def copy_feat(act, ac, st, g, dst):
        return nc.scalar.activation(dst[:, st.lin(1), :], bank(st.mod(2, 1, g), 0), ACT.Copy)

    def project_act(act, ac, name, n, copy, *args, skip=0):
        def one(st):
            act.wait_ge(chunk_done, st.lin(1, CH[name] + 1))
            copy(act, ac, st, TC[name], *args).then_inc(tile_copied, 1)

        steps(act, None, skip, skip + n, RING, one)

    def qk_pe(pe):
        pe.wait_ge(h_ready, 3)

        def swap(st):
            pe.wait_ge(tile_copied, st.lin(1))
            if st.s >= 3:
                pe.wait_ge(rope_done, st.lin(1, -2))
            nc.tensor.matmul(bank(st.mod(2, 1, 1), 2), con_("swap"), copied[:, st.mod(2, 1, 1), :],
                             start=True, stop=True).then_inc(rot_ready, 1)

        def one(st):
            if st.s >= 2:
                pe.wait_ge(tile_copied, st.lin(1, -1))
            up(pe, arrived(pe, st, 1, CH["qkv"]), bank(st.mod(2), 0))
            if st.s >= 1:
                swap(st)

        steps(pe, None, 0, 16, RING, one, first=4)
        swap(Step(16))

    def qk_act(act):
        def one(st):
            act.wait_ge(chunk_done, st.lin(1, CH["qkv"] + 1))
            if st.s >= 2:
                act.wait_ge(rope_done, st.lin(1, -1))
            nc.scalar.activation(copied[:, st.mod(2), :], bank(st.mod(2), 0), ACT.Copy).then_inc(tile_copied, 1)

        steps(act, None, 0, 16, 2, one, first=2)

    def qk_dve(dve, dc):
        def one(st):
            dve.wait_ge(rot_ready, st.lin(1, 1))
            if st.s >= 1:
                dve.wait_ge(rope_done, st.lin(1))
            dc.mark(nc.vector.tensor_tensor(rope_a, copied[:, st.mod(2), :], con_("cos"), ALU.mult))
            dc.link(nc.vector.tensor_tensor(rope_b, bank(st.mod(2), 2), con_("sin"), ALU.mult))
            nc.vector.tensor_tensor(heads[:, st.lin(2), :], rope_a[0:HD], rope_b[0:HD], ALU.add)
            nc.vector.tensor_tensor(heads[:, st.lin(2, 1), :], rope_a[HD:P], rope_b[HD:P],
                                    ALU.add).then_inc(rope_done, 1)

        steps(dve, dc, 0, 16, 2, one, first=2, per=2)

    def heads_pool(pool, base, n, q):
        def one(st):
            if base + st.s >= 2:
                pool.wait_ge(s_ready, st.lin(1, base - 1))
            nc.gpsimd.tensor_copy(a_q[:, st.mod(2), :], q(st)).then_inc(q_staged, 1)

        steps(pool, None, 0, n, 2, one, first=2)

    def heads_pe(pe, base, n, k, v, lag):
        def scores(st):
            pe.wait_ge(q_staged, st.lin(1, base + 1))
            if base + st.s >= 2:
                pe.wait_ge(s_read, st.lin(1, base - 1))
            p = st.mod(2)
            nc.tensor.matmul(ps[:, 4 + p, 0:P], a_q[:, p, 0:P], k(st)[:, 0:P], start=True, stop=True)
            nc.tensor.matmul(ps[:, 4 + p, P:SC3], a_q[:, p, P:T], k(st), start=True, stop=True).then_inc(s_ready, 1)

        def turn(st):
            pe.wait_ge(e_ready, st.lin(1, base + 1))
            if base + st.s >= 2:
                pe.wait_ge(et_copied, st.lin(1, base - 1))
            p = st.mod(2)
            for b in range(3):
                ins = nc.tensor.transpose(ps[:, 6 + p, b * P:b * P + P], a_e[:, p, b * P:b * P + P], ident)
            ins.then_inc(et_ready, 1)

        def values(st):
            pe.wait_ge(et_copied, st.lin(1, base + 1))
            if base + st.s >= 2:
                pe.wait_ge(o_read, st.lin(1, base - 1))
            p = st.mod(2)
            nc.tensor.matmul(ps[:, p, 0:HD], a_t[:, p, 0:P], v(st, 0), start=True, stop=True)
            nc.tensor.matmul(ps[:, p, HD:2 * HD], a_t[:, p, P:2 * P], v(st, 0), start=True, stop=False)
            nc.tensor.matmul(ps[:, p, HD:2 * HD], a_t[:, p, 2 * P:SC3], v(st, 1), start=False,
                             stop=True).then_inc(pv_ready, 1)

        def one(st):
            if st.s < n:
                scores(st)
            if 0 <= st.s - lag < n:
                turn(Step(st.s - lag, st.stride, st.i))
            if st.s - lag - 1 >= 0:
                values(Step(st.s - lag - 1, st.stride, st.i))

        steps(pe, None, 0, n, 2, one, first=lag + 1)
        for j in range(n, n + lag + 1):
            one(Step(j))

    def copy_weights(act, base, st):
        act.wait_ge(et_ready, st.lin(1, base + 1))
        if base + st.s >= 2:
            act.wait_ge(pv_ready, st.lin(1, base - 1))
        nc.scalar.activation(a_t[:, st.mod(2), :], ps[:, 6 + st.mod(2), 0:SC3], ACT.Copy).then_inc(et_copied, 1)

    def soft_act(act, base, n):
        def one(st):
            p = st.mod(2)
            if st.s < n:
                act.wait_ge(max_ready, st.lin(1, MB[base] + 1))
                if base + st.s >= 2:
                    act.wait_ge(et_ready, st.lin(1, base - 1))
                for c, (lo, hi) in enumerate(((0, P), (P, SC3))):
                    ins = nc.scalar.activation(a_e[:, p, lo:hi], a_s[:, p, lo:hi], ACT.Exp,
                                               bias=a_max[:, p, c:c + 1],
                                               accum_out=a_sum[:, st.lin(1, base), c:c + 1])
                ins.then_inc(e_ready, 1)
            if st.s >= 1:
                copy_weights(act, base, Step(st.s - 1, st.stride, st.i))

        steps(act, None, 0, n, 2, one, first=2)
        one(Step(n))

    def soft_dve(dve, dc, base, n, bias, out, marks):
        def score(st):
            p = st.mod(2)
            dve.wait_ge(s_ready, st.lin(1, base + 1))
            if base + st.s >= 2:
                dve.wait_ge(e_ready, st.lin(1, base - 1))
            nc.vector.scalar_tensor_tensor(a_s[:, p, :], ps[:, 4 + p, 0:SC3], SCALE, bias(st), ALU.mult, ALU.add).then_inc(s_read, 1)
            dve.wait_ge(s_read, st.lin(1, base + 1))
            nc.vector.tensor_reduce(a_max[:, p, 0:1], a_s[:, p, 0:P], AX.X, ALU.max, negate=True)
            nc.vector.tensor_reduce(a_max[:, p, 1:2], a_s[:, p, P:SC3], AX.X, ALU.max,
                                    negate=True).then_inc(max_ready, 1)

        def rows(st):
            dve.wait_ge(pv_ready, st.lin(1, base + 1))
            if base + st.s >= 1:
                dve.wait_ge(o_read, st.lin(1, base))
            dc.link(nc.vector.reciprocal(a_r[:, 0, :], a_sum[:, st.lin(1, base), :]))
            out(st, ps[:, st.mod(2), 0:2 * HD].rearrange("p (c d) -> p c d", c=2)).then_inc(o_read, 1)

        def one(st):
            if st.s < n:
                score(st)
            if st.s >= 2:
                rows(Step(st.s - 2, st.stride, st.i))

        steps(dve, dc, 0, n, 2, one, first=2, per=marks)
        one(Step(n))
        one(Step(n + 1))

    def stick_act(act, ac, base, n):
        def soft(st):
            p = st.mod(2)
            act.wait_ge(s_read, st.lin(1, base + 1))
            if st.s >= 2:
                act.wait_ge(e_ready, st.lin(1, base - 1))
            ac.link(nc.scalar.activation(a_l[:, p, :], a_s[:, p, :], ACT.Abs))
            ac.link(nc.scalar.activation(a_l[:, p, :], a_l[:, p, :], ACT.Exp, scale=-1.0))
            nc.scalar.activation(a_l[:, p, :], a_l[:, p, :], ACT.Ln, bias=1.0).then_inc(soft_ready, 1)

        def weight(st):
            p = st.mod(2)
            act.wait_ge(logit_ready, st.lin(1, 1))
            if base + st.s >= 2:
                act.wait_ge(et_ready, st.lin(1, base - 1))
            nc.scalar.activation(a_e[:, p, :], a_l[:, p, :], ACT.Exp).then_inc(e_ready, 1)

        def one(st):
            if st.s < n:
                soft(st)
            if 0 <= st.s - 1 < n:
                weight(Step(st.s - 1, st.stride, st.i))
            if st.s - 2 >= 0:
                copy_weights(act, base, Step(st.s - 2, st.stride, st.i))

        steps(act, ac, 0, n, 2, one, first=2, per=2)
        one(Step(n))
        one(Step(n + 1))

    def stick_dve(dve, dc, base, n, out):
        def mask(st):
            p = st.mod(2)
            dve.wait_ge(s_ready, st.lin(1, base + 1))
            if st.s >= 2:
                dve.wait_ge(logit_ready, st.lin(1, -1))
            nc.vector.scalar_tensor_tensor(a_s[:, p, :], ps[:, 4 + p, 0:SC3], SCALE, con_("strict"), ALU.mult, ALU.add).then_inc(s_read, 1)

        def logit(st):
            p = st.mod(2)
            dve.wait_ge(soft_ready, st.lin(1, 1))
            if st.s >= 1:
                dve.wait_ge(logit_ready, st.lin(1))
            dc.link(nc.vector.scalar_tensor_tensor(a_l[:, p, :], a_s[:, p, :], 0.0, a_l[:, p, :], ALU.max, ALU.add))
            for lo, hi in ((0, P), (P, SC3)):
                rev = slice(hi - 1, lo - 1 if lo else None, -1)
                dc.mark(nc.vector.tensor_tensor_scan(a_c[:, rev], ones[:, 0:hi - lo], a_l[:, p, rev], 0.0,
                                                     ALU.mult, ALU.add))
            dc.need()
            nc.vector.tensor_tensor(a_l[:, p, :], a_s[:, p, :], a_c, ALU.subtract).then_inc(logit_ready, 1)

        def rows(st):
            dve.wait_ge(pv_ready, st.lin(1, base + 1))
            out(st, ps[:, st.mod(2), 0:2 * HD].rearrange("p (c d) -> p c d", c=2)).then_inc(o_read, 1)

        def one(st):
            if st.s < n:
                mask(st)
            if 0 <= st.s - 1 < n:
                logit(Step(st.s - 1, st.stride, st.i))
            if st.s - 3 >= 0:
                rows(Step(st.s - 3, st.stride, st.i))

        steps(dve, dc, 0, n, 2, one, first=4, per=3)
        for j in range(n, n + 3):
            one(Step(j))

    def head_cols(st, o=0):
        return otok[:, :, bass.ds(st.lin(HD, o), HD)]

    def rows_soft(st, o):
        dst = head_cols(st)
        nc.vector.tensor_scalar(dst[:, 0, :], o[:, 0, :], a_r[:, 0, 0:1], None, ALU.mult)
        return nc.vector.tensor_scalar(dst[:, 1, :], o[:, 1, :], a_r[:, 0, 1:2], None, ALU.mult)

    def turn_out_pe(pe, base):
        for g in range(4):
            for b in range(4):
                j, c = 2 * g + b // 2, b % 2
                ins = nc.tensor.transpose(ps[:, 4 + g, b * P:b * P + P], otok[:, c, j * P:j * P + P], ident)
            ins.then_inc(ot_ready, 1)

    def turn_out_act(act, base):
        for g in range(4):
            act.wait_ge(ot_ready, base + g + 1)
            nc.scalar.activation(oT[:, 2 * g:2 * g + 2, :], ps[:, 4 + g, :].rearrange("p (a t) -> p a t", a=2),
                                 ACT.Copy).then_inc(ot_copied, 1)

    def wo_pe(pe):
        for j in range(KD):
            pe.wait_ge(ot_copied, j // 2 + 1)
            down(pe, arrived(pe, Step(j), 1, CH["wo"]), oT[:, j, :], j == 0, j == KD - 1)

    def gates_pe(pe):
        for c in range(2):
            for k in range(KD):
                ins = nc.tensor.matmul(ps[:, 0, c * 24:c * 24 + 24], h[:, k, c * P:c * P + P], wg_s[:, k, :],
                                       start=(k == 0), stop=(k == KD - 1))
        ins.then_inc(gate_ready, 1)

    def gates_act(act):
        act.wait_ge(gate_ready, 1)
        nc.scalar.activation(gates, ps[:, 0, 0:48].rearrange("p (c g) -> p c g", c=2), ACT.Sigmoid)\
            .then_inc(gate_copied, 1)

    def cmp_dve(dve, dc):
        dve.wait_ge(s_small, 16 * 6)
        dve.wait_ge(tile_copied, TC["p_tok"])
        dc.mark(nc.vector.memset(blk_k, 0.0))
        dc.link(nc.vector.memset(blk_v, 0.0))
        for dst, hd in ((blk_k, 24), (blk_v, 26)):
            src = heads[:, hd:hd + 2, :].rearrange("p g (c l) -> p l g c", l=16)
            for half in range(2):
                ins = nc.vector.tensor_tensor(
                    dst[:, 16 * half:16 * half + 16, :, 0:15], src[:, :, :, half:half + 15],
                    pe_s[:, 16 * half:16 * half + 16].unsqueeze(2).unsqueeze(3).broadcast_to([HD, 16, 2, 15]), ALU.add)
        ins.then_inc(cmp_dve_s, 1)
        dve.wait_ge(cmp_pe_s, 2)
        nc.vector.scalar_tensor_tensor(ce, ps[:, 4, 0:256], SCALE, con_("cmpbias"), ALU.mult, ALU.add)\
            .then_inc(cmp_dve_s, 1)
        dve.wait_ge(cmp_dve_s, 2)
        ce3 = ce.rearrange("p (r c) -> p r c", c=CMP)
        dc.link(nc.vector.tensor_reduce(cm, ce3, AX.X, ALU.max))
        nc.vector.tensor_tensor(ce3, ce3, cm.unsqueeze(2).broadcast_to([P, 16, CMP]), ALU.subtract)\
            .then_inc(cmp_dve_s, 1)
        dve.wait_ge(cmp_act_s, 2)
        dve.wait_ge(gate_copied, 1)
        dc.link(nc.vector.tensor_reduce(cm, ce3, AX.X, ALU.add))
        dc.link(nc.vector.reciprocal(cm, cm))
        g = gates.rearrange("p c (h b) -> p h c b", b=3)[:, :, :, 0]
        cm2 = cm.rearrange("p (h c) -> p h c", c=2)
        dc.link(nc.vector.tensor_tensor(cm2, cm2, g, ALU.mult))
        dc.link(nc.vector.tensor_tensor(cm2, cm2, con_("rowok").unsqueeze(1).broadcast_to([P, 8, 2]), ALU.mult))
        nc.vector.tensor_tensor(ce3, ce3, cm.unsqueeze(2).broadcast_to([P, 16, CMP]), ALU.mult)\
            .then_inc(cmp_dve_s, 1)
        dve.wait_ge(cmp_pe_s, 4)
        for b in range(2):
            src = ps[:, 2 + b, :].rearrange("p (h c d) -> p h c d", h=4, c=2)
            for c in range(2):
                ins = nc.vector.tensor_copy(
                    otok[:, c, 512 + b * 256:512 + b * 256 + 256].rearrange("p (h d) -> p h d", h=4), src[:, :, c, :])
        ins.then_inc(cmp_dve_s, 1)
        dve.wait_ge(cmp_dve_s, 5)

    def cmp_pe(pe):
        pe.wait_ge(s_small, 16 * 6)
        pe.wait_ge(cmp_dve_s, 1)
        pe.wait_ge(gate_copied, 1)
        for l in range(32):
            nc.tensor.matmul(ps[0:HD, 0, 0:32], wk_s[:, l, :], blk_k[:, l, :, :].rearrange("p g c -> p (g c)"),
                             start=(l == 0), stop=(l == 31))
        for g in range(2):
            for l in range(32):
                ins = nc.tensor.matmul(ps[0:CMP, 1, g * HD:g * HD + HD], blk_v[:, l, g, :], wv_s[:, l, :],
                                       start=(l == 0), stop=(l == 31))
        ins.then_inc(cmp_pe_s, 1)
        pe.wait_ge(cmp_act_s, 1)
        for hd in range(8):
            for c in range(2):
                r = 2 * hd + c
                ins = nc.tensor.matmul(ps[:, 4, r * CMP:r * CMP + CMP], heads[:, 16 + hd, c * P:c * P + P],
                                       kc[:, hd // 4, :], start=True, stop=True)
        ins.then_inc(cmp_pe_s, 1)
        pe.wait_ge(cmp_dve_s, 4)
        for r in range(16):
            ins = nc.tensor.transpose(ps[0:CMP, 4 + r // 4, (r % 4) * P:(r % 4) * P + P],
                                      ce[:, r * CMP:r * CMP + CMP], ident)
        ins.then_inc(cmp_pe_s, 1)
        pe.wait_ge(cmp_act_s, 3)
        for r in range(16):
            ins = nc.tensor.matmul(ps[:, 2 + r // 8, (r % 8) * HD:(r % 8) * HD + HD], ceT[:, r, :], vc[:, r // 8, :],
                                   start=True, stop=True)
        ins.then_inc(cmp_pe_s, 1)

    def cmp_act(act):
        act.wait_ge(cmp_pe_s, 1)
        nc.scalar.activation(kc.rearrange("p g c -> p (g c)"), ps[0:HD, 0, 0:32], ACT.Copy)
        nc.scalar.activation(vc.rearrange("p g c -> p (g c)"), ps[0:CMP, 1, 0:P], ACT.Copy).then_inc(cmp_act_s, 1)
        act.wait_ge(cmp_dve_s, 3)
        nc.scalar.activation(ce, ce, ACT.Exp).then_inc(cmp_act_s, 1)
        act.wait_ge(cmp_pe_s, 3)
        nc.scalar.activation(ceT.rearrange("p r t -> p (r t)"), ps[0:CMP, 4:8, :].rearrange("p b t -> p (b t)"),
                             ACT.Copy).then_inc(cmp_act_s, 1)

    def rows_stick(st, o):
        return nc.vector.tensor_copy(head_cols(st), o)

    def rows_nsa(branch, g0, dc):
        gh = gates.rearrange("p c (h b) -> p b h c", b=3)[:, branch, :, :]

        def out(st, o):
            dst = otok[:, :, bass.ds(st.lin(HD, 512 + g0 * HD), HD)]
            dc.link(nc.vector.tensor_tensor(a_r[:, 0, :], a_r[:, 0, :], gh[:, st.lin(1, g0), :], ALU.mult))
            nc.vector.scalar_tensor_tensor(dst[:, 0, :], o[:, 0, :], a_r[:, 0, 0:1], dst[:, 0, :], ALU.mult, ALU.add)
            return nc.vector.scalar_tensor_tensor(dst[:, 1, :], o[:, 1, :], a_r[:, 0, 1:2], dst[:, 1, :],
                                                  ALU.mult, ALU.add)
        return out

    NSA = [("nsa0w", 0, 2, 30, 640), ("nsa0s", 0, 1, 28, 512), ("nsa1w", 4, 2, 31, 704), ("nsa1s", 4, 1, 29, 576)]

    def hg_act(act, ac):
        act.wait_ge(tile_copied, TC["p_feat"] + 16)
        act.wait_ge(cmp_pe_s, 4)
        act.wait_ge(cmp_dve_s, 5)
        ac.mark(nc.scalar.activation(hq, hq, ACT.Silu))
        ac.mark(nc.scalar.activation(hg, hg, ACT.Silu))
        ac.link(nc.scalar.activation(h_tmp, hf, ACT.Abs))
        ac.link(nc.scalar.activation(h_tmp, h_tmp, ACT.Exp, scale=-1.0))
        nc.scalar.activation(h_tmp, h_tmp, ACT.Ln, bias=1.0).then_inc(hg_act_s, 1)
        act.wait_ge(hg_dve_s, 1)
        nc.scalar.activation(h_k, h_tmp, ACT.Exp)
        act.wait_ge(hg_dve_s, 2)
        nc.scalar.activation(h_q, h_lb, ACT.Exp)
        nc.scalar.activation(h_kn, h_lf, ACT.Exp)
        nc.scalar.activation(h_e, h_lb.rearrange("p a (b t) -> p a b t", t=BLK)[:, :, :, BLK - 1], ACT.Exp)\
            .then_inc(hg_act_s, 1)
        act.wait_ge(hg_pe_s, 1)
        nc.scalar.activation(h_itok, ps[:, 0:2, :], ACT.Copy).then_inc(hg_act_s, 1)
        for a in range(4):
            act.wait_ge(hd_masked, a + 1)
            nc.scalar.activation(h_x, h_x, ACT.Exp).then_inc(hd_exp, 1)
        act.wait_ge(w_used, NBLK)
        for a in range(4):
            nc.scalar.activation(h_att[:, a, 0:T], ps[:, 4 + a, 0:T], ACT.Copy)
            ins = nc.scalar.activation(h_att[:, a, T:T + P], ps[:, 4 + a, T + P:2 * T], ACT.Copy)
        ins.then_inc(hg_act_s, 1)
        act.wait_ge(hg_dve_s, 4)
        nc.scalar.activation(h_tmp, h_o, ACT.Square).then_inc(hg_act_s, 1)
        act.wait_ge(hg_dve_s, 5)
        nc.scalar.activation(h_tmp, h_tmp, ACT.Sqrt).then_inc(hg_act_s, 1)

    def hg_pool(pool):
        pool.wait_ge(o_read, HB["end"])
        nc.gpsimd.memset(h_w, 0.0).then_inc(w_zeroed, 1)
        for a in range(4):
            pool.wait_ge(hd_sub, a + 1)
            nc.gpsimd.affine_select(out=h_x4, in_=h_x4, compare_op=ALU.is_ge, fill=NEG, base=0,
                                    pattern=[[0, NBLK], [1, BLK], [-1, BLK]], channel_multiplier=0)\
                .then_inc(hd_masked, 1)

    def hg_dve(dve, dc):
        dve.wait_ge(hg_act_s, 1)
        dc.link(nc.vector.scalar_tensor_tensor(h_lf, hf, 0.0, h_tmp, ALU.min, ALU.subtract))
        nc.vector.tensor_tensor(h_tmp, h_lf, hf, ALU.subtract).then_inc(hg_dve_s, 1)
        for a in range(4):
            dc.mark(nc.vector.tensor_tensor_scan(h_lb[:, a, :], con_("blkmask"), h_lf[:, a, :], 0.0,
                                                 ALU.mult, ALU.add))
        dc.need()
        b4 = h_lb.rearrange("p a (b t) -> p (a b) t", t=BLK)
        nc.vector.tensor_tensor(h_lf.rearrange("p a (b t) -> p (a b) t", t=BLK),
                                b4[:, :, BLK - 1:BLK].broadcast_to([P, 4 * NBLK, BLK]), b4, ALU.subtract)\
            .then_inc(hg_dve_s, 1)
        dve.wait_ge(hg_act_s, 2)
        nc.vector.tensor_tensor(h_q, h_q, hq, ALU.mult)
        nc.vector.tensor_tensor(h_kn, h_kn, h_k, ALU.mult).then_inc(hg_dve_s, 1)
        dve.wait_ge(hg_dve_s, 3)
        dve.wait_ge(w_zeroed, 1)

        def decay(width):
            def one(st):
                p = st.mod(2)
                if st.s >= 1:
                    dve.wait_ge(w_ready, st.lin(1))
                    dve.wait_ge(w_used, st.lin(1))
                dc.link(nc.vector.tensor_tensor(
                    h_w[:, 1 - p, :, 0:width], h_w[:, p, :, 0:width],
                    h_e[:, :, bass.ds(st.lin(1), 1)].broadcast_to([P, 4, width]), ALU.mult))
                nc.vector.tensor_copy(h_w[:, 1 - p, :, bass.ds(st.lin(BLK), BLK)],
                                      h_kn[:, :, bass.ds(st.lin(BLK), BLK)]).then_inc(w_ready, 1)
            return one

        steps(dve, dc, 0, NBLK // 2, 2, decay(P), first=2, per=1)
        steps(dve, dc, NBLK // 2, NBLK - 1, 2, decay(T), per=1)
        for a in range(4):
            lb = h_lb[:, a, :].rearrange("p (b t) -> p b t", t=BLK)
            kk = h_k[:, a, :].rearrange("p (b t) -> p b t", t=BLK)
            qq = hq[:, a, :].rearrange("p (b t) -> p b t", t=BLK)
            ii = hi[:, a, :].rearrange("p (b t) -> p b t", t=BLK)
            full = [P, NBLK, BLK, BLK]
            if a:
                dve.wait_ge(hd_sum, a)
            nc.vector.tensor_tensor(h_x4, lb.unsqueeze(3).broadcast_to(full), lb.unsqueeze(2).broadcast_to(full),
                                    ALU.subtract).then_inc(hd_sub, 1)
            dve.wait_ge(hd_exp, a + 1)
            dc.link(nc.vector.tensor_tensor(h_x4, h_x4, kk.unsqueeze(2).broadcast_to(full), ALU.mult))
            nc.vector.tensor_tensor(h_x4, h_x4, qq.unsqueeze(3).broadcast_to(full), ALU.mult).then_inc(hd_x, 1)
            dve.wait_ge(hd_sum, a + 1)
            if a:
                dve.wait_ge(hd_red, a)
            dc.link(nc.vector.tensor_tensor(
                h_p.rearrange("p (b t s) -> p b t s", b=NBLK, t=BLK),
                ps[:, 0:4, :].rearrange("p a b -> p (a b)").rearrange("p (b t s) -> p b t s", b=NBLK, t=BLK),
                ii.unsqueeze(2).broadcast_to(full), ALU.mult))
            nc.vector.tensor_reduce(h_od[:, a, :], h_p.rearrange("p (t s) -> p t s", s=BLK), AX.X, ALU.add)\
                .then_inc(hd_red, 1)
        dve.wait_ge(hd_red, 4)
        dve.wait_ge(hg_pe_s, 2)
        for b in range(2):
            ins = nc.vector.tensor_tensor(h_o[:, 2 * b:2 * b + 2, :],
                                          ps[:, b, :].rearrange("p (a t) -> p a t", a=2),
                                          h_od[:, 2 * b:2 * b + 2, :], ALU.add)
        ins.then_inc(hg_dve_s, 1)
        dve.wait_ge(hg_dve_s, 4)
        dve.wait_ge(hg_pe_s, 3)
        tmp2 = h_tmp.rearrange("p a t -> p (a t)")
        dc.link(nc.vector.tensor_scalar(tmp2, ps[:, 2:4, :].rearrange("p a t -> p (a t)"), 1.0 / P, EPS,
                                        ALU.mult, ALU.add))
        nc.vector.reciprocal(tmp2, tmp2).then_inc(hg_dve_s, 1)
        dve.wait_ge(hg_act_s, 6)
        dc.link(nc.vector.tensor_tensor(h_o, h_o, h_tmp, ALU.mult))
        for a in range(4):
            ins = nc.vector.scalar_tensor_tensor(oT[:, 8 + a, :], h_o[:, a, :], par_("hnorm", a), hg[:, a, :],
                                                 ALU.mult, ALU.mult)
        ins.then_inc(hg_dve_s, 1)

    def hg_pe(pe):
        pe.wait_ge(o_read, HB["end"])
        pe.wait_ge(ot_copied, 8)
        for c in range(2):
            for a in range(4):
                ins = nc.tensor.transpose(ps[:, c, a * P:a * P + P], hi[:, a, c * P:c * P + P], ident)
        ins.then_inc(hg_pe_s, 1)
        pe.wait_ge(hg_dve_s, 3)
        pe.wait_ge(w_zeroed, 1)

        def earlier(tiles):
            def one(st):
                if st.s >= 1:
                    pe.wait_ge(w_ready, st.lin(1))
                for a in range(4):
                    for kt in range(tiles):
                        ins = nc.tensor.matmul(ps[:, 4 + a, bass.ds(st.lin(BLK, kt * T), BLK)],
                                               h_w[:, st.mod(2), a, kt * P:kt * P + P],
                                               h_q[:, a, bass.ds(st.lin(BLK), BLK)], start=True, stop=True)
                ins.then_inc(w_used, 1)
            return one

        steps(pe, None, 0, NBLK // 2, 2, earlier(1), first=2)
        steps(pe, None, NBLK // 2, NBLK, 2, earlier(2))
        for a in range(4):
            pe.wait_ge(hd_x, a + 1)
            if a:
                pe.wait_ge(hd_red, a)
            else:
                pe.wait_ge(hg_act_s, 3)
            for b in range(4):
                ins = nc.tensor.matmul(ps[:, b, :], ones[:, 0:P], h_x[:, b * 512:b * 512 + 512], start=True, stop=True)
            ins.then_inc(hd_sum, 1)
        pe.wait_ge(hd_red, 4)
        pe.wait_ge(hg_act_s, 4)
        for a in range(4):
            out = ps[:, a // 2, (a % 2) * T:(a % 2) * T + T]
            nc.tensor.matmul(out, h_itok[:, 0, a * P:a * P + P], h_att[:, a, 0:T], start=True, stop=False)
            ins = nc.tensor.matmul(out[:, P:T], h_itok[:, 1, a * P:a * P + P], h_att[:, a, T:T + P],
                                   start=False, stop=True)
        ins.then_inc(hg_pe_s, 1)
        pe.wait_ge(hg_act_s, 5)
        tmp2 = h_tmp.rearrange("p a t -> p (a t)")
        for b in range(2):
            ins = nc.tensor.matmul(ps[:, 2 + b, :], ones[:, 0:P], tmp2[:, b * 512:b * 512 + 512], start=True, stop=True)
        ins.then_inc(hg_pe_s, 1)

    def merge_at(j, k):
        return 6, CH["merge"] + k - (1 if j > 0 else 0)

    def merge_pe(pe):
        pe.wait_ge(hg_dve_s, 6)
        n = KD

        def one(st):
            if st.s < n:
                def gate(i, k):
                    if st.s >= 1:
                        pe.wait_ge(branch_taken, st.lin(3, i - 2))
                    up(pe, arrived(pe, st, *merge_at(st.s, k)), ps[:, 4 + i, 0:T])

                gate(0, 0)
                gate(1, 1)
                r = arrived(pe, st, *merge_at(st.s, 2))
                up(pe, r, ps[:, 4, T:2 * T], 0, 4, oT[:, 0:4, :], inc=False)
                up(pe, r, ps[:, 5, T:2 * T], 4, 4, oT[:, 4:8, :])
                gate(2, 3)
                up(pe, arrived(pe, st, *merge_at(st.s, 4)), ps[:, 6, T:2 * T], 0, 4, oT[:, 8:12, :])
            if st.s >= 1:
                pe.wait_ge(z_ready, st.lin(1, ZB["merge"]))
                down(pe, arrived(pe, st, 6, CH["merge"] + (4 if st.s < n else -1)), z, st.s == 1, st.s == n)

        steps(pe, None, 0, n, 1, one, first=2)
        one(Step(n))

    def merge_act(act):
        def one(st):
            for i, k in enumerate((2, 2, 4)):
                a, b = merge_at(st.s, k)
                act.wait_ge(chunk_done, st.lin(a, b + 1))
                if st.s >= 1:
                    act.wait_ge(branch_taken, st.lin(3, i - 2))
                nc.scalar.activation(sg[:, i, :], ps[:, 4 + i, 0:T], ACT.Sigmoid).then_inc(sg_ready, 1)

        steps(act, None, 0, KD, 1, one, first=2)

    def merge_dve(dve, dc):
        def one(st):
            if st.s >= 1:
                dve.wait_ge(z_ready, st.lin(1, ZB["merge"]))
            for i, k in enumerate((2, 2, 4)):
                a, b = merge_at(st.s, k)
                dve.wait_ge(chunk_done, st.lin(a, b + 1))
                dve.wait_ge(sg_ready, st.lin(3, i + 1))
                if i == 2:
                    dc.link(nc.vector.tensor_tensor(conv_g, conv_g, conv_u, ALU.add))
                nc.vector.tensor_tensor(conv_u if i else conv_g, sg[:, i, :], ps[:, 4 + i, T:2 * T], ALU.mult)\
                    .then_inc(branch_taken, 1)
                dve.wait_ge(branch_taken, st.lin(3, i + 1))
            if st.s >= 1:
                dve.wait_ge(chunk_done, st.lin(6, CH["merge"] + 5))
            nc.vector.tensor_tensor(z, conv_g, conv_u, ALU.add).then_inc(z_ready, 1)

        steps(dve, dc, 0, KD, 1, one, first=2, per=1)
        dve.wait_ge(chunk_done, CH["merge"] + 6 * KD)

    def peer_scores_pe(pe):
        pe.wait_ge(tile_copied, TC["pq"] + KD)
        pe.wait_ge(s_small, 16 * 6)
        for c in range(2):
            for a in range(PH):
                ins = nc.tensor.matmul(ps[:, 4 * c + a // 2, (a % 2) * T:(a % 2) * T + T], t_q[:, a, c * P:c * P + P],
                                       keys_s, start=True, stop=True)
                if a % 2:
                    ins.then_inc(tk_pe, 1)

    def peer_top_act(act):
        for b in range(8):
            act.wait_ge(tk_pe, b + 1)
            nc.scalar.activation(t_s[:, 4 * b:4 * b + 4, :], ps[:, b, :].rearrange("p (r k) -> p r k", r=4),
                                 ACT.Copy).then_inc(tk_act, 1)
        act.wait_ge(tk_dve, 1)
        nc.scalar.activation(t_g, t_g, ACT.Exp).then_inc(tk_act, 1)
        act.wait_ge(tk_pe, 9)
        nc.scalar.activation(idx, ps[:, 0:3, 0:T], ACT.Copy).then_inc(tk_act, 1)

    def top16(dve, dc, rows, src, best, where, n):
        for lo in range(0, rows, 8):
            rs = range(lo, min(lo + 8, rows))
            for r in rs:
                dc.mark(nc.vector.max(best[:, r, 0:8], src[:, r, :]))
            dc.need()
            for r in rs:
                dc.mark(nc.vector.max_index(where[:, r, 0:8], best[:, r, 0:8], src[:, r, :]))
            dc.need()
            for r in rs:
                dc.mark(nc.vector.match_replace(src[:, r, :], best[:, r, 0:8], src[:, r, :], -3e38))
            dc.need()
            for r in rs:
                dc.mark(nc.vector.max(best[:, r, 8:16], src[:, r, :]))
            dc.need()
            for r in rs:
                dc.mark(nc.vector.max_index(where[:, r, 8:16], best[:, r, 8:16], src[:, r, :]))
            dc.need()

    def peer_top_dve(dve, dc):
        dve.wait_ge(tk_act, 8)
        top16(dve, dc, 32, t_s, t_b, t_i, NKEY)
        dc.link(nc.vector.tensor_copy(t_if, t_i))
        for c in range(2):
            b = t_b.rearrange("p (c a h) k -> p c a h k", c=2, h=2)[:, c]
            dc.mark(nc.vector.tensor_tensor(
                t_c[:, 8 * c:8 * c + 8, :].rearrange("p a (i j) -> p a i j", i=TOPK),
                b[:, :, 0, :].unsqueeze(3).broadcast_to([P, PH, TOPK, TOPK]),
                b[:, :, 1, :].unsqueeze(2).broadcast_to([P, PH, TOPK, TOPK]), ALU.add))
        dc.need()
        top16(dve, dc, 16, t_c, t_g, t_w, TOPK * TOPK)
        dc.mark(nc.vector.tensor_scalar(t_wi, t_w, 4, None, ALU.logical_shift_right))
        dc.link(nc.vector.tensor_scalar(t_wj, t_w, 15, None, ALU.bitwise_and))
        dc.mark(nc.vector.tensor_copy(t_wf[:, 0], t_wi))
        dc.mark(nc.vector.tensor_copy(t_wf[:, 1], t_wj))
        dc.mark(nc.vector.tensor_copy(t_m, t_g[:, :, 0:1]))
        dc.need()
        nc.vector.tensor_tensor(t_g, t_g, t_m.broadcast_to([P, 16, TOPK]), ALU.subtract).then_inc(tk_dve, 1)
        for half in range(2):
            for c in range(2):
                w = t_wf[:, half, 8 * c:8 * c + 8, :].rearrange("p a k -> p (a k)")
                dc.link(nc.vector.tensor_tensor(t_1, con_("iota16").unsqueeze(1).broadcast_to([P, P, TOPK]),
                                                w.unsqueeze(2).broadcast_to([P, P, TOPK]), ALU.is_equal))
                t14 = t_1.rearrange("p (a k) i -> p a k i", a=PH)
                f = t_if.rearrange("p (c a h) k -> p c h a k", c=2, h=2)[:, c, half]
                dc.link(nc.vector.tensor_tensor(t14, t14, f.unsqueeze(2).broadcast_to([P, PH, TOPK, TOPK]), ALU.mult))
                dc.link(nc.vector.tensor_reduce(t_key[:, half, c, :], t_1, AX.X, ALU.add))
        dve.wait_ge(tk_act, 9)
        dc.link(nc.vector.tensor_reduce(t_m, t_g, AX.X, ALU.add))
        dc.link(nc.vector.reciprocal(t_m, t_m))
        nc.vector.tensor_tensor(t_key[:, 2, :, :].rearrange("p c (a k) -> p (c a) k", a=PH), t_g,
                                t_m.broadcast_to([P, 16, TOPK]), ALU.mult).then_inc(tk_dve, 1)

    def peer_turn_pe(pe):
        pe.wait_ge(tk_dve, 2)
        for i in range(3):
            for c in range(2):
                ins = nc.tensor.transpose(ps[:, i, c * P:c * P + P], t_key[:, i, c, :], ident)
        ins.then_inc(tk_pe, 1)

    def gmap_dve(dve, dc):
        dve.wait_ge(tk_act, 10)

        def one(st):
            p = st.mod(2)
            if st.s >= 2:
                dve.wait_ge(gm_done, st.lin(1, -1))
            for q in range(4):
                nc.vector.tensor_scalar(hot_a[:, 4 * p + q, :], con_("iota"), idx[:, 0, bass.ds(st.lin(4, q), 1)],
                                        idx[:, 2, bass.ds(st.lin(4, q), 1)], ALU.is_equal, ALU.mult)
                ins = nc.vector.tensor_scalar(hot_b[:, 4 * p + q, :], con_("iota"), idx[:, 1, bass.ds(st.lin(4, q), 1)],
                                              None, ALU.is_equal)
            ins.then_inc(hot_ready, 1)

        steps(dve, dc, 0, T // 4, 2, one, first=2)

    def gmap_pe(pe):
        def one(st):
            p = st.mod(2)
            pe.wait_ge(hot_ready, st.lin(1, 1))
            if st.s >= 2:
                pe.wait_ge(gm_copied, st.lin(1, -1))
            for q in range(4):
                ins = nc.tensor.matmul(ps[:, 4 + p, q * P:q * P + P], hot_b[:, 4 * p + q, :], hot_a[:, 4 * p + q, :],
                                       start=True, stop=True)
            ins.then_inc(gm_done, 1)

        steps(pe, None, 0, T // 4, 2, one, first=2)

    def gmap_act(act):
        def one(st):
            act.wait_ge(gm_done, st.lin(1, 1))
            nc.scalar.activation(gmap[:, bass.ds(st.lin(4 * NKEY), 4 * NKEY)], ps[:, 4 + st.mod(2), :],
                                 ACT.Copy).then_inc(gm_copied, 1)

        steps(act, None, 0, T // 4, 2, one, first=2)

    def peer_act(act):
        def one(st):
            a, b = up_at("peer", 2, st.s, 0)
            act.wait_ge(chunk_done, st.lin(a, b + 1))
            if st.s >= 1:
                act.wait_ge(z_ready, st.lin(1, ZB["peer"]))
            nc.scalar.activation(silu_o, bank(st.mod(2), 0), ACT.Gelu).then_inc(gelu_done, 1)

        steps(act, None, 0, NKEY, 2, one, first=2)

    def peer_dve(dve):
        g3 = gmap.rearrange("p (t a) -> p t a", a=NKEY)
        dve.wait_ge(gm_copied, T // 4)

        def one(st):
            dve.wait_ge(gelu_done, st.lin(1, 1))
            if st.s >= 1:
                a, b = down_at("peer", 2, NKEY, st.s)
                dve.wait_ge(chunk_done, st.lin(a, b + 1))
            nc.vector.tensor_tensor(z.unsqueeze(2), silu_o.unsqueeze(2), g3[:, :, bass.ds(st.lin(1), 1)], ALU.mult)\
                .then_inc(z_ready, 1)

        steps(dve, None, 0, NKEY, 2, one, first=2)
        dve.wait_ge(chunk_done, CH["peer"] + 2 * NKEY)

    with nc.Block() as block:
        @block.sync
        def _(sp):
            sp.dma_start(x[:, :, :], xT).then_inc(s_x, 16)
            sp.dma_start(tabs[:, :], par).then_inc(s_par, 16)
            sp.dma_start(cons[:, :], con).then_inc(s_par, 16)
            stream_all(sp)
            sp.wait_ge(h_ready, 8)
            sp.dma_start(y, x[:, :, :]).then_inc(s_y, 16)
            sp.wait_ge(s_y, 16)

        @block.gpsimd
        def _(pool):
            nc.gpsimd.memset(ones[:, :], 1.0).then_inc(s_ones, 1)
            nc.gpsimd.memset(keys_s, 0.0).then_inc(pool_c, 1)
            pool.dma_start(wg_s, wg).then_inc(s_small, 16)
            pool.dma_start(wk_s, wcmpk).then_inc(s_small, 16)
            pool.dma_start(wv_s, wcmpv).then_inc(s_small, 16)
            pool.dma_start(pe_s, peT).then_inc(s_small, 16)
            pool.wait_ge(pool_c, 1)
            pool.dma_start(keys_s[0:HD, 0:NKEY], subk[0, :, :]).then_inc(s_small, 16)
            pool.dma_start(keys_s[HD:P, NKEY:2 * NKEY], subk[1, :, :]).then_inc(s_small, 16)
            pool.wait_ge(rope_done, 16)
            heads_pool(pool, HB["moba"], 16, lambda st: heads[:, st.lin(1), :])
            pool.wait_ge(tile_copied, TC["p_tok"])
            heads_pool(pool, HB["sb"], 8, lambda st: heads[:, st.lin(1), :])
            for name, g0, *_ in NSA:
                heads_pool(pool, HB[name], 4, lambda st, g0=g0: heads[:, st.lin(1, 16 + g0), :])
            hg_pool(pool)

        @block.tensor
        def _(pe):
            pe.wait_ge(s_ones, 1)
            pe.wait_ge(s_par, 32)
            norm_pe(pe, 0)
            gated_pe(pe, "sc", KD, 3, 6, z_ready, 0, 1)
            norm_pe(pe, 4)
            gated_pe(pe, "ffn0", NF, 2, 2, conv_u_done, 0, 2)
            norm_pe(pe, 8)
            qk_pe(pe)
            project_pe(pe, "qkv", 8, tokens_out=True, skip=16)
            pe.wait_ge(tile_copied, 24)
            heads_pe(pe, HB["moba"], 16, lambda st: heads[:, st.lin(1, 16), :],
                     lambda st, c: vtok[:, c, bass.ds(st.lin(HD), HD)], 1)
            pe.wait_ge(o_read, 16)
            turn_out_pe(pe, 0)
            wo_pe(pe)
            norm_pe(pe, 12)
            gated_pe(pe, "ffn1", NF, 2, 2, conv_u_done, NF, 4)
            norm_pe(pe, 16)
            norm_pe(pe, 20)
            pe.wait_ge(h_ready, 6)
            project_pe(pe, "p_split", 16)
            project_pe(pe, "p_tok", 6, tokens_out=True)
            project_pe(pe, "p_feat", 16)
            pe.wait_ge(s_small, 16 * 6)
            gates_pe(pe)
            pe.wait_ge(tile_copied, TC["p_feat"] + 16)
            cmp_pe(pe)
            pe.wait_ge(cmp_dve_s, 5)
            heads_pe(pe, HB["sb"], 8, lambda st: heads[:, st.lin(1, 8), :],
                     lambda st, c: vtok[:, c, bass.ds(st.lin(HD), HD)], 2)
            for name, g0, br, kh, vcol in NSA:
                heads_pe(pe, HB[name], 4, lambda st, kh=kh: heads[:, kh, :],
                         lambda st, c, vcol=vcol: vtok[:, c, vcol:vcol + HD], 1)
            pe.wait_ge(o_read, HB["end"])
            turn_out_pe(pe, 4)
            hg_pe(pe)
            merge_pe(pe)
            norm_pe(pe, 24)
            pe.wait_ge(h_ready, 7)
            project_pe(pe, "pq", KD)
            peer_scores_pe(pe)
            peer_turn_pe(pe)
            gmap_pe(pe)
            pe.wait_ge(gm_copied, T // 4)
            gated_pe(pe, "peer", NKEY, 1, 6, gelu_done, 0, 7)
            norm_pe(pe, 28)

        @block.scalar
        def _(act):
            ac = Chain(act, act_c)
            norm_act(act, 0, s_x, 16)
            sc_act(act)
            norm_act(act, 1, x_part, 0)
            ffn_act(act, "ffn0", 0)
            norm_act(act, 2, x_part, 4)
            qk_act(act)
            project_act(act, ac, "qkv", 8, copy_tokens, vtok, 16, skip=16)
            soft_act(act, HB["moba"], 16)
            turn_out_act(act, 0)
            norm_act(act, 3, x_part, 8)
            ffn_act(act, "ffn1", NF)
            norm_act(act, 4, x_part, 12)
            norm_act(act, 5, h_ready, 5)
            project_act(act, ac, "p_split", 16, copy_heads, heads)
            project_act(act, ac, "p_tok", 6, copy_tokens, vtok, 0)
            project_act(act, ac, "p_feat", 16, copy_feat, hfeat)
            gates_act(act)
            cmp_act(act)
            stick_act(act, ac, HB["sb"], 8)
            for name, *_ in NSA:
                soft_act(act, HB[name], 4)
            turn_out_act(act, 4)
            hg_act(act, ac)
            merge_act(act)
            norm_act(act, 6, x_part, 16)
            project_act(act, ac, "pq", KD, copy_feat, t_q)
            peer_top_act(act)
            gmap_act(act)
            peer_act(act)
            norm_act(act, 7, x_part, 20)

        @block.vector
        def _(dve):
            dc = Chain(dve, dve_c)
            dve.wait_ge(s_par, 32)
            norm_dve(dve, dc, 0, "mix0", h)
            sc_dve(dve, dc)
            residual_dve(dve, dc)
            norm_dve(dve, dc, 1, "ffn0", h)
            ffn_dve(dve, dc, "ffn0", "fconv0", 0)
            residual_dve(dve, dc)
            norm_dve(dve, dc, 2, "mix1", h)
            qk_dve(dve, dc)
            soft_dve(dve, dc, HB["moba"], 16, lambda st: con_("causal"), rows_soft, 1)
            dve.wait_ge(chunk_done, CH["wo"] + KD)
            residual_dve(dve, dc)
            norm_dve(dve, dc, 3, "ffn1", h)
            ffn_dve(dve, dc, "ffn1", "fconv1", NF)
            residual_dve(dve, dc)
            norm_dve(dve, dc, 4, "fin1", x)
            norm_dve(dve, dc, 5, "mix2", h)
            cmp_dve(dve, dc)
            stick_dve(dve, dc, HB["sb"], 8, rows_stick)
            for name, g0, br, kh, vcol in NSA:
                dve.wait_ge(o_read, HB[name])
                soft_dve(dve, dc, HB[name], 4,
                         lambda st, g0=g0: con_("alibi").rearrange("p (h s) -> p h s", h=8)[:, st.lin(1, g0), :],
                         rows_nsa(br, g0, dc), 2)
            hg_dve(dve, dc)
            merge_dve(dve, dc)
            residual_dve(dve, dc)
            norm_dve(dve, dc, 6, "ffn2", h)
            peer_top_dve(dve, dc)
            gmap_dve(dve, dc)
            peer_dve(dve)
            residual_dve(dve, dc)
            norm_dve(dve, dc, 7, "fin2", x)


_PARAMS = ("xT", "par", "con", "wg", "wcmpk", "wcmpv", "peT", "subk")


def constants():
    c = np.zeros((P, NCON), np.float32)

    def put(name, a):
        a = np.asarray(a, np.float32).reshape(P, -1)
        c[:, COFF[name]:COFF[name] + a.shape[1]] = a

    p = np.arange(P)
    put("ident", np.eye(P))
    swap = np.zeros((P, P))
    swap[p ^ 32, p] = 1.0
    put("swap", swap)
    half = HD // 2
    inv = (10000.0 ** (-np.arange(half, dtype=np.float32) / np.float32(half))).astype(np.float32)
    ang = inv[p % half][:, None] * np.arange(T, dtype=np.float32)[None, :]
    ang = ang.astype(np.float32)
    put("cos", np.cos(ang))
    put("sin", np.sin(ang) * np.where(p % HD < half, -1.0, 1.0)[:, None])
    t = np.concatenate([np.broadcast_to(p[:, None], (P, P)), np.broadcast_to(p[:, None] + P, (P, T))], 1)
    k = np.concatenate([np.broadcast_to(np.arange(P)[None], (P, P)), np.broadcast_to(np.arange(T)[None], (P, T))], 1)
    put("causal", np.where(k <= t, 0.0, NEG))
    put("strict", np.where(k < t, 0.0, NEG))
    slopes = 2.0 ** (-(np.arange(8) + 1.0))
    put("alibi", np.stack([np.where(k <= t, -s * (t - k), NEG) for s in slopes], 1))
    tok = p[:, None, None, None] + P * np.arange(2)[None, None, :, None]
    dist = tok - (16 * np.arange(CMP)[None, None, None, :] + 31)
    ok = (dist >= 0) & (np.arange(CMP) < CMP - 1)
    put("cmpbias", np.where(ok, -slopes[None, :, None, None] * dist, NEG))
    put("rowok", (p[:, None] + P * np.arange(2)[None] >= 31) * 1.0)
    put("blkmask", np.broadcast_to((np.arange(T) % BLK != 0) * 1.0, (P, T)))
    put("iota", np.broadcast_to(np.arange(P), (P, P)))
    put("iota16", np.broadcast_to(np.arange(TOPK), (P, TOPK)))
    return c


def up_chunks(w, cols):
    w = w[:, cols] if not isinstance(cols, slice) or cols != slice(None) else w
    n = w.shape[1] // P
    return w.reshape(KD, P, n, P).transpose(2, 1, 0, 3).reshape(n, P, D)


def interleave(ups, downs):
    out = []
    for j in range(len(ups)):
        out += list(ups[j])
        if j:
            out.append(downs[j - 1])
    return out + [downs[-1]]


def lay_out(a):
    w = {k: np.asarray(v) for k, v in a.items()}
    s = []
    b = up_chunks(w["sc_w_in"][0], slice(None))
    s += interleave([(b[j], b[KD + j], b[2 * KD + j]) for j in range(KD)], w["sc_w_out"][0].reshape(KD, P, D))

    def ffn(i):
        b = up_chunks(w["ffn_w_up"][i], slice(None))
        return interleave([(b[j], b[NF + j]) for j in range(NF)], w["ffn_w_down"][i].reshape(NF, P, D))

    s += ffn(0)
    s += list(up_chunks(w["moba_w_qkv"][0], slice(None)))
    s += list(w["moba_w_o"][0].reshape(KD, P, D))
    s += ffn(1)
    win = w["w_in_2"][0]
    kv = 2048
    hg = kv + 768 + 24
    s += list(up_chunks(win[:, 0:1024], slice(None)))
    s += list(up_chunks(win[:, 1536:2048], slice(None)))
    for i in (0, 1, 2, 4):
        s += list(up_chunks(win[:, kv + i * P:kv + i * P + P], slice(None)))
    s += list(up_chunks(win[:, 1024:1536], slice(None)))
    for i in (3, 5):
        s += list(up_chunks(win[:, kv + i * P:kv + i * P + P], slice(None)))
    s += list(up_chunks(win[:, hg:hg + 2048], slice(None)))
    gm = up_chunks(win[:, hg + 2048:], slice(None))
    br = [w[n][0].reshape(4, P, KD, P).transpose(2, 1, 0, 3).reshape(KD, P, 4 * P)
          for n in ("w_branch_sb_2", "w_branch_nsa_2", "w_branch_hgrn_2")]
    pad = np.zeros((P, 4 * P), np.float32)
    s += interleave([(gm[j], gm[KD + j], np.concatenate([br[0][j], br[1][j]], 1), gm[2 * KD + j],
                      np.concatenate([br[2][j], pad], 1)) for j in range(KD)],
                    w["w_out_2"][0].reshape(KD, P, D))
    s += list(up_chunks(w["peer_w_q_2"][0], slice(None)))
    u = w["peer_u_2"][0].reshape(NKEY, NKEY, KD, P).transpose(0, 3, 2, 1).reshape(NKEY, P, D)
    v = w["peer_v_2"][0].reshape(NKEY, NKEY, D)
    s += interleave([(u[j],) for j in range(NKEY)], v)
    stream = np.empty((len(s), P, D), np.float32)
    for i, c in enumerate(s):
        stream[i] = c
    par = np.zeros((P, NPAR), np.float32)

    def put(name, a):
        a = a.reshape(P, -1)
        par[:, POFF[name]:POFF[name] + a.shape[1]] = a

    def vec(v):
        return v.reshape(-1, P).T

    def taps(v):
        return v.reshape(3, -1, P).transpose(2, 1, 0)

    for name, v in (("mix0", w["mix_norm"][0]), ("mix1", w["mix_norm"][1]), ("ffn0", w["ffn_norm"][0]),
                    ("ffn1", w["ffn_norm"][1]), ("fin1", w["final_norm"]), ("mix2", w["norm_mix_2"][0]),
                    ("ffn2", w["norm_ffn_2"][0]), ("fin2", w["norm_final_2"]), ("hnorm", w["hgrn_norm_2"][0])):
        put(name, vec(v))
    put("sconv", taps(w["sc_w_conv"][0]))
    put("fconv0", taps(w["ffn_w_conv"][0]))
    put("fconv1", taps(w["ffn_w_conv"][1]))
    return {
        "stream": stream,
        "xT": w["x"][0].T.reshape(KD, P, T).transpose(1, 0, 2),
        "par": par,
        "con": constants(),
        "wg": win[:, kv + 768:hg].reshape(KD, P, 24).transpose(1, 0, 2),
        "wcmpk": w["nsa_w_cmp_k_2"][0].reshape(32, HD, HD).transpose(1, 0, 2),
        "wcmpv": w["nsa_w_cmp_v_2"][0].reshape(32, HD, HD).transpose(1, 0, 2),
        "peT": w["nsa_cmp_pe_2"][0].T,
        "subk": w["peer_sub_keys_2"][0].transpose(0, 2, 1),
    }


def kernel(**inputs):
    import concourse.bacc as bacc
    from concourse.bass_utils import run_bass_kernel_spmd as run

    nc = bacc.Bacc("TRN2", target_bir_lowering=False, num_devices=1)
    arrays, args = {}, []
    for name, a in lay_out(inputs).items():
        a = np.ascontiguousarray(a)
        arrays[name] = a
        args.append(nc.dram_tensor(name, a.shape, F32, kind="ExternalInput").ap())
    y = nc.dram_tensor("y", (P, KD, T), F32, kind="ExternalOutput").ap()
    build(nc, *args, y)
    r = run(nc, [arrays], core_ids=[0])
    return r.results[0]["y"].transpose(2, 1, 0).reshape(1, T, D)
```

```python
import numpy as np
import concourse.bass as bass
from concourse import mybir

F32 = mybir.dt.float32
F32R = mybir.dt.float32r
BF16 = mybir.dt.bfloat16
U32 = mybir.dt.uint32
ALU = mybir.AluOpType
ACT = mybir.ActivationFunctionType
AX = mybir.AxisListType

P = 128
T = 256
D = 1024
KD = D // P
FF = 2816
NF = FF // P
HD = 64
EPS = 1e-6
NEG = -1e30
SCALE = HD ** -0.5
RING = 3
CUT = 672
LEVELS = [1 << l for l in range(8)]
NKEY = 128
TOPK = 16
PH = 8
CMP = 16
SC3 = 384

PARTS = [("mix0", KD), ("mix1", KD), ("ffn0", KD), ("ffn1", KD), ("fin1", KD), ("mix2", KD),
         ("ffn2", KD), ("fin2", KD), ("sconv", KD * 3), ("fconv0", 2 * NF * 3), ("fconv1", 2 * NF * 3),
         ("hnorm", 4)]
POFF = {}
_o = 0
for _n, _w in PARTS:
    POFF[_n] = _o
    _o += _w
NPAR = _o
CPARTS = [("ident", P), ("iota", P), ("iota16", TOPK), ("swap", P), ("cos", T), ("sin", T),
          ("causal", SC3), ("strict", SC3), ("cmpbias", 8 * 2 * CMP), ("pairs", (len(LEVELS) - 2) * P), ("rowok", 2)]
COFF = {}
_o = 0
for _n, _w in CPARTS:
    COFF[_n] = _o
    _o += _w
NCON = _o


class Step:

    def __init__(self, s, stride=0, i=None):
        self.s, self.stride, self.i = s, stride, i

    def lin(self, a, b=0):
        v = a * self.s + b
        return v if self.i is None else self.i * (a * self.stride) + v

    def mod(self, n, a=1, b=0):
        assert self.i is None or (a * self.stride) % n == 0
        return (a * self.s + b) % n

    def div(self, n, a=1, b=0):
        assert self.i is None or (a * self.stride) % n == 0
        v = (a * self.s + b) // n
        return v if self.i is None else self.i * (a * self.stride // n) + v


class Chain:

    def __init__(self, eng, sem):
        self.eng, self.sem, self.n, self.per, self.i = eng, sem, 0, 0, None

    def mark(self, ins):
        ins.then_inc(self.sem, 1)
        self.n += 1
        return self.n

    def need(self, k=None):
        k = self.n if k is None else k
        self.eng.wait_ge(self.sem, k if self.i is None else self.i * self.per + k)

    def link(self, ins):
        self.mark(ins)
        self.need()


def steps(eng, chain, lo, hi, body, fn, first=0, per=0):
    n = lo
    while n < min(first, hi):
        fn(Step(n))
        n += 1
    turns = (hi - n) // body
    if turns > 1:
        with eng.Fori(0, turns) as i:
            if chain is not None:
                at = chain.n
                chain.i, chain.per = i, per * body
            for u in range(body):
                fn(Step(n + u, body, i))
            if chain is not None:
                assert chain.n - at == per * body, (chain.n - at, per, body)
                chain.n = at + per * body * turns
                chain.i = None
        n += body * turns
    while n < hi:
        fn(Step(n))
        n += 1


def chunk_plan():
    at, out = 0, {}
    for name, n in [("sc", 4 * KD), ("ffn0", 3 * NF), ("qkv", 24), ("wo", KD), ("ffn1", 3 * NF),
                    ("p_split", 16), ("p_tok", 6), ("p_feat", 16), ("merge", 6 * KD),
                    ("pq", KD), ("peer", 2 * NKEY)]:
        out[name] = at
        at += n
    out["end"] = at
    return out


CH = chunk_plan()
UP0, DOWN0 = CH["peer"], CH["peer"] + NKEY
HALF = NKEY // 2
GT = 8


def build(nc, stream, xT, par, con, alibi_t, wg, wcmpk, wcmpv, peT, subk, y):
    def sem(name):
        return nc.alloc_semaphore(name)

    def sb(name, shape, dt=F32):
        return nc.alloc_sbuf_tensor(name, shape, dt)

    base = (nc.sbuf_base + 63) // 64 * 64
    END = (nc.sbuf_usable_end - base) // 32 * 8
    names = {}

    def at(o, *dims, parts=P, dt=F32):
        n = int(np.prod(dims))
        assert o >= 0 and o + n <= END, (o, n, END)
        name = f"m{o}_{len(names)}"
        names[name] = 1
        v = nc.alloc_sbuf_tensor_at(name, [parts, n], dt, offset=base + 4 * o)[:, :]
        if len(dims) == 2:
            v = v.rearrange("p (a b) -> p a b", a=dims[0])
        elif len(dims) == 3:
            v = v.rearrange("p (a b c) -> p a b c", a=dims[0], b=dims[1])
        elif len(dims) == 4:
            v = v.rearrange("p (a b c d) -> p a b c d", a=dims[0], b=dims[1], c=dims[2])
        return v

    class Area:

        def __init__(self, at_, end=END):
            self.at, self.end = at_, end

        def take(self, *dims, parts=P, dt=F32):
            o = self.at
            size = int(np.prod(dims)) // (2 if dt == BF16 else 1)
            self.at += (size + 7) // 8 * 8
            assert self.at <= self.end, (self.at, self.end)
            return at(o, *dims, parts=parts, dt=dt)

    l_ = Area(0)
    raw = l_.take(RING, D)
    w_hi, w_lo = l_.take(RING, D, dt=F32R), l_.take(RING, D, dt=F32R)
    x = l_.take(KD, T)
    h_hi, h_lo = l_.take(KD, T, dt=F32R), l_.take(KD, T, dt=F32R)
    z_hi, z_lo = l_.take(T, dt=F32R), l_.take(T, dt=F32R)
    tabs = l_.take(NPAR)
    ones = l_.take(T)
    O_NORM = l_.at
    norm_t, rstd = l_.take(T), l_.take(T)
    O_CONS = l_.at
    cons = l_.take(NCON)
    A0 = l_.at

    def con_(name, n=None):
        o = COFF[name]
        return cons[:, o:o + (n or dict(CPARTS)[name])]

    def par_(name, a, n=1):
        return tabs[:, bass.ds(a + POFF[name], n)]

    ident = con_("ident")
    ps = nc.alloc_psum_tensor("ps", [P, 8, 512], F32)
    acc = ps[:, 0:4, :]

    f_ = Area(END - 8 * T)
    conv_g, conv_u, copied, rope_a, rope_b = f_.take(T), f_.take(T), f_.take(2, T), f_.take(T), f_.take(T)
    silu_o, z_f = f_.take(T), f_.take(T)
    sg = at(END - 6 * T, 3, T)
    m_ = Area(A0)
    heads = m_.take(32, T, parts=HD)
    vtok = m_.take(2, D)
    otok = m_.take(2, D)
    O_ATT = m_.at
    a_s, a_e, a_t, a_l = (m_.take(2, SC3) for _ in range(4))
    a_q = m_.take(2, T, parts=HD)
    a_max = m_.take(2, 2)
    a_sum = m_.take(64, 2)
    a_r = m_.take(1, 2)
    a_c = m_.take(SC3)
    O_OT = m_.at
    oT_hi, oT_lo = m_.take(12, T, dt=F32R), m_.take(12, T, dt=F32R)
    O_HF = m_.at
    hfeat = m_.take(16, T)
    gates = m_.take(2, 24)
    wg_s = m_.take(KD, 24)
    SCR = m_.at
    sq, h_f = at(O_HF, KD, T), at(O_HF + KD * T, KD, T)
    c_ = Area(O_OT, O_HF)
    wk_s, wv_s = c_.take(32, HD, parts=HD), c_.take(32, HD, parts=HD)
    pe_s = c_.take(32, parts=HD)
    kc, vc = c_.take(2, CMP, parts=HD), c_.take(2, HD, parts=CMP)
    ce, cm = c_.take(16 * CMP), c_.take(16)
    ceT = at(O_ATT, 16, P, parts=CMP)
    s_ = Area(SCR)
    alibi = s_.take(8, SC3)
    blk_k, blk_v = s_.take(32, 2, CMP, parts=HD), s_.take(32, 2, CMP, parts=HD)
    hq, hf, hi, hg = (hfeat[:, 4 * i:4 * i + 4, :] for i in range(4))
    g_ = Area(SCR)
    h_tmp, h_lf, h_k, h_lb = (g_.take(4, T) for _ in range(4))
    h_o = h_lb
    g2_ = Area(A0, O_ATT - 2 * D)
    lv_q, lv_k = g2_.take(2, 4 * P), g2_.take(2, 4 * P)
    lv_a, lv_i = g2_.take(2, 4, P), g2_.take(2, 4 * P)
    lv_v = g2_.take(2, 4 * P)
    h_c, h_r = h_lf, at(O_ATT, 4, T)

    emap = at(A0, NKEY, T)
    assert A0 + T * NKEY <= END
    t_ = Area(A0 + HALF * T, A0 + NKEY * T)
    O_TQ = t_.at
    t_q, t_s = t_.take(PH, T), t_.take(32, NKEY)
    t_1 = at(O_TQ, P, TOPK)
    t_b, t_if = t_.take(32, TOPK), t_.take(32, TOPK)
    t_i = t_.take(32, TOPK).bitcast(U32)
    t_c = t_.take(16, TOPK * TOPK)
    t_g = t_.take(16, TOPK)
    t_w, t_wi, t_wj = (t_.take(16, TOPK).bitcast(U32) for _ in range(3))
    t_wf = t_.take(2, 16, TOPK)
    t_m = t_.take(16, 1)
    t_key = t_.take(3, 2, P)
    keys_s = t_.take(2 * NKEY)
    b_ = Area(O_CONS + COFF["swap"], O_CONS + COFF["rowok"])
    idx = b_.take(2, T, dt=BF16)
    gate_left = b_.take(1, T)
    gate_part = b_.take(3, T, dt=BF16)
    iota_b = b_.take(P, dt=BF16)
    hot_b, hot_a = b_.take(GT, P, dt=BF16), b_.take(3, GT, HALF, dt=BF16)
    ez = [(z_hi, z_lo), (at(O_NORM, T, dt=F32R), at(O_NORM + T, T, dt=F32R))]

    s_x = sem("x_loaded")
    s_par = sem("params_loaded")
    s_con = sem("constants_loaded")
    s_small = sem("gate_weights_loaded")
    s_cmp = sem("compression_loaded")
    s_keys = sem("sub_keys_loaded")
    keys_zeroed = sem("sub_keys_zeroed")
    ring_full = [sem(f"ring_full{r}") for r in range(RING)]
    chunk_done = sem("chunk_multiplied")
    s_ones = sem("ones_written")
    x_part = sem("x_part_updated")
    sq_part = sem("square_ready")
    sum_ready = sem("square_sum_ready")
    recip_ready = sem("recip_ready")
    rstd_ready = sem("rstd_ready")
    h_tile = sem("h_tile_ready")
    h_part = sem("h_pair_split")
    hi_part = sem("h_pair_hi")
    x_normed = sem("x_normed")
    hi_done = sem("chunk_hi_ready")
    lo_done = [sem(f"chunk_lo_ready{r}") for r in range(RING)]
    z_full = sem("z_full_ready")
    tile_copied = sem("tile_copied")
    conv_g_done = sem("conv_g_done")
    conv_u_done = sem("conv_u_done")
    c_copied = sem("c_copied")
    silu_done = sem("silu_done")
    z_ready = sem("z_ready")
    rot_ready = sem("rotated_ready")
    rope_done = sem("rope_done")
    dve_c, act_c, pool_c, pe_c = sem("dve_chain"), sem("act_chain"), sem("pool_chain"), sem("pe_chain")
    q_staged = sem("q_staged")
    s_ready = sem("scores_ready")
    s_read = sem("scores_read")
    max_ready = sem("max_ready")
    soft_ready = sem("softplus_ready")
    logit_ready = sem("log_weight_ready")
    e_ready = sem("weights_ready")
    et_ready = sem("weights_transposed")
    et_copied = sem("weights_transposed_copied")
    pv_ready = sem("pv_ready")
    o_read = sem("o_read")
    ot_ready = sem("o_transposed")
    ot_copied = sem("o_transposed_hi")
    ot_split = sem("o_transposed_split")
    gate_ready, gate_copied = sem("gate_ready"), sem("gate_copied")
    cmp_dve_s, cmp_pe_s, cmp_act_s = sem("cmp_vector_stage"), sem("cmp_tensor_stage"), sem("cmp_scalar_stage")
    hg_dve_s, hg_pe_s, hg_act_s = sem("hgrn_vector_stage"), sem("hgrn_tensor_stage"), sem("hgrn_scalar_stage")
    lv_widened, lv_exp, r_zeroed = sem("level_sums_widened"), sem("level_decays_ready"), sem("sums_behind_zeroed")
    lv_ready, lv_scored = sem("level_operands_ready"), sem("level_scores_ready")
    lv_values, lv_masked, lv_turned = sem("level_values_gathered"), sem("level_scores_masked"), sem("level_values_transposed")
    lv_copied, lv_added = sem("level_values_copied"), sem("level_added")
    sg_ready, branch_taken = sem("merge_gate_ready"), sem("branch_taken")
    tk_pe, tk_act, tk_dve = sem("topk_tensor_stage"), sem("topk_scalar_stage"), sem("topk_vector_stage")
    hot_ready, gm_done, gm_taken = sem("one_hots_ready"), sem("gate_map_ready"), sem("gate_map_taken")
    gelu_done, ez_hi = sem("gelu_done"), sem("gated_expert_hi")
    s_y = sem("y_stored")

    NCH = CH["end"]

    ZB = {"sc": 0, "ffn0": KD, "ffn1": KD + NF, "merge": KD + 2 * NF, "peer": 2 * KD + 2 * NF}
    HB = {"moba": 0, "sb": 16, "nsa0w": 24, "nsa0s": 28, "nsa1w": 32, "nsa1s": 36, "end": 40}
    MB = {b: b - 8 * (b > HB["sb"]) for b in HB.values()}
    TC = {"qkv": 0, "p_split": 24, "p_tok": 40, "p_feat": 46, "pq": 62}

    def bank(par, sub):
        return ps[:, 4 + 2 * par + sub // 2, (sub % 2) * T:(sub % 2) * T + T]

    def stream_all(sp):
        def one(st):
            r = st.mod(RING)
            if st.s >= RING:
                sp.wait_ge(lo_done[r], lo_count(st, 1, 0) - 2)
            sp.dma_start(raw[:, r, :], stream[st.lin(1), :, :]).then_inc(ring_full[r], 16)

        steps(sp, None, 0, NCH, RING, one, first=RING)

    def split_hi(act, st, a, b):
        if st.i is None and a * st.s + b >= NCH:
            return
        r = st.mod(RING, a, b)
        v = 16 * ((a * st.s + b) // RING + 1)
        act.wait_ge(ring_full[r], v if st.i is None else st.i * (16 * (a * st.stride // RING)) + v)
        nc.scalar.activation(w_hi[:, r, :], raw[:, r, :], ACT.Copy).then_inc(hi_done, 1)

    def lo_count(st, a, b):
        v = 2 * ((a * st.s + b) // RING + 1)
        return v if st.i is None else st.i * (2 * (a * st.stride // RING)) + v

    def split_lo(eng, ops, st, a, b):
        if st.i is None and a * st.s + b >= NCH:
            return
        r = st.mod(RING, a, b)
        cols = slice(CUT, D) if ops is nc.gpsimd else slice(0, CUT)
        eng.wait_ge(hi_done, st.lin(a, b + 1))
        ops.tensor_tensor(w_lo[:, r, cols], raw[:, r, cols], w_hi[:, r, cols].bitcast(F32), ALU.subtract)\
            .then_inc(lo_done[r], 1)

    def walk_act(act, st, a, b):
        act.wait_ge(chunk_done, st.lin(a, b + 1))
        split_hi(act, st, a, b + RING)

    def walk_dve(dve, st, a, b):
        split_lo(dve, nc.vector, st, a, b + RING)

    def range_act(act, lo, hi):
        steps(act, None, lo, hi, RING, lambda st: walk_act(act, st, 1, 0), first=lo + 1)

    def range_dve(dve, lo, hi):
        steps(dve, None, lo, hi, RING, lambda st: walk_dve(dve, st, 1, 0))

    def range_pool(pool, lo, hi):
        steps(pool, None, lo, hi, RING, lambda st: split_lo(pool, nc.gpsimd, st, 1, 0))

    def arrived(pe, st, a, b):
        r = st.mod(RING, a, b)
        pe.wait_ge(lo_done[r], lo_count(st, a, b))
        return r

    def exact(out, lhs, rhs, start, stop, **kw):
        nc.tensor.matmul(out, lhs[0], rhs[0], start=start, stop=False, **kw)
        nc.tensor.matmul(out, lhs[0], rhs[1], start=False, stop=False, **kw)
        return nc.tensor.matmul(out, lhs[1], rhs[0], start=False, stop=stop, **kw)

    def wt(r, k):
        return w_hi[:, r, k * P:k * P + P], w_lo[:, r, k * P:k * P + P]

    def up(pe, slot, out, k0=0, nk=KD, rhs=(h_hi, h_lo), r0=0, inc=True, hwait=None):
        for k in range(nk):
            if hwait is not None and k % 2 == 0:
                pe.wait_ge(h_part, hwait + k // 2 + 1)
            ins = exact(out, wt(slot, k0 + k), (rhs[0][:, r0 + k, :], rhs[1][:, r0 + k, :]), k == 0, k == nk - 1)
        if inc:
            ins.then_inc(chunk_done, 1)

    def down(pe, slot, src, first, final):
        for o in range(KD):
            ins = exact(acc[:, o // 2, (o % 2) * T:(o % 2) * T + T], wt(slot, o), src, first and o % 2 == 0,
                        final, skip_group_check=True)
        ins.then_inc(chunk_done, 1)

    def up_at(name, per, j, u):
        return per, CH[name] + u - (1 if j > 0 else 0)

    def down_at(name, per, n, j):
        return per, CH[name] + (per - 2 if j < n else -1)

    def norm_pe(pe, parts):
        for k in range(4):
            pe.wait_ge(sq_part, parts + k + 1)
            for j in (2 * k, 2 * k + 1):
                ins = nc.tensor.matmul(ps[:, 7, 0:T], ones[:, 0:P], sq[:, j, :], start=(j == 0), stop=(j == 7))
        ins.then_inc(sum_ready, 1)

    def gated_pe(pe, name, n, ups, body, free, free_base, hb):
        def one(st):
            if st.s < n:
                if st.s >= 2:
                    pe.wait_ge(free, st.lin(1, free_base - 1))
                for u in range(ups):
                    up(pe, arrived(pe, st, *up_at(name, ups + 1, st.s, u)), bank(st.mod(2), u),
                       hwait=hb if st.s == 0 and u == 0 else None)
            if st.s >= 1:
                pe.wait_ge(z_ready, st.lin(1, ZB[name]))
                r = arrived(pe, st, *down_at(name, ups + 1, n, st.s))
                down(pe, r, (z_hi, z_lo), st.s == 1, st.s == n)

        steps(pe, None, 0, n, body, one, first=2)
        one(Step(n))

    def residual_dve(dve, dc):
        for k in range(4):
            nc.vector.tensor_tensor(x[:, 2 * k:2 * k + 2, :], x[:, 2 * k:2 * k + 2, :],
                                    acc[:, k, :].rearrange("p (a t) -> p a t", a=2), ALU.add).then_inc(x_part, 1)

    def norm_act(act, n, source, base, hb=None):
        for k in range(4):
            act.wait_ge(source, base + (k + 1 if source is x_part else 0))
            nc.scalar.activation(sq[:, 2 * k:2 * k + 2, :], x[:, 2 * k:2 * k + 2, :], ACT.Square).then_inc(sq_part, 1)
        act.wait_ge(recip_ready, n + 1)
        nc.scalar.activation(rstd[:, :], norm_t[:, :], ACT.Sqrt).then_inc(rstd_ready, 1)
        if hb is not None:
            for k in range(4):
                act.wait_ge(h_tile, 2 * (hb + k + 1))
                nc.scalar.activation(h_hi[:, 2 * k:2 * k + 2, :], h_f[:, 2 * k:2 * k + 2, :], ACT.Copy)\
                    .then_inc(hi_part, 1)

    def norm_dve(dve, dc, n, weight, hb=None):
        dve.wait_ge(sum_ready, n + 1)
        dc.link(nc.vector.tensor_scalar(norm_t[:, :], ps[:, 7, 0:T], 1.0 / D, EPS, ALU.mult, ALU.add))
        nc.vector.reciprocal(norm_t[:, :], norm_t[:, :]).then_inc(recip_ready, 1)
        dve.wait_ge(rstd_ready, n + 1)
        dst = x if hb is None else h_f
        if hb:
            dve.wait_ge(h_part, hb)
        for k in range(KD):
            ins = nc.vector.scalar_tensor_tensor(dst[:, k, :], x[:, k, :], par_(weight, k), rstd[:, :],
                                                 ALU.mult, ALU.mult)
            if hb is not None:
                ins.then_inc(h_tile, 1)
        if hb is None:
            ins.then_inc(x_normed, 1)
            dve.wait_ge(x_normed, 1 if n < 7 else 2)
            return
        for k in range(4):
            dve.wait_ge(hi_part, hb + k + 1)
            nc.vector.tensor_tensor(h_lo[:, 2 * k:2 * k + 2, :], h_f[:, 2 * k:2 * k + 2, :],
                                    h_hi[:, 2 * k:2 * k + 2, :].bitcast(F32), ALU.subtract).then_inc(h_part, 1)
        dve.wait_ge(h_part, hb + 4)

    def split_z(dve, dc, st, name, per, n):
        dve.wait_ge(z_full, st.lin(1, ZB[name] + 1))
        if st.s >= 1:
            a, b = down_at(name, per, n, st.s)
            dve.wait_ge(chunk_done, st.lin(a, b + 1))
        dc.link(nc.vector.tensor_copy(z_hi, z_f))
        nc.vector.tensor_tensor(z_lo, z_f, z_hi.bitcast(F32), ALU.subtract).then_inc(z_ready, 1)
        if st.s >= 1:
            walk_dve(dve, st, a, b)

    def last_down_dve(dve, name, per, n):
        dve.wait_ge(chunk_done, CH[name] + per * n)
        walk_dve(dve, Step(n), *down_at(name, per, n, n))

    def conv(dve, dc, dst, src, wname, tap0):
        yield nc.vector.tensor_scalar(dst, src, par_(wname, tap0 + 2), None, ALU.mult)
        yield nc.vector.scalar_tensor_tensor(dst[:, 1:T], src[:, 0:T - 1], par_(wname, tap0 + 1), dst[:, 1:T],
                                             ALU.mult, ALU.add)
        yield nc.vector.scalar_tensor_tensor(dst[:, 2:T], src[:, 0:T - 2], par_(wname, tap0), dst[:, 2:T],
                                             ALU.mult, ALU.add)

    def ffn_dve(dve, dc, name, wname, sems0):
        n = NF

        def one(st):
            for u in range(2):
                a, b = up_at(name, 3, st.s, u)
                walk_dve(dve, st, a, b)
            dve.wait_ge(chunk_done, st.lin(a, b + 1))
            if st.s >= 1:
                dve.wait_ge(z_ready, st.lin(1, ZB[name]))
            par = st.mod(2)
            cg = conv(dve, dc, conv_g, bank(par, 0), wname, st.lin(3, 0))
            cu = conv(dve, dc, conv_u, bank(par, 1), wname, st.lin(3, NF * 3))
            g1, u1 = dc.mark(next(cg)), dc.mark(next(cu))
            dc.need(g1)
            g2 = dc.mark(next(cg))
            dc.need(u1)
            u2 = dc.mark(next(cu))
            dc.need(g2)
            next(cg).then_inc(conv_g_done, 1)
            dc.need(u2)
            next(cu).then_inc(conv_u_done, 1)
            dve.wait_ge(conv_u_done, st.lin(1, sems0 + 1))
            dve.wait_ge(silu_done, st.lin(1, sems0 + 1))
            nc.vector.tensor_tensor(z_f, silu_o, conv_u, ALU.mult).then_inc(z_full, 1)
            split_z(dve, dc, st, name, 3, n)

        steps(dve, dc, 0, n, 2, one, first=2, per=5)
        last_down_dve(dve, name, 3, n)

    def ffn_act(act, name, sems0):
        def one(st):
            for u in range(2):
                walk_act(act, st, *up_at(name, 3, st.s, u))
            act.wait_ge(conv_g_done, st.lin(1, sems0 + 1))
            nc.scalar.activation(silu_o, conv_g, ACT.Silu).then_inc(silu_done, 1)
            if st.s >= 1:
                walk_act(act, st, *down_at(name, 3, NF, st.s))

        steps(act, None, 0, NF, 2, one, first=2)
        walk_act(act, Step(NF), *down_at(name, 3, NF, NF))

    def sc_dve(dve, dc):
        def one(st):
            par = st.mod(2)
            for u in range(3):
                a, b = up_at("sc", 4, st.s, u)
                walk_dve(dve, st, a, b)
            dve.wait_ge(chunk_done, st.lin(a, b + 1))
            dve.wait_ge(c_copied, st.lin(1, 1))
            if st.s >= 1:
                dve.wait_ge(z_ready, st.lin(1))
            dc.link(nc.vector.tensor_tensor(conv_u, silu_o, bank(par, 2), ALU.mult))
            for ins in conv(dve, dc, conv_g, conv_u, "sconv", st.lin(3)):
                dc.link(ins)
            nc.vector.tensor_tensor(z_f, conv_g, bank(par, 0), ALU.mult).then_inc(z_full, 1)
            split_z(dve, dc, st, "sc", 4, KD)

        steps(dve, dc, 0, KD, 6, one)
        last_down_dve(dve, "sc", 4, KD)

    def sc_act(act):
        def one(st):
            for u in range(2):
                walk_act(act, st, *up_at("sc", 4, st.s, u))
            if st.s >= 1:
                act.wait_ge(z_ready, st.lin(1))
            nc.scalar.activation(silu_o, bank(st.mod(2), 1), ACT.Copy).then_inc(c_copied, 1)
            walk_act(act, st, *up_at("sc", 4, st.s, 2))
            if st.s >= 1:
                walk_act(act, st, *down_at("sc", 4, KD, st.s))

        steps(act, None, 0, KD, 6, one)
        walk_act(act, Step(KD), *down_at("sc", 4, KD, KD))

    def project_pe(pe, name, n, tokens_out=False, skip=0, hb=None):
        def one(st):
            g = TC[name]
            if g + st.s >= 2:
                pe.wait_ge(tile_copied, st.lin(1, g - 1))
            r = arrived(pe, st, 1, CH[name])
            par = st.mod(2, 1, g)
            if not tokens_out:
                up(pe, r, bank(par, 0), hwait=hb if st.s == 0 else None)
                return
            for c in range(2):
                for k in range(KD):
                    hk = (h_hi[:, k, c * P:c * P + P], h_lo[:, k, c * P:c * P + P])
                    ins = exact(ps[:, 4 + 2 * par, c * P:c * P + P], hk, wt(r, k), k == 0, k == KD - 1)
            ins.then_inc(chunk_done, 1)

        steps(pe, None, skip, skip + n, 6, one, first=1 if hb is not None else 0)

    def copy_heads(act, ac, st, g, dst):
        src = bank(st.mod(2, 1, g), 0)
        nc.scalar.activation(dst[:, st.lin(2), :], src[0:HD, :], ACT.Copy)
        return nc.scalar.activation(dst[:, st.lin(2, 1), :], src[HD:P, :], ACT.Copy)

    def copy_tokens(act, ac, st, g, dst, skip):
        src = bank(st.mod(2, 1, g), 0).rearrange("p (c f) -> p c f", c=2)
        return nc.scalar.activation(dst[:, :, bass.ds(st.lin(P, -P * skip), P)], src, ACT.Copy)

    def copy_feat(act, ac, st, g, dst):
        return nc.scalar.activation(dst[:, st.lin(1), :], bank(st.mod(2, 1, g), 0), ACT.Copy)

    def project_act(act, ac, name, n, copy, *args, skip=0):
        def one(st):
            act.wait_ge(chunk_done, st.lin(1, CH[name] + 1))
            copy(act, ac, st, TC[name], *args).then_inc(tile_copied, 1)
            split_hi(act, st, 1, CH[name] + RING)

        steps(act, None, skip, skip + n, 6, one)

    def qk_pe(pe):
        def swap(st):
            pe.wait_ge(tile_copied, st.lin(1))
            if st.s >= 3:
                pe.wait_ge(rope_done, st.lin(1, -2))
            nc.tensor.matmul(bank(st.mod(2, 1, 1), 2), con_("swap"), copied[:, st.mod(2, 1, 1), :],
                             start=True, stop=True).then_inc(rot_ready, 1)

        def one(st):
            if st.s >= 2:
                pe.wait_ge(tile_copied, st.lin(1, -1))
            up(pe, arrived(pe, st, 1, CH["qkv"]), bank(st.mod(2), 0), hwait=8 if st.s == 0 else None)
            if st.s >= 1:
                swap(st)

        steps(pe, None, 0, 16, 6, one, first=4)
        swap(Step(16))

    def qk_act(act):
        def one(st):
            act.wait_ge(chunk_done, st.lin(1, CH["qkv"] + 1))
            if st.s >= 2:
                act.wait_ge(rope_done, st.lin(1, -1))
            nc.scalar.activation(copied[:, st.mod(2), :], bank(st.mod(2), 0), ACT.Copy).then_inc(tile_copied, 1)
            split_hi(act, st, 1, CH["qkv"] + RING)

        steps(act, None, 0, 16, 6, one, first=4)

    def qk_dve(dve, dc):
        def one(st):
            walk_dve(dve, st, 1, CH["qkv"])
            dve.wait_ge(rot_ready, st.lin(1, 1))
            if st.s >= 1:
                dve.wait_ge(rope_done, st.lin(1))
            dc.mark(nc.vector.tensor_tensor(rope_a, copied[:, st.mod(2), :], con_("cos"), ALU.mult))
            dc.link(nc.vector.tensor_tensor(rope_b, bank(st.mod(2), 2), con_("sin"), ALU.mult))
            nc.vector.tensor_tensor(heads[:, st.lin(2), :], rope_a[0:HD], rope_b[0:HD], ALU.add)
            nc.vector.tensor_tensor(heads[:, st.lin(2, 1), :], rope_a[HD:P], rope_b[HD:P],
                                    ALU.add).then_inc(rope_done, 1)

        steps(dve, dc, 0, 16, 6, one, first=4, per=2)

    def heads_pool(pool, base, n, q):
        def one(st):
            if base + st.s >= 2:
                pool.wait_ge(s_ready, st.lin(1, base - 1))
            nc.gpsimd.tensor_copy(a_q[:, st.mod(2), :], q(st)).then_inc(q_staged, 1)

        steps(pool, None, 0, n, 2, one, first=2)

    def heads_pe(pe, base, n, k, v, lag):
        def scores(st):
            pe.wait_ge(q_staged, st.lin(1, base + 1))
            if base + st.s >= 2:
                pe.wait_ge(s_read, st.lin(1, base - 1))
            p = st.mod(2)
            nc.tensor.matmul(ps[:, 4 + p, 0:P], a_q[:, p, 0:P], k(st)[:, 0:P], start=True, stop=True)
            nc.tensor.matmul(ps[:, 4 + p, P:SC3], a_q[:, p, P:T], k(st), start=True, stop=True).then_inc(s_ready, 1)

        def turn(st):
            pe.wait_ge(e_ready, st.lin(1, base + 1))
            if base + st.s >= 2:
                pe.wait_ge(et_copied, st.lin(1, base - 1))
            p = st.mod(2)
            for b in range(3):
                ins = nc.tensor.transpose(ps[:, 6 + p, b * P:b * P + P], a_e[:, p, b * P:b * P + P], ident)
            ins.then_inc(et_ready, 1)

        def values(st):
            pe.wait_ge(et_copied, st.lin(1, base + 1))
            if base + st.s >= 2:
                pe.wait_ge(o_read, st.lin(1, base - 1))
            p = st.mod(2)
            nc.tensor.matmul(ps[:, p, 0:HD], a_t[:, p, 0:P], v(st, 0), start=True, stop=True)
            nc.tensor.matmul(ps[:, p, HD:2 * HD], a_t[:, p, P:2 * P], v(st, 0), start=True, stop=False)
            nc.tensor.matmul(ps[:, p, HD:2 * HD], a_t[:, p, 2 * P:SC3], v(st, 1), start=False,
                             stop=True).then_inc(pv_ready, 1)

        def one(st):
            if st.s < n:
                scores(st)
            if 0 <= st.s - lag < n:
                turn(Step(st.s - lag, st.stride, st.i))
            if st.s - lag - 1 >= 0:
                values(Step(st.s - lag - 1, st.stride, st.i))

        steps(pe, None, 0, n, 2, one, first=lag + 1)
        for j in range(n, n + lag + 1):
            one(Step(j))

    def copy_weights(act, base, st):
        act.wait_ge(et_ready, st.lin(1, base + 1))
        if base + st.s >= 2:
            act.wait_ge(pv_ready, st.lin(1, base - 1))
        nc.scalar.activation(a_t[:, st.mod(2), :], ps[:, 6 + st.mod(2), 0:SC3], ACT.Copy).then_inc(et_copied, 1)

    def soft_act(act, base, n):
        def one(st):
            p = st.mod(2)
            if st.s < n:
                act.wait_ge(max_ready, st.lin(1, MB[base] + 1))
                if base + st.s >= 2:
                    act.wait_ge(et_ready, st.lin(1, base - 1))
                for c, (lo, hi) in enumerate(((0, P), (P, SC3))):
                    ins = nc.scalar.activation(a_e[:, p, lo:hi], a_s[:, p, lo:hi], ACT.Exp,
                                               bias=a_max[:, p, c:c + 1],
                                               accum_out=a_sum[:, st.lin(1, base), c:c + 1])
                ins.then_inc(e_ready, 1)
            if st.s >= 1:
                copy_weights(act, base, Step(st.s - 1, st.stride, st.i))

        steps(act, None, 0, n, 2, one, first=2)
        one(Step(n))

    def soft_dve(dve, dc, base, n, bias, out, marks):
        def score(st):
            p = st.mod(2)
            dve.wait_ge(s_ready, st.lin(1, base + 1))
            if base + st.s >= 2:
                dve.wait_ge(e_ready, st.lin(1, base - 1))
            nc.vector.scalar_tensor_tensor(a_s[:, p, :], ps[:, 4 + p, 0:SC3], SCALE, bias(st), ALU.mult, ALU.add).then_inc(s_read, 1)
            dve.wait_ge(s_read, st.lin(1, base + 1))
            nc.vector.tensor_reduce(a_max[:, p, 0:1], a_s[:, p, 0:P], AX.X, ALU.max, negate=True)
            nc.vector.tensor_reduce(a_max[:, p, 1:2], a_s[:, p, P:SC3], AX.X, ALU.max,
                                    negate=True).then_inc(max_ready, 1)

        def rows(st):
            dve.wait_ge(pv_ready, st.lin(1, base + 1))
            if base + st.s >= 1:
                dve.wait_ge(o_read, st.lin(1, base))
            dc.link(nc.vector.reciprocal(a_r[:, 0, :], a_sum[:, st.lin(1, base), :]))
            out(st, ps[:, st.mod(2), 0:2 * HD].rearrange("p (c d) -> p c d", c=2)).then_inc(o_read, 1)

        def one(st):
            if st.s < n:
                score(st)
            if st.s >= 2:
                rows(Step(st.s - 2, st.stride, st.i))

        steps(dve, dc, 0, n, 2, one, first=2, per=marks)
        one(Step(n))
        one(Step(n + 1))

    def stick_act(act, ac, base, n):
        def soft(st):
            p = st.mod(2)
            act.wait_ge(s_read, st.lin(1, base + 1))
            if st.s >= 2:
                act.wait_ge(e_ready, st.lin(1, base - 1))
            ac.link(nc.scalar.activation(a_l[:, p, :], a_s[:, p, :], ACT.Abs))
            ac.link(nc.scalar.activation(a_l[:, p, :], a_l[:, p, :], ACT.Exp, scale=-1.0))
            nc.scalar.activation(a_l[:, p, :], a_l[:, p, :], ACT.Ln, bias=1.0).then_inc(soft_ready, 1)

        def weight(st):
            p = st.mod(2)
            act.wait_ge(logit_ready, st.lin(1, 1))
            if base + st.s >= 2:
                act.wait_ge(et_ready, st.lin(1, base - 1))
            nc.scalar.activation(a_e[:, p, :], a_l[:, p, :], ACT.Exp).then_inc(e_ready, 1)

        def one(st):
            if st.s < n:
                soft(st)
            if 0 <= st.s - 1 < n:
                weight(Step(st.s - 1, st.stride, st.i))
            if st.s - 2 >= 0:
                copy_weights(act, base, Step(st.s - 2, st.stride, st.i))

        steps(act, ac, 0, n, 2, one, first=2, per=2)
        one(Step(n))
        one(Step(n + 1))

    def stick_dve(dve, dc, base, n, out):
        def mask(st):
            p = st.mod(2)
            dve.wait_ge(s_ready, st.lin(1, base + 1))
            if st.s >= 2:
                dve.wait_ge(logit_ready, st.lin(1, -1))
            nc.vector.scalar_tensor_tensor(a_s[:, p, :], ps[:, 4 + p, 0:SC3], SCALE, con_("strict"), ALU.mult, ALU.add).then_inc(s_read, 1)

        def logit(st):
            p = st.mod(2)
            dve.wait_ge(soft_ready, st.lin(1, 1))
            if st.s >= 1:
                dve.wait_ge(logit_ready, st.lin(1))
            dc.link(nc.vector.scalar_tensor_tensor(a_l[:, p, :], a_s[:, p, :], 0.0, a_l[:, p, :], ALU.max, ALU.add))
            for lo, hi in ((0, P), (P, SC3)):
                rev = slice(hi - 1, lo - 1 if lo else None, -1)
                dc.mark(nc.vector.tensor_tensor_scan(a_c[:, rev], ones[:, 0:hi - lo], a_l[:, p, rev], 0.0,
                                                     ALU.mult, ALU.add))
            dc.need()
            nc.vector.tensor_tensor(a_l[:, p, :], a_s[:, p, :], a_c, ALU.subtract).then_inc(logit_ready, 1)

        def rows(st):
            dve.wait_ge(pv_ready, st.lin(1, base + 1))
            out(st, ps[:, st.mod(2), 0:2 * HD].rearrange("p (c d) -> p c d", c=2)).then_inc(o_read, 1)

        def one(st):
            if st.s < n:
                mask(st)
            if 0 <= st.s - 1 < n:
                logit(Step(st.s - 1, st.stride, st.i))
            if st.s - 3 >= 0:
                rows(Step(st.s - 3, st.stride, st.i))

        steps(dve, dc, 0, n, 2, one, first=4, per=3)
        for j in range(n, n + 3):
            one(Step(j))

    def head_cols(st, o=0):
        return otok[:, :, bass.ds(st.lin(HD, o), HD)]

    def rows_soft(st, o):
        dst = head_cols(st)
        nc.vector.tensor_scalar(dst[:, 0, :], o[:, 0, :], a_r[:, 0, 0:1], None, ALU.mult)
        return nc.vector.tensor_scalar(dst[:, 1, :], o[:, 1, :], a_r[:, 0, 1:2], None, ALU.mult)

    def turn_out_pe(pe, base):
        for g in range(4):
            for b in range(4):
                j, c = 2 * g + b // 2, b % 2
                ins = nc.tensor.transpose(ps[:, 4 + g, b * P:b * P + P], otok[:, c, j * P:j * P + P], ident)
            ins.then_inc(ot_ready, 1)

    def turn_out_act(act, base):
        for g in range(4):
            act.wait_ge(ot_ready, base + g + 1)
            nc.scalar.activation(oT_hi[:, 2 * g:2 * g + 2, :], ps[:, 4 + g, :].rearrange("p (a t) -> p a t", a=2),
                                 ACT.Copy).then_inc(ot_copied, 1)

    def turn_out_dve(dve, base):
        for g in range(4):
            dve.wait_ge(ot_copied, base + g + 1)
            nc.vector.tensor_tensor(oT_lo[:, 2 * g:2 * g + 2, :], ps[:, 4 + g, :].rearrange("p (a t) -> p a t", a=2),
                                    oT_hi[:, 2 * g:2 * g + 2, :].bitcast(F32), ALU.subtract).then_inc(ot_split, 1)

    def wo_pe(pe):
        for j in range(KD):
            pe.wait_ge(ot_split, j // 2 + 1)
            down(pe, arrived(pe, Step(j), 1, CH["wo"]), (oT_hi[:, j, :], oT_lo[:, j, :]), j == 0, j == KD - 1)

    def gates_pe(pe):
        pe.wait_ge(s_small, 16 * 1)
        pe.wait_ge(h_tile, 2 * 20)
        for c in range(2):
            for k in range(KD):
                ins = nc.tensor.matmul(ps[:, 0, c * 24:c * 24 + 24], h_f[:, k, c * P:c * P + P], wg_s[:, k, :],
                                       start=(k == 0), stop=(k == KD - 1))
        ins.then_inc(gate_ready, 1)

    def gates_act(act):
        act.wait_ge(gate_ready, 1)
        nc.scalar.activation(gates, ps[:, 0, 0:48].rearrange("p (c g) -> p c g", c=2), ACT.Sigmoid)\
            .then_inc(gate_copied, 1)

    def cmp_dve(dve, dc):
        dve.wait_ge(s_cmp, 16 * 4)
        dve.wait_ge(tile_copied, TC["p_tok"])
        dc.mark(nc.vector.memset(blk_k, 0.0))
        dc.link(nc.vector.memset(blk_v, 0.0))
        for dst, hd in ((blk_k, 24), (blk_v, 26)):
            src = heads[:, hd:hd + 2, :].rearrange("p g (c l) -> p l g c", l=16)
            for half in range(2):
                ins = nc.vector.tensor_tensor(
                    dst[:, 16 * half:16 * half + 16, :, 0:15], src[:, :, :, half:half + 15],
                    pe_s[:, 16 * half:16 * half + 16].unsqueeze(2).unsqueeze(3).broadcast_to([HD, 16, 2, 15]), ALU.add)
        ins.then_inc(cmp_dve_s, 1)
        dve.wait_ge(cmp_pe_s, 2)
        nc.vector.scalar_tensor_tensor(ce, ps[:, 4, 0:256], SCALE, con_("cmpbias"), ALU.mult, ALU.add)\
            .then_inc(cmp_dve_s, 1)
        dve.wait_ge(cmp_dve_s, 2)
        ce3 = ce.rearrange("p (r c) -> p r c", c=CMP)
        dc.link(nc.vector.tensor_reduce(cm, ce3, AX.X, ALU.max))
        nc.vector.tensor_tensor(ce3, ce3, cm.unsqueeze(2).broadcast_to([P, 16, CMP]), ALU.subtract)\
            .then_inc(cmp_dve_s, 1)
        dve.wait_ge(cmp_act_s, 2)
        dve.wait_ge(gate_copied, 1)
        dc.link(nc.vector.tensor_reduce(cm, ce3, AX.X, ALU.add))
        dc.link(nc.vector.reciprocal(cm, cm))
        g = gates.rearrange("p c (h b) -> p h c b", b=3)[:, :, :, 0]
        cm2 = cm.rearrange("p (h c) -> p h c", c=2)
        dc.link(nc.vector.tensor_tensor(cm2, cm2, g, ALU.mult))
        dc.link(nc.vector.tensor_tensor(cm2, cm2, con_("rowok").unsqueeze(1).broadcast_to([P, 8, 2]), ALU.mult))
        nc.vector.tensor_tensor(ce3, ce3, cm.unsqueeze(2).broadcast_to([P, 16, CMP]), ALU.mult)\
            .then_inc(cmp_dve_s, 1)
        dve.wait_ge(cmp_pe_s, 4)
        for b in range(2):
            src = ps[:, 2 + b, :].rearrange("p (h c d) -> p h c d", h=4, c=2)
            for c in range(2):
                ins = nc.vector.tensor_copy(
                    otok[:, c, 512 + b * 256:512 + b * 256 + 256].rearrange("p (h d) -> p h d", h=4), src[:, :, c, :])
        ins.then_inc(cmp_dve_s, 1)
        dve.wait_ge(cmp_dve_s, 5)

    def cmp_pe(pe):
        pe.wait_ge(s_cmp, 16 * 4)
        pe.wait_ge(cmp_dve_s, 1)
        pe.wait_ge(gate_copied, 1)
        for l in range(32):
            nc.tensor.matmul(ps[0:HD, 0, 0:32], wk_s[:, l, :], blk_k[:, l, :, :].rearrange("p g c -> p (g c)"),
                             start=(l == 0), stop=(l == 31))
        for g in range(2):
            for l in range(32):
                ins = nc.tensor.matmul(ps[0:CMP, 1, g * HD:g * HD + HD], blk_v[:, l, g, :], wv_s[:, l, :],
                                       start=(l == 0), stop=(l == 31))
        ins.then_inc(cmp_pe_s, 1)
        pe.wait_ge(cmp_act_s, 1)
        for hd in range(8):
            for c in range(2):
                r = 2 * hd + c
                ins = nc.tensor.matmul(ps[:, 4, r * CMP:r * CMP + CMP], heads[:, 16 + hd, c * P:c * P + P],
                                       kc[:, hd // 4, :], start=True, stop=True)
        ins.then_inc(cmp_pe_s, 1)
        pe.wait_ge(cmp_dve_s, 4)
        for r in range(16):
            ins = nc.tensor.transpose(ps[0:CMP, 4 + r // 4, (r % 4) * P:(r % 4) * P + P],
                                      ce[:, r * CMP:r * CMP + CMP], ident)
        ins.then_inc(cmp_pe_s, 1)
        pe.wait_ge(cmp_act_s, 3)
        for r in range(16):
            ins = nc.tensor.matmul(ps[:, 2 + r // 8, (r % 8) * HD:(r % 8) * HD + HD], ceT[:, r, :], vc[:, r // 8, :],
                                   start=True, stop=True)
        ins.then_inc(cmp_pe_s, 1)

    def cmp_act(act):
        act.wait_ge(cmp_pe_s, 1)
        nc.scalar.activation(kc.rearrange("p g c -> p (g c)"), ps[0:HD, 0, 0:32], ACT.Copy)
        nc.scalar.activation(vc.rearrange("p g c -> p (g c)"), ps[0:CMP, 1, 0:P], ACT.Copy).then_inc(cmp_act_s, 1)
        act.wait_ge(cmp_dve_s, 3)
        nc.scalar.activation(ce, ce, ACT.Exp).then_inc(cmp_act_s, 1)
        act.wait_ge(cmp_pe_s, 3)
        nc.scalar.activation(ceT.rearrange("p r t -> p (r t)"), ps[0:CMP, 4:8, :].rearrange("p b t -> p (b t)"),
                             ACT.Copy).then_inc(cmp_act_s, 1)

    def rows_stick(st, o):
        return nc.vector.tensor_copy(head_cols(st), o)

    def rows_nsa(branch, g0, dc):
        gh = gates.rearrange("p c (h b) -> p b h c", b=3)[:, branch, :, :]

        def out(st, o):
            dst = otok[:, :, bass.ds(st.lin(HD, 512 + g0 * HD), HD)]
            dc.link(nc.vector.tensor_tensor(a_r[:, 0, :], a_r[:, 0, :], gh[:, st.lin(1, g0), :], ALU.mult))
            nc.vector.scalar_tensor_tensor(dst[:, 0, :], o[:, 0, :], a_r[:, 0, 0:1], dst[:, 0, :], ALU.mult, ALU.add)
            return nc.vector.scalar_tensor_tensor(dst[:, 1, :], o[:, 1, :], a_r[:, 0, 1:2], dst[:, 1, :],
                                                  ALU.mult, ALU.add)
        return out

    NSA = [("nsa0w", 0, 2, 30, 640), ("nsa0s", 0, 1, 28, 512), ("nsa1w", 4, 2, 31, 704), ("nsa1s", 4, 1, 29, 576)]

    def halves(v, lv, a=None):
        v = v.rearrange("p a t -> p (a t)") if a is None else v[:, a, :]
        v = v.rearrange("p (m s u) -> p m s u", s=2, u=LEVELS[lv])
        return v[:, :, 0, :], v[:, :, 1, :]

    def compact(v, lv):
        return v.rearrange("p (m u) -> p m u", u=LEVELS[lv])

    o_acc = ps[:, 0:2, :].rearrange("p a t -> p (a t)").rearrange("p (a t) -> p a t", a=4)

    def hg_act(act, ac):
        act.wait_ge(tile_copied, TC["p_feat"] + 16)
        act.wait_ge(cmp_pe_s, 4)
        act.wait_ge(cmp_dve_s, 5)
        ac.link(nc.scalar.activation(h_tmp, hf, ACT.Abs))
        ac.link(nc.scalar.activation(h_tmp, h_tmp, ACT.Exp, scale=-1.0))
        nc.scalar.activation(h_tmp, h_tmp, ACT.Ln, bias=1.0).then_inc(hg_act_s, 1)
        act.wait_ge(hg_dve_s, 1)
        nc.scalar.activation(h_k, h_tmp, ACT.Exp)
        nc.scalar.activation(hq, hq, ACT.Silu)
        nc.scalar.activation(hg, hg, ACT.Silu).then_inc(hg_act_s, 1)
        for lv, L in enumerate(LEVELS):
            p = lv % 2
            if lv == 0:
                act.wait_ge(r_zeroed, 1)
            else:
                act.wait_ge(lv_widened, lv)
            if lv >= 2:
                act.wait_ge(lv_scored, lv - 1)
            nc.scalar.activation(compact(lv_q[:, p, :], lv), halves(h_c, lv)[1], ACT.Exp)
            nc.scalar.activation(compact(lv_k[:, p, :], lv), halves(h_r, lv)[0], ACT.Exp).then_inc(lv_exp, 1)
            act.wait_ge(lv_turned, lv + 1)
            if lv >= 2:
                act.wait_ge(lv_added, lv - 1)
            nc.scalar.activation(lv_i[:, p, :], ps[:, 4 + p, :], ACT.Copy).then_inc(lv_copied, 1)
        act.wait_ge(lv_added, len(LEVELS))
        nc.scalar.activation(h_tmp, o_acc, ACT.Square).then_inc(hg_act_s, 1)
        act.wait_ge(hg_dve_s, 4)
        nc.scalar.activation(h_tmp, h_tmp, ACT.Sqrt).then_inc(hg_act_s, 1)

    def hg_pool(pool):
        pool.wait_ge(o_read, HB["end"])
        nc.gpsimd.memset(h_r, 0.0).then_inc(r_zeroed, 1)
        for lv in range(len(LEVELS)):
            if lv >= 2:
                pool.wait_ge(lv_turned, lv - 1)
            nc.gpsimd.tensor_copy(compact(lv_v[:, lv % 2, :], lv), halves(hi, lv)[0]).then_inc(lv_values, 1)

    def hg_dve(dve, dc):
        dve.wait_ge(hg_act_s, 1)
        dc.link(nc.vector.scalar_tensor_tensor(h_lf, hf, 0.0, h_tmp, ALU.min, ALU.subtract))
        nc.vector.tensor_tensor(h_tmp, h_lf, hf, ALU.subtract).then_inc(hg_dve_s, 1)

        def widen(lv):
            dve.wait_ge(lv_exp, lv)
            for_c, for_r = halves(h_c, lv - 1), halves(h_r, lv - 1)
            L = LEVELS[lv - 1]
            shape = [P, 4 * P // L, L]
            dc.link(nc.vector.tensor_tensor(for_r[0], for_r[0], for_c[1][:, :, L - 1:L].broadcast_to(shape), ALU.add))
            nc.vector.tensor_tensor(for_c[1], for_c[1], for_c[0][:, :, L - 1:L].broadcast_to(shape), ALU.add)\
                .then_inc(lv_widened, 1)
            dve.wait_ge(lv_widened, lv)

        def decay(lv):
            p = lv % 2
            dve.wait_ge(lv_exp, lv + 1)
            q, k = compact(lv_q[:, p, :], lv), compact(lv_k[:, p, :], lv)
            nc.vector.tensor_tensor(q, q, halves(hq, lv)[1], ALU.mult)
            nc.vector.tensor_tensor(k, k, halves(h_k, lv)[0], ALU.mult).then_inc(lv_ready, 1)

        def mask(lv):
            p = lv % 2
            dve.wait_ge(lv_scored, lv + 1)
            if lv >= 2:
                dve.wait_ge(lv_added, lv - 1)
            src = ps[:, 2 + p, :].rearrange("p (a t) -> p a t", a=4)
            if lv < len(LEVELS) - 1:
                m = con_("pairs")[:, lv * P - P:lv * P] if lv else ident
                m = m.unsqueeze(1).broadcast_to([P, 4, P])
                ins = nc.vector.tensor_tensor(lv_a[:, p], src, m, ALU.mult)
            else:
                ins = nc.vector.tensor_copy(lv_a[:, p], src)
            ins.then_inc(lv_masked, 1)

        dve.wait_ge(hg_dve_s, 1)
        dve.wait_ge(hg_act_s, 2)
        nc.vector.tensor_tensor(h_o, hq, h_k, ALU.mult).then_inc(hg_dve_s, 1)
        dve.wait_ge(hg_pe_s, 1)
        nc.vector.tensor_tensor(h_o.rearrange("p a t -> p (a t)"), ps[:, 6:8, :].rearrange("p a t -> p (a t)"),
                                hi.rearrange("p a t -> p (a t)"), ALU.mult).then_inc(hg_dve_s, 1)
        for lv in range(len(LEVELS) + 1):
            if lv + 1 < len(LEVELS):
                widen(lv + 1)
            if lv < len(LEVELS):
                decay(lv)
            if lv >= 1:
                mask(lv - 1)
        tmp2 = h_tmp.rearrange("p a t -> p (a t)")
        dve.wait_ge(hg_pe_s, 2)
        dc.link(nc.vector.tensor_scalar(tmp2, ps[:, 6:8, :].rearrange("p a t -> p (a t)"), 1.0 / P, EPS,
                                        ALU.mult, ALU.add))
        nc.vector.reciprocal(tmp2, tmp2).then_inc(hg_dve_s, 1)
        dve.wait_ge(hg_act_s, 4)
        dc.link(nc.vector.tensor_tensor(h_o, o_acc, h_tmp, ALU.mult))
        for a in range(4):
            dc.mark(nc.vector.scalar_tensor_tensor(h_o[:, a, :], h_o[:, a, :], par_("hnorm", a), hg[:, a, :],
                                                   ALU.mult, ALU.mult))
        dc.need()
        dc.link(nc.vector.tensor_copy(oT_hi[:, 8:12, :], h_o))
        nc.vector.tensor_tensor(oT_lo[:, 8:12, :], h_o, oT_hi[:, 8:12, :].bitcast(F32), ALU.subtract)\
            .then_inc(hg_dve_s, 1)

    def hg_pe(pe):
        pe.wait_ge(o_read, HB["end"])
        pe.wait_ge(ot_split, 8)
        pe.wait_ge(hg_dve_s, 2)
        o2 = h_o.rearrange("p a t -> p (a t)")
        for b in range(2):
            ins = nc.tensor.matmul(ps[:, 6 + b, :], ones[:, 0:P], o2[:, b * 512:b * 512 + 512], start=True, stop=True)
        ins.then_inc(hg_pe_s, 1)

        def added(lv):
            p, L = lv % 2, LEVELS[lv]
            pe.wait_ge(lv_masked, lv + 1)
            pe.wait_ge(lv_copied, lv + 1)
            for a in range(4):
                ins = nc.tensor.matmul(halves(o_acc, lv, a)[1], lv_i[:, p, a * P:a * P + P],
                                       compact(lv_a[:, p, a, :], lv), start=False, stop=lv == len(LEVELS) - 1,
                                       skip_group_check=True)
            ins.then_inc(lv_added, 1)

        for lv in range(len(LEVELS)):
            p = lv % 2
            if lv >= 2:
                pe.wait_ge(lv_copied, lv - 1)
            pe.wait_ge(lv_values, lv + 1)
            for a in range(4):
                ins = nc.tensor.transpose(ps[:, 4 + p, a * P:a * P + P], lv_v[:, p, a * P:a * P + P], ident)
            ins.then_inc(lv_turned, 1)
            pe.wait_ge(lv_ready, lv + 1)
            if lv >= 2:
                pe.wait_ge(lv_masked, lv - 1)
            for a in range(4):
                ins = nc.tensor.matmul(ps[:, 2 + p, a * P:a * P + P], lv_k[:, p, a * P:a * P + P],
                                       lv_q[:, p, a * P:a * P + P], start=True, stop=True)
            ins.then_inc(lv_scored, 1)
            if lv == 0:
                pe.wait_ge(hg_dve_s, 3)
                for b in range(2):
                    nc.tensor.matmul(ps[:, b, :], ident, o2[:, b * 512:b * 512 + 512], start=True, stop=False,
                                     skip_group_check=True)
            else:
                added(lv - 1)
        added(len(LEVELS) - 1)
        pe.wait_ge(hg_act_s, 3)
        tmp2 = h_tmp.rearrange("p a t -> p (a t)")
        for b in range(2):
            ins = nc.tensor.matmul(ps[:, 6 + b, :], ones[:, 0:P], tmp2[:, b * 512:b * 512 + 512], start=True, stop=True)
        ins.then_inc(hg_pe_s, 1)

    def merge_at(j, k):
        return 6, CH["merge"] + k - (1 if j > 0 else 0)

    def merge_pe(pe):
        pe.wait_ge(hg_dve_s, 5)
        n = KD

        def one(st):
            if st.s < n:
                def gate(i, k):
                    if st.s >= 1:
                        pe.wait_ge(branch_taken, st.lin(3, i - 2))
                    up(pe, arrived(pe, st, *merge_at(st.s, k)), ps[:, 4 + i, 0:T])

                gate(0, 0)
                gate(1, 1)
                r = arrived(pe, st, *merge_at(st.s, 2))
                up(pe, r, ps[:, 4, T:2 * T], 0, 4, (oT_hi, oT_lo), 0, inc=False)
                up(pe, r, ps[:, 5, T:2 * T], 4, 4, (oT_hi, oT_lo), 4)
                gate(2, 3)
                up(pe, arrived(pe, st, *merge_at(st.s, 4)), ps[:, 6, T:2 * T], 0, 4, (oT_hi, oT_lo), 8)
            if st.s >= 1:
                pe.wait_ge(z_ready, st.lin(1, ZB["merge"]))
                down(pe, arrived(pe, st, 6, CH["merge"] + (4 if st.s < n else -1)), (z_hi, z_lo),
                     st.s == 1, st.s == n)

        steps(pe, None, 0, n, 1, one, first=2)
        one(Step(n))

    def merge_act(act):
        def one(st):
            for k in (0, 1, 2):
                walk_act(act, st, *merge_at(st.s, k))
            for i in range(3):
                if i == 2:
                    walk_act(act, st, *merge_at(st.s, 3))
                    walk_act(act, st, *merge_at(st.s, 4))
                if st.s >= 1:
                    act.wait_ge(branch_taken, st.lin(3, i - 2))
                nc.scalar.activation(sg[:, i, :], ps[:, 4 + i, 0:T], ACT.Sigmoid).then_inc(sg_ready, 1)
            if st.s >= 1:
                walk_act(act, st, *down_at("merge", 6, KD, st.s))

        steps(act, None, 0, KD, 1, one, first=2)
        walk_act(act, Step(KD), *down_at("merge", 6, KD, KD))

    def merge_dve(dve, dc):
        def one(st):
            if st.s >= 1:
                dve.wait_ge(z_ready, st.lin(1, ZB["merge"]))
            for k in (0, 1, 2):
                walk_dve(dve, st, *merge_at(st.s, k))
            for i in range(3):
                if i == 2:
                    walk_dve(dve, st, *merge_at(st.s, 3))
                    walk_dve(dve, st, *merge_at(st.s, 4))
                    dc.link(nc.vector.tensor_tensor(conv_g, conv_g, conv_u, ALU.add))
                dve.wait_ge(sg_ready, st.lin(3, i + 1))
                nc.vector.tensor_tensor(conv_u if i else conv_g, sg[:, i, :], ps[:, 4 + i, T:2 * T], ALU.mult)\
                    .then_inc(branch_taken, 1)
                dve.wait_ge(branch_taken, st.lin(3, i + 1))
            nc.vector.tensor_tensor(z_f, conv_g, conv_u, ALU.add).then_inc(z_full, 1)
            split_z(dve, dc, st, "merge", 6, KD)

        steps(dve, dc, 0, KD, 1, one, first=2, per=2)
        last_down_dve(dve, "merge", 6, KD)

    def peer_turn_pe(pe):
        pe.wait_ge(tk_dve, 2)
        for i in range(3):
            for c in range(2):
                ins = nc.tensor.transpose(ps[:, i, c * P:c * P + P], t_key[:, i, c, :], ident)
        ins.then_inc(tk_pe, 1)

    def peer_scores_pe(pe):
        pe.wait_ge(tile_copied, TC["pq"] + KD)
        pe.wait_ge(s_keys, 32)
        for c in range(2):
            for a in range(PH):
                ins = nc.tensor.matmul(ps[:, 4 * c + a // 2, (a % 2) * T:(a % 2) * T + T], t_q[:, a, c * P:c * P + P],
                                       keys_s, start=True, stop=True)
                if a % 2:
                    ins.then_inc(tk_pe, 1)

    def peer_top_act(act):
        for b in range(8):
            act.wait_ge(tk_pe, b + 1)
            nc.scalar.activation(t_s[:, 4 * b:4 * b + 4, :], ps[:, b, :].rearrange("p (r k) -> p r k", r=4),
                                 ACT.Copy).then_inc(tk_act, 1)

    def top16(dc, rows, src, best, where, us):
        for lo in range(0, rows, 8):
            rs = range(lo, min(lo + 8, rows))
            for at0 in (0, 8):
                for r in rs:
                    dc.mark(nc.vector.max(best[:, r, at0:at0 + 8], src[:, r, :]))
                    yield us
                dc.need()
                for r in rs:
                    dc.mark(nc.vector.max_index(where[:, r, at0:at0 + 8], best[:, r, at0:at0 + 8], src[:, r, :]))
                    yield us
                dc.need()
                for r in rs if at0 == 0 else ():
                    dc.mark(nc.vector.match_replace(src[:, r, :], best[:, r, 0:8], src[:, r, :], -3e38))
                    yield us
                dc.need()

    def peer_top(dve, dc):
        dve.wait_ge(tk_act, 8)
        yield from top16(dc, 32, t_s, t_b, t_i, 0.22)
        dc.link(nc.vector.tensor_copy(t_if, t_i))
        yield 0.6
        for c in range(2):
            b = t_b.rearrange("p (c a h) k -> p c a h k", c=2, h=2)[:, c]
            dc.mark(nc.vector.tensor_tensor(
                t_c[:, 8 * c:8 * c + 8, :].rearrange("p a (i j) -> p a i j", i=TOPK),
                b[:, :, 0, :].unsqueeze(3).broadcast_to([P, PH, TOPK, TOPK]),
                b[:, :, 1, :].unsqueeze(2).broadcast_to([P, PH, TOPK, TOPK]), ALU.add))
            yield 2.2
        dc.need()
        yield from top16(dc, 16, t_c, t_g, t_w, 0.36)
        dc.mark(nc.vector.tensor_scalar(t_wi, t_w, 4, None, ALU.logical_shift_right))
        dc.link(nc.vector.tensor_scalar(t_wj, t_w, 15, None, ALU.bitwise_and))
        dc.mark(nc.vector.tensor_copy(t_wf[:, 0], t_wi))
        dc.mark(nc.vector.tensor_copy(t_wf[:, 1], t_wj))
        dc.mark(nc.vector.tensor_copy(t_m, t_g[:, :, 0:1]))
        dc.need()
        nc.vector.tensor_tensor(t_g, t_g, t_m.broadcast_to([P, 16, TOPK]), ALU.subtract).then_inc(tk_dve, 1)
        yield 2.0
        for half in range(2):
            for c in range(2):
                w = t_wf[:, half, 8 * c:8 * c + 8, :].rearrange("p a k -> p (a k)")
                dc.link(nc.vector.tensor_tensor(t_1, con_("iota16").unsqueeze(1).broadcast_to([P, P, TOPK]),
                                                w.unsqueeze(2).broadcast_to([P, P, TOPK]), ALU.is_equal))
                yield 2.2
                t14 = t_1.rearrange("p (a k) i -> p a k i", a=PH)
                f = t_if.rearrange("p (c a h) k -> p c h a k", c=2, h=2)[:, c, half]
                dc.link(nc.vector.tensor_tensor(t14, t14, f.unsqueeze(2).broadcast_to([P, PH, TOPK, TOPK]), ALU.mult))
                yield 2.2
                dc.link(nc.vector.tensor_reduce(t_key[:, half, c, :], t_1, AX.X, ALU.add))
                yield 2.2
        dve.wait_ge(tk_act, 9)
        dc.link(nc.vector.tensor_reduce(t_m, t_g, AX.X, ALU.add))
        dc.link(nc.vector.reciprocal(t_m, t_m))
        nc.vector.tensor_tensor(t_key[:, 2, :, :].rearrange("p c (a k) -> p (c a) k", a=PH), t_g,
                                t_m.broadcast_to([P, 16, TOPK]), ALU.mult).then_inc(tk_dve, 1)
        yield 1.0

    def emap_of(half, st):
        v = emap[:, half * HALF:half * HALF + HALF, bass.ds(st.lin(GT), GT)]
        return v.rearrange("p a t -> p t a")

    NB = T // GT

    def hots(dve, dc, half, st):
        if half or st.s >= 1:
            dve.wait_ge(gm_done, st.lin(1, NB * half))
        tok = bass.ds(st.lin(GT), GT)
        sa, sb_ = [P, GT, HALF], [P, GT, P]
        iota = iota_b
        dc.mark(nc.vector.tensor_tensor(hot_a[:, 2], iota[:, half * HALF:half * HALF + HALF].unsqueeze(1).broadcast_to(sa),
                                        idx[:, 0, tok].unsqueeze(2).broadcast_to(sa), ALU.is_equal))
        nc.vector.tensor_tensor(hot_b, iota.unsqueeze(1).broadcast_to(sb_),
                                idx[:, 1, tok].unsqueeze(2).broadcast_to(sb_), ALU.is_equal)
        dc.need()
        for i in range(3):
            ins = nc.vector.tensor_tensor(hot_a[:, i], hot_a[:, 2],
                                          gate_part[:, i, tok].unsqueeze(2).broadcast_to(sa), ALU.mult)
            if i == 1:
                dc.link(ins)
        ins.then_inc(hot_ready, 1)

    def take_gates(dve, half, st):
        dve.wait_ge(gm_done, st.lin(1, NB * half + 1))
        v = emap_of(half, st)
        nc.vector.tensor_tensor(v, v, ps[:, 6 + st.mod(2), :].rearrange("p (t a) -> p t a", t=GT), ALU.mult)\
            .then_inc(gm_taken, 1)

    def gates_of_batch_pe(pe, half, st):
        pe.wait_ge(hot_ready, st.lin(1, NB * half + 1))
        if half or st.s >= 2:
            pe.wait_ge(gm_taken, st.lin(1, NB * half - 1))
        for q in range(GT):
            out = ps[:, 6 + st.mod(2), q * HALF:q * HALF + HALF]
            for i in range(3):
                ins = nc.tensor.matmul(out, hot_b[:, q, :], hot_a[:, i, q, :], start=i == 0, stop=i == 2)
        ins.then_inc(gm_done, 1)

    def prev(st):
        return Step(st.s - 1, st.stride, st.i)

    def expert_up_pe(pe, st, a, b):
        if a * st.s + b >= 2:
            pe.wait_ge(gelu_done, st.lin(a, b - 1))
        up(pe, arrived(pe, st, a, b + UP0), ps[:, 4 + st.mod(2, a, b), 0:T])

    def expert_down_pe(pe, st, a, b):
        pe.wait_ge(z_ready, st.lin(a, b + ZB["peer"] + 1))
        n = a * st.s + b
        down(pe, arrived(pe, st, a, b + DOWN0), ez[st.mod(2, a, b)], n == 0, n == NKEY - 1)

    def peer_pe(pe):
        pe.wait_ge(tk_act, 8)
        steps(pe, None, 0, HALF, 6, lambda st: expert_up_pe(pe, st, 1, 0), first=2)
        peer_turn_pe(pe)

        def second(st):
            for u in range(2):
                expert_up_pe(pe, st, 2, HALF + u)
            gates_of_batch_pe(pe, 0, st)

        steps(pe, None, 0, NB, 6, second, first=2)

        def third(st):
            for u in range(2):
                expert_down_pe(pe, st, 2, u)
            gates_of_batch_pe(pe, 1, st)

        steps(pe, None, 0, NB, 6, third, first=2)
        steps(pe, None, HALF, NKEY - 1, 6, lambda st: expert_down_pe(pe, st, 1, 0))
        expert_down_pe(pe, Step(NKEY - 1), 1, 0)

    def peer_act(act):
        def one(st):
            act.wait_ge(chunk_done, st.lin(1, UP0 + 1))
            nc.scalar.activation(emap[:, st.lin(1), :], ps[:, 4 + st.mod(2), 0:T], ACT.Gelu).then_inc(gelu_done, 1)
            split_hi(act, st, 1, UP0 + RING)

        steps(act, None, 0, 48, 6, one)
        act.wait_ge(tk_dve, 1)
        nc.scalar.activation(t_g, t_g, ACT.Exp).then_inc(tk_act, 1)
        steps(act, None, 48, HALF, 6, one)
        act.wait_ge(tk_pe, 9)
        nc.scalar.activation(iota_b, con_("iota"), ACT.Copy)
        nc.scalar.activation(idx, ps[:, 0:2, 0:T], ACT.Copy)
        nc.scalar.activation(gate_part[:, 0], ps[:, 2, 0:T], ACT.Copy).then_inc(tk_act, 1)
        steps(act, None, HALF, NKEY, 6, one)

        def z(st, gates=None):
            if st.s >= 2:
                walk_act(act, st, 1, DOWN0 - 2)
            if gates is not None:
                act.wait_ge(gm_taken, gates)
            nc.scalar.activation(ez[st.mod(2)][0], emap[:, st.lin(1), :], ACT.Copy).then_inc(ez_hi, 1)

        z(Step(0), NB)
        steps(act, None, 1, HALF, 6, z, first=2)
        z(Step(HALF), 2 * NB)
        steps(act, None, HALF + 1, NKEY - RING, 6, z)
        for n in range(NKEY - RING, NKEY):
            z(Step(n))
        for n in (NKEY, NKEY + 1):
            walk_act(act, Step(n), 1, DOWN0 - 2)

    def peer_dve(dve, dc):
        done, us = 0, 0.0
        for price in peer_top(dve, dc):
            us += price
            while done < HALF and us >= 1.8 * (done + 1):
                walk_dve(dve, Step(done), 1, UP0)
                done += 1
        range_dve(dve, UP0 + done, UP0 + HALF)
        dve.wait_ge(tk_act, 10)
        dc.link(nc.vector.tensor_tensor(gate_left[:, 0], ps[:, 2, 0:T], gate_part[:, 0], ALU.subtract))
        dc.link(nc.vector.tensor_copy(gate_part[:, 1], gate_left[:, 0]))
        dc.link(nc.vector.tensor_tensor(gate_part[:, 2], gate_left[:, 0], gate_part[:, 1], ALU.subtract))

        def second(st):
            hots(dve, dc, 0, st)
            for u in range(2):
                walk_dve(dve, st, 2, UP0 + HALF + u - 1) if st.s or u else None
            if st.s >= 1:
                take_gates(dve, 0, prev(st))

        steps(dve, dc, 0, NB, 6, second, first=1, per=2)
        walk_dve(dve, Step(NKEY - 1), 1, UP0)
        take_gates(dve, 0, Step(NB - 1))

        def z_rest(st, a, b):
            p = st.mod(2, a, b)
            dve.wait_ge(ez_hi, st.lin(a, b + 1))
            nc.vector.tensor_tensor(ez[p][1], emap[:, st.lin(a, b), :], ez[p][0].bitcast(F32), ALU.subtract)\
                .then_inc(z_ready, 1)

        z_rest(Step(0), 1, 0)

        def third(st, last=False):
            z_rest(st, 2, 1)
            hots(dve, dc, 1, st)
            if st.s >= 1:
                walk_dve(dve, st, 2, DOWN0 - 1)
            if not last:
                z_rest(st, 2, 2)
            walk_dve(dve, st, 2, DOWN0)
            if st.s >= 1:
                take_gates(dve, 1, prev(st))

        steps(dve, dc, 0, NB - 1, 6, third, first=1, per=2)
        third(Step(NB - 1), last=True)
        take_gates(dve, 1, Step(NB - 1))

        def fourth(st):
            z_rest(st, 1, 0)
            walk_dve(dve, st, 1, DOWN0 - 1)

        steps(dve, None, HALF, NKEY - RING, 6, fourth)
        for n in range(NKEY - RING, NKEY):
            fourth(Step(n))
        dve.wait_ge(chunk_done, NCH)

    HP = {0: 0, 1: 4, 2: 8, 3: 12, 5: 16, 6: 20}

    with nc.Block() as block:
        @block.sync
        def _(sp):
            sp.dma_start(x[:, :, :], xT).then_inc(s_x, 16)
            sp.dma_start(tabs[:, :], par).then_inc(s_par, 16)
            stream_all(sp)
            sp.wait_ge(x_normed, 2)
            sp.dma_start(y, x[:, :, :]).then_inc(s_y, 16)
            sp.wait_ge(s_y, 16)

        @block.gpsimd
        def _(pool):
            nc.gpsimd.memset(ones[:, :], 1.0).then_inc(s_ones, 1)
            pool.dma_start(cons[:, :], con).then_inc(s_con, 16)
            pool.dma_start(wg_s, wg).then_inc(s_small, 16)
            range_pool(pool, 0, CH["wo"] + RING)
            pool.wait_ge(rope_done, 16)
            heads_pool(pool, HB["moba"], 16, lambda st: heads[:, st.lin(1), :])
            range_pool(pool, CH["wo"] + RING, CH["ffn1"] + RING)
            pool.wait_ge(chunk_done, CH["ffn1"])
            pool.dma_start(wk_s, wcmpk).then_inc(s_cmp, 16)
            pool.dma_start(wv_s, wcmpv).then_inc(s_cmp, 16)
            pool.dma_start(pe_s, peT).then_inc(s_cmp, 16)
            pool.dma_start(alibi, alibi_t).then_inc(s_cmp, 16)
            range_pool(pool, CH["ffn1"] + RING, CH["merge"] + RING)
            pool.wait_ge(tile_copied, TC["p_tok"])
            heads_pool(pool, HB["sb"], 8, lambda st: heads[:, st.lin(1), :])
            for name, g0, *_ in NSA:
                heads_pool(pool, HB[name], 4, lambda st, g0=g0: heads[:, st.lin(1, 16 + g0), :])
            hg_pool(pool)
            range_pool(pool, CH["merge"] + RING, CH["pq"] + RING)
            pool.wait_ge(chunk_done, CH["pq"])
            nc.gpsimd.memset(keys_s, 0.0).then_inc(keys_zeroed, 1)
            pool.wait_ge(keys_zeroed, 1)
            pool.dma_start(keys_s[0:HD, 0:NKEY], subk[0, :, :]).then_inc(s_keys, 16)
            pool.dma_start(keys_s[HD:P, NKEY:2 * NKEY], subk[1, :, :]).then_inc(s_keys, 16)
            range_pool(pool, CH["pq"] + RING, NCH)

        @block.tensor
        def _(pe):
            pe.wait_ge(s_ones, 1)
            norm_pe(pe, 0)
            gated_pe(pe, "sc", KD, 3, 6, z_full, 0, HP[0])
            norm_pe(pe, 4)
            gated_pe(pe, "ffn0", NF, 2, 2, conv_u_done, 0, HP[1])
            norm_pe(pe, 8)
            pe.wait_ge(s_con, 16)
            qk_pe(pe)
            project_pe(pe, "qkv", 8, tokens_out=True, skip=16)
            pe.wait_ge(tile_copied, 24)
            heads_pe(pe, HB["moba"], 16, lambda st: heads[:, st.lin(1, 16), :],
                     lambda st, c: vtok[:, c, bass.ds(st.lin(HD), HD)], 1)
            pe.wait_ge(o_read, 16)
            turn_out_pe(pe, 0)
            wo_pe(pe)
            norm_pe(pe, 12)
            gated_pe(pe, "ffn1", NF, 2, 2, conv_u_done, NF, HP[3])
            norm_pe(pe, 16)
            norm_pe(pe, 20)
            gates_pe(pe)
            project_pe(pe, "p_split", 16, hb=HP[5])
            project_pe(pe, "p_tok", 6, tokens_out=True)
            project_pe(pe, "p_feat", 16)
            pe.wait_ge(tile_copied, TC["p_feat"] + 16)
            cmp_pe(pe)
            pe.wait_ge(cmp_dve_s, 5)
            heads_pe(pe, HB["sb"], 8, lambda st: heads[:, st.lin(1, 8), :],
                     lambda st, c: vtok[:, c, bass.ds(st.lin(HD), HD)], 2)
            for name, g0, br, kh, vcol in NSA:
                heads_pe(pe, HB[name], 4, lambda st, kh=kh: heads[:, kh, :],
                         lambda st, c, vcol=vcol: vtok[:, c, vcol:vcol + HD], 1)
            pe.wait_ge(o_read, HB["end"])
            turn_out_pe(pe, 4)
            hg_pe(pe)
            merge_pe(pe)
            norm_pe(pe, 24)
            project_pe(pe, "pq", KD, hb=HP[6])
            peer_scores_pe(pe)
            peer_pe(pe)
            norm_pe(pe, 28)

        @block.scalar
        def _(act):
            ac = Chain(act, act_c)
            for c in range(RING):
                split_hi(act, Step(c), 1, 0)
            norm_act(act, 0, s_x, 16, HP[0])
            sc_act(act)
            norm_act(act, 1, x_part, 0, HP[1])
            ffn_act(act, "ffn0", 0)
            norm_act(act, 2, x_part, 4, HP[2])
            qk_act(act)
            project_act(act, ac, "qkv", 8, copy_tokens, vtok, 16, skip=16)
            soft_act(act, HB["moba"], 16)
            turn_out_act(act, 0)
            range_act(act, CH["wo"], CH["ffn1"])
            norm_act(act, 3, x_part, 8, HP[3])
            ffn_act(act, "ffn1", NF)
            norm_act(act, 4, x_part, 12)
            norm_act(act, 5, x_normed, 1, HP[5])
            gates_act(act)
            project_act(act, ac, "p_split", 16, copy_heads, heads)
            project_act(act, ac, "p_tok", 6, copy_tokens, vtok, 0)
            project_act(act, ac, "p_feat", 16, copy_feat, hfeat)
            cmp_act(act)
            stick_act(act, ac, HB["sb"], 8)
            for name, *_ in NSA:
                soft_act(act, HB[name], 4)
            turn_out_act(act, 4)
            hg_act(act, ac)
            merge_act(act)
            norm_act(act, 6, x_part, 16, HP[6])
            project_act(act, ac, "pq", KD, copy_feat, t_q)
            peer_top_act(act)
            peer_act(act)
            norm_act(act, 7, x_part, 20)

        @block.vector
        def _(dve):
            dc = Chain(dve, dve_c)
            for c in range(RING):
                split_lo(dve, nc.vector, Step(c), 1, 0)
            dve.wait_ge(s_par, 16)
            norm_dve(dve, dc, 0, "mix0", HP[0])
            sc_dve(dve, dc)
            residual_dve(dve, dc)
            norm_dve(dve, dc, 1, "ffn0", HP[1])
            ffn_dve(dve, dc, "ffn0", "fconv0", 0)
            residual_dve(dve, dc)
            norm_dve(dve, dc, 2, "mix1", HP[2])
            dve.wait_ge(s_con, 16)
            qk_dve(dve, dc)
            range_dve(dve, CH["qkv"] + 16, CH["wo"])
            soft_dve(dve, dc, HB["moba"], 16, lambda st: con_("causal"), rows_soft, 1)
            turn_out_dve(dve, 0)
            range_dve(dve, CH["wo"], CH["ffn1"])
            dve.wait_ge(chunk_done, CH["ffn1"])
            residual_dve(dve, dc)
            norm_dve(dve, dc, 3, "ffn1", HP[3])
            ffn_dve(dve, dc, "ffn1", "fconv1", NF)
            residual_dve(dve, dc)
            norm_dve(dve, dc, 4, "fin1")
            norm_dve(dve, dc, 5, "mix2", HP[5])
            range_dve(dve, CH["p_split"], CH["merge"])
            cmp_dve(dve, dc)
            stick_dve(dve, dc, HB["sb"], 8, rows_stick)
            for name, g0, br, kh, vcol in NSA:
                dve.wait_ge(o_read, HB[name])
                soft_dve(dve, dc, HB[name], 4, lambda st, g0=g0: alibi[:, st.lin(1, g0), :],
                         rows_nsa(br, g0, dc), 2)
            turn_out_dve(dve, 4)
            hg_dve(dve, dc)
            merge_dve(dve, dc)
            residual_dve(dve, dc)
            norm_dve(dve, dc, 6, "ffn2", HP[6])
            range_dve(dve, CH["pq"], CH["peer"])
            peer_dve(dve, dc)
            residual_dve(dve, dc)
            norm_dve(dve, dc, 7, "fin2")


def constants():
    c = np.zeros((P, NCON), np.float32)

    def put(name, a):
        a = np.asarray(a, np.float32).reshape(P, -1)
        c[:, COFF[name]:COFF[name] + a.shape[1]] = a

    p = np.arange(P)
    put("ident", np.eye(P))
    swap = np.zeros((P, P))
    swap[p ^ 32, p] = 1.0
    put("swap", swap)
    half = HD // 2
    inv = (10000.0 ** (-np.arange(half, dtype=np.float32) / np.float32(half))).astype(np.float32)
    ang = inv[p % half][:, None] * np.arange(T, dtype=np.float32)[None, :]
    ang = ang.astype(np.float32)
    put("cos", np.cos(ang))
    put("sin", np.sin(ang) * np.where(p % HD < half, -1.0, 1.0)[:, None])
    t = np.concatenate([np.broadcast_to(p[:, None], (P, P)), np.broadcast_to(p[:, None] + P, (P, T))], 1)
    k = np.concatenate([np.broadcast_to(np.arange(P)[None], (P, P)), np.broadcast_to(np.arange(T)[None], (P, T))], 1)
    put("causal", np.where(k <= t, 0.0, NEG))
    put("strict", np.where(k < t, 0.0, NEG))
    slopes = 2.0 ** (-(np.arange(8) + 1.0))
    tok = p[:, None, None, None] + P * np.arange(2)[None, None, :, None]
    dist = tok - (16 * np.arange(CMP)[None, None, None, :] + 31)
    ok = (dist >= 0) & (np.arange(CMP) < CMP - 1)
    put("cmpbias", np.where(ok, -slopes[None, :, None, None] * dist, NEG))
    put("rowok", (p[:, None] + P * np.arange(2)[None] >= 31) * 1.0)
    put("pairs", np.stack([p[:, None] // L == p[None] // L for L in LEVELS[1:-1]], 1) * 1.0)
    put("iota", np.broadcast_to(np.arange(P), (P, P)))
    put("iota16", np.broadcast_to(np.arange(TOPK), (P, TOPK)))
    alibi = np.stack([np.where(k <= t, -s * (t - k), NEG) for s in slopes], 1).astype(np.float32)
    return c, alibi


def up_chunks(w, cols):
    w = w[:, cols] if not isinstance(cols, slice) or cols != slice(None) else w
    n = w.shape[1] // P
    return w.reshape(KD, P, n, P).transpose(2, 1, 0, 3).reshape(n, P, D)


def interleave(ups, downs):
    out = []
    for j in range(len(ups)):
        out += list(ups[j])
        if j:
            out.append(downs[j - 1])
    return out + [downs[-1]]


def lay_out(a):
    w = {k: np.asarray(v) for k, v in a.items()}
    s = []
    b = up_chunks(w["sc_w_in"][0], slice(None))
    s += interleave([(b[j], b[KD + j], b[2 * KD + j]) for j in range(KD)], w["sc_w_out"][0].reshape(KD, P, D))

    def ffn(i):
        b = up_chunks(w["ffn_w_up"][i], slice(None))
        return interleave([(b[j], b[NF + j]) for j in range(NF)], w["ffn_w_down"][i].reshape(NF, P, D))

    s += ffn(0)
    s += list(up_chunks(w["moba_w_qkv"][0], slice(None)))
    s += list(w["moba_w_o"][0].reshape(KD, P, D))
    s += ffn(1)
    win = w["w_in_2"][0]
    kv = 2048
    hg = kv + 768 + 24
    s += list(up_chunks(win[:, 0:1024], slice(None)))
    s += list(up_chunks(win[:, 1536:2048], slice(None)))
    for i in (0, 1, 2, 4):
        s += list(up_chunks(win[:, kv + i * P:kv + i * P + P], slice(None)))
    s += list(up_chunks(win[:, 1024:1536], slice(None)))
    for i in (3, 5):
        s += list(up_chunks(win[:, kv + i * P:kv + i * P + P], slice(None)))
    s += list(up_chunks(win[:, hg:hg + 2048], slice(None)))
    gm = up_chunks(win[:, hg + 2048:], slice(None))
    br = [w[n][0].reshape(4, P, KD, P).transpose(2, 1, 0, 3).reshape(KD, P, 4 * P)
          for n in ("w_branch_sb_2", "w_branch_nsa_2", "w_branch_hgrn_2")]
    pad = np.zeros((P, 4 * P), np.float32)
    s += interleave([(gm[j], gm[KD + j], np.concatenate([br[0][j], br[1][j]], 1), gm[2 * KD + j],
                      np.concatenate([br[2][j], pad], 1)) for j in range(KD)],
                    w["w_out_2"][0].reshape(KD, P, D))
    s += list(up_chunks(w["peer_w_q_2"][0], slice(None)))
    u = w["peer_u_2"][0].reshape(NKEY, NKEY, KD, P).transpose(0, 3, 2, 1).reshape(NKEY, P, D)
    v = w["peer_v_2"][0].reshape(NKEY, NKEY, D)
    s += list(u) + list(v)
    stream = np.empty((len(s), P, D), np.float32)
    for i, c in enumerate(s):
        stream[i] = c
    par = np.zeros((P, NPAR), np.float32)

    def put(name, a):
        a = a.reshape(P, -1)
        par[:, POFF[name]:POFF[name] + a.shape[1]] = a

    def vec(v):
        return v.reshape(-1, P).T

    def taps(v):
        return v.reshape(3, -1, P).transpose(2, 1, 0)

    for name, v in (("mix0", w["mix_norm"][0]), ("mix1", w["mix_norm"][1]), ("ffn0", w["ffn_norm"][0]),
                    ("ffn1", w["ffn_norm"][1]), ("fin1", w["final_norm"]), ("mix2", w["norm_mix_2"][0]),
                    ("ffn2", w["norm_ffn_2"][0]), ("fin2", w["norm_final_2"]), ("hnorm", w["hgrn_norm_2"][0])):
        put(name, vec(v))
    put("sconv", taps(w["sc_w_conv"][0]))
    put("fconv0", taps(w["ffn_w_conv"][0]))
    put("fconv1", taps(w["ffn_w_conv"][1]))
    return {
        "stream": stream,
        "xT": w["x"][0].T.reshape(KD, P, T).transpose(1, 0, 2),
        "par": par,
        "con": constants()[0],
        "alibi_t": constants()[1],
        "wg": win[:, kv + 768:hg].reshape(KD, P, 24).transpose(1, 0, 2),
        "wcmpk": w["nsa_w_cmp_k_2"][0].reshape(32, HD, HD).transpose(1, 0, 2),
        "wcmpv": w["nsa_w_cmp_v_2"][0].reshape(32, HD, HD).transpose(1, 0, 2),
        "peT": w["nsa_cmp_pe_2"][0].T,
        "subk": w["peer_sub_keys_2"][0].transpose(0, 2, 1),
    }


def kernel(**inputs):
    import concourse.bacc as bacc
    from concourse.bass_utils import run_bass_kernel_spmd as run

    nc = bacc.Bacc("TRN2", target_bir_lowering=False, num_devices=1)
    arrays, args = {}, []
    for name, a in lay_out(inputs).items():
        a = np.ascontiguousarray(a)
        arrays[name] = a
        args.append(nc.dram_tensor(name, a.shape, F32, kind="ExternalInput").ap())
    y = nc.dram_tensor("y", (P, KD, T), F32, kind="ExternalOutput").ap()
    build(nc, *args, y)
    r = run(nc, [arrays], core_ids=[0])
    return r.results[0]["y"].transpose(2, 1, 0).reshape(1, T, D)
```

```python
import numpy as np
import concourse.bass as bass
from concourse import mybir

F32 = mybir.dt.float32
F32R = mybir.dt.float32r
BF16 = mybir.dt.bfloat16
U32 = mybir.dt.uint32
ALU = mybir.AluOpType
ACT = mybir.ActivationFunctionType
AX = mybir.AxisListType

P = 128
T = 256
D = 1024
KD = D // P
FF = 2816
NF = FF // P
HD = 64
EPS = 1e-6
NEG = -1e30
SCALE = HD ** -0.5
RING = 3
CUT, CUT_PEER = 672, 384
LEVELS = [1 << l for l in range(8)]
NKEY = 128
TOPK = 16
PH = 8
CMP = 16
SC3 = 384

PARTS = [("mix0", KD), ("mix1", KD), ("ffn0", KD), ("ffn1", KD), ("fin1", KD), ("mix2", KD),
         ("ffn2", KD), ("fin2", KD), ("sconv", KD * 3), ("fconv0", 2 * NF * 3), ("fconv1", 2 * NF * 3),
         ("hnorm", 4)]
POFF = {}
_o = 0
for _n, _w in PARTS:
    POFF[_n] = _o
    _o += _w
NPAR = _o
CPARTS = [("ident", P), ("iota", P), ("iota16", TOPK), ("swap", P), ("cos", T), ("sin", T),
          ("causal", SC3), ("strict", SC3), ("cmpbias", 8 * 2 * CMP), ("pairs", (len(LEVELS) - 2) * P), ("rowok", 2)]
COFF = {}
_o = 0
for _n, _w in CPARTS:
    COFF[_n] = _o
    _o += _w
NCON = _o


class Step:

    def __init__(self, s, stride=0, i=None):
        self.s, self.stride, self.i = s, stride, i

    def lin(self, a, b=0):
        v = a * self.s + b
        return v if self.i is None else self.i * (a * self.stride) + v

    def mod(self, n, a=1, b=0):
        assert self.i is None or (a * self.stride) % n == 0
        return (a * self.s + b) % n


class Chain:

    def __init__(self, eng, sem):
        self.eng, self.sem, self.n, self.per, self.i = eng, sem, 0, 0, None

    def mark(self, ins):
        ins.then_inc(self.sem, 1)
        self.n += 1
        return self.n

    def need(self, k=None):
        k = self.n if k is None else k
        self.eng.wait_ge(self.sem, k if self.i is None else self.i * self.per + k)

    def link(self, ins):
        self.mark(ins)
        self.need()


def steps(eng, chain, lo, hi, body, fn, first=0, per=0):
    n = lo
    while n < min(first, hi):
        fn(Step(n))
        n += 1
    turns = (hi - n) // body
    if turns > 1:
        with eng.Fori(0, turns) as i:
            if chain is not None:
                at = chain.n
                chain.i, chain.per = i, per * body
            for u in range(body):
                fn(Step(n + u, body, i))
            if chain is not None:
                assert chain.n - at == per * body, (chain.n - at, per, body)
                chain.n = at + per * body * turns
                chain.i = None
        n += body * turns
    while n < hi:
        fn(Step(n))
        n += 1


def chunk_plan():
    at, out = 0, {}
    for name, n in [("sc", 4 * KD), ("ffn0", 3 * NF), ("qkv", 24), ("wo", KD), ("ffn1", 3 * NF),
                    ("p_split", 16), ("p_tok", 6), ("p_feat", 16), ("merge", 6 * KD),
                    ("pq", KD), ("peer", 2 * NKEY)]:
        out[name] = at
        at += n
    out["end"] = at
    return out


CH = chunk_plan()
UP0, DOWN0 = CH["peer"], CH["peer"] + NKEY
HALF = NKEY // 2
GT = 8


def build(nc, stream, xT, par, con, alibi_t, wg, wcmpk, wcmpv, peT, subk, y):
    def sem(name):
        return nc.alloc_semaphore(name)

    def sb(name, shape, dt=F32):
        return nc.alloc_sbuf_tensor(name, shape, dt)

    base = (nc.sbuf_base + 63) // 64 * 64
    END = (nc.sbuf_usable_end - base) // 32 * 8
    names = {}

    def at(o, *dims, parts=P, dt=F32):
        n = int(np.prod(dims))
        assert o >= 0 and o + n <= END, (o, n, END)
        name = f"m{o}_{len(names)}"
        names[name] = 1
        v = nc.alloc_sbuf_tensor_at(name, [parts, n], dt, offset=base + 4 * o)[:, :]
        if len(dims) == 2:
            v = v.rearrange("p (a b) -> p a b", a=dims[0])
        elif len(dims) == 3:
            v = v.rearrange("p (a b c) -> p a b c", a=dims[0], b=dims[1])
        elif len(dims) == 4:
            v = v.rearrange("p (a b c d) -> p a b c d", a=dims[0], b=dims[1], c=dims[2])
        return v

    class Area:

        def __init__(self, at_, end=END):
            self.at, self.end = at_, end

        def take(self, *dims, parts=P, dt=F32):
            o = self.at
            size = int(np.prod(dims)) // (2 if dt == BF16 else 1)
            self.at += (size + 7) // 8 * 8
            assert self.at <= self.end, (self.at, self.end)
            return at(o, *dims, parts=parts, dt=dt)

    l_ = Area(0)
    raw = l_.take(RING, D)
    w_hi, w_lo = l_.take(RING, D, dt=F32R), l_.take(RING, D, dt=F32R)
    x = l_.take(KD, T)
    h_hi, h_lo = l_.take(KD, T, dt=F32R), l_.take(KD, T, dt=F32R)
    z_hi, z_lo = l_.take(T, dt=F32R), l_.take(T, dt=F32R)
    tabs = l_.take(NPAR)
    ones = l_.take(T)
    O_NORM = l_.at
    norm_t, rstd = l_.take(T), l_.take(T)
    O_CONS = l_.at
    cons = l_.take(NCON)
    A0 = l_.at

    def con_(name, n=None):
        o = COFF[name]
        return cons[:, o:o + (n or dict(CPARTS)[name])]

    def par_(name, a, n=1):
        return tabs[:, bass.ds(a + POFF[name], n)]

    ident = con_("ident")
    ps = nc.alloc_psum_tensor("ps", [P, 8, 512], F32)
    acc = ps[:, 0:4, :]

    f_ = Area(END - 8 * T)
    conv_g, conv_u, copied, rope_a, rope_b = f_.take(T), f_.take(T), f_.take(2, T), f_.take(T), f_.take(T)
    silu_o, z_f = f_.take(T), f_.take(T)
    sg = at(END - 6 * T, 3, T)
    m_ = Area(A0)
    heads = m_.take(32, T, parts=HD)
    vtok = m_.take(2, D)
    otok = m_.take(2, D)
    O_ATT = m_.at
    a_s, a_e, a_t = (m_.take(2, SC3) for _ in range(3))
    m_.take(2, SC3)
    a_q = m_.take(2, T, parts=HD)
    a_max = m_.take(2, 2)
    a_sum = m_.take(64, 2)
    a_r = m_.take(1, 2)
    a_c = m_.take(SC3)
    O_OT = m_.at
    oT_hi, oT_lo = m_.take(12, T, dt=F32R), m_.take(12, T, dt=F32R)
    O_HF = m_.at
    hfeat = m_.take(16, T)
    gates = m_.take(2, 24)
    wg_s = m_.take(KD, 24)
    SCR = m_.at
    sq, h_f = at(O_HF, KD, T), at(O_HF + KD * T, KD, T)
    c_ = Area(O_OT, O_HF)
    wk_s, wv_s = c_.take(16, HD), c_.take(16, HD)
    pe_s = c_.take(32, parts=HD)
    kc, vc = c_.take(2, CMP, parts=HD), c_.take(2, HD, parts=CMP)
    ce, cm = c_.take(16 * CMP), c_.take(16)
    ceT = at(O_ATT, 16, P, parts=CMP)
    st_s, st_l = at(O_OT, 8, SC3), at(O_OT + 8 * SC3, 8, SC3)
    assert O_OT + 16 * SC3 <= O_HF
    s_ = Area(SCR)
    alibi = s_.take(8, SC3)
    blk_k, blk_v = s_.take(16, 2, CMP), s_.take(16, 2, 32)
    h_lf = s_.take(4, T)
    hq, hf, hi, hg = (hfeat[:, 4 * i:4 * i + 4, :] for i in range(4))
    g_ = Area(SCR)
    h_o = g_.take(4, T)
    h_k = hf
    h_tmp = at(O_ATT + 16 * P, 4, T)
    g2_ = Area(A0, O_ATT - 2 * D)
    lv_q, lv_k = g2_.take(2, 4 * P), g2_.take(2, 4 * P)
    lv_a, lv_i = g2_.take(2, 4, P), g2_.take(2, 4 * P)
    lv_v = g2_.take(2, 4 * P)
    h_c, h_r = h_lf, at(O_ATT, 4, T)

    emap = at(A0, NKEY, T)
    assert A0 + T * NKEY <= END
    t_ = Area(A0 + HALF * T, A0 + NKEY * T)
    O_TQ = t_.at
    t_q, t_s = t_.take(PH, T), t_.take(32, NKEY)
    t_1 = at(O_TQ, P, TOPK)
    t_b, t_if = t_.take(32, TOPK), t_.take(32, TOPK)
    t_i = t_.take(32, TOPK).bitcast(U32)
    t_c = t_.take(16, TOPK * TOPK)
    t_g = t_.take(16, TOPK)
    t_w, t_wi, t_wj = (t_.take(16, TOPK).bitcast(U32) for _ in range(3))
    t_wf = t_.take(2, 16, TOPK)
    t_m = t_.take(16, 1)
    t_key = t_.take(3, 2, P)
    keys_s = t_.take(2 * NKEY)
    b_ = Area(O_CONS + COFF["swap"], O_CONS + COFF["rowok"])
    idx = b_.take(2, T, dt=BF16)
    gate_left = b_.take(1, T)
    gate_part = b_.take(3, T, dt=BF16)
    iota_b = b_.take(P, dt=BF16)
    hot_b, hot_a = b_.take(GT, P, dt=BF16), b_.take(3, GT, HALF, dt=BF16)
    ez = [(z_hi, z_lo), (at(O_NORM, T, dt=F32R), at(O_NORM + T, T, dt=F32R))]

    s_x = sem("x_loaded")
    s_par = sem("params_loaded")
    s_con = sem("constants_loaded")
    s_small = sem("gate_weights_loaded")
    s_cmp = sem("compression_loaded")
    s_keys = sem("sub_keys_loaded")
    keys_zeroed = sem("sub_keys_zeroed")
    ring_full = [sem(f"ring_full{r}") for r in range(RING)]
    chunk_done = sem("chunk_multiplied")
    s_ones = sem("ones_written")
    x_part = sem("x_part_updated")
    sq_part = sem("square_ready")
    sum_ready = sem("square_sum_ready")
    recip_ready = sem("recip_ready")
    rstd_ready = sem("rstd_ready")
    h_tile = sem("h_tile_ready")
    h_part = sem("h_pair_split")
    hi_part = sem("h_pair_hi")
    x_normed = sem("x_normed")
    hi_done = sem("chunk_hi_ready")
    lo_done = [sem(f"chunk_lo_ready{r}") for r in range(RING)]
    z_full = sem("z_full_ready")
    tile_copied = sem("tile_copied")
    conv_g_done = sem("conv_g_done")
    conv_u_done = sem("conv_u_done")
    c_copied = sem("c_copied")
    silu_done = sem("silu_done")
    z_ready = sem("z_ready")
    rot_ready = sem("rotated_ready")
    rope_done = sem("rope_done")
    dve_c, act_c, pool_c, pe_c = sem("dve_chain"), sem("act_chain"), sem("pool_chain"), sem("pe_chain")
    q_staged = sem("q_staged")
    s_ready = sem("scores_ready")
    s_read = sem("scores_read")
    max_ready = sem("max_ready")
    soft_ready = sem("softplus_ready")
    logit_ready = sem("log_weight_ready")
    e_ready = sem("weights_ready")
    et_ready = sem("weights_transposed")
    et_copied = sem("weights_transposed_copied")
    pv_ready = sem("pv_ready")
    o_read = sem("o_read")
    ot_ready = sem("o_transposed")
    ot_copied = sem("o_transposed_hi")
    ot_split = sem("o_transposed_split")
    gate_ready, gate_copied = sem("gate_ready"), sem("gate_copied")
    cmp_dve_s, cmp_pe_s, cmp_act_s = sem("cmp_vector_stage"), sem("cmp_tensor_stage"), sem("cmp_scalar_stage")
    hg_dve_s, hg_pe_s, hg_act_s = sem("hgrn_vector_stage"), sem("hgrn_tensor_stage"), sem("hgrn_scalar_stage")
    lv_widened, lv_exp, r_zeroed = sem("level_sums_widened"), sem("level_decays_ready"), sem("sums_behind_zeroed")
    lv_ready, lv_scored = sem("level_operands_ready"), sem("level_scores_ready")
    lv_values, lv_masked, lv_turned = sem("level_values_gathered"), sem("level_scores_masked"), sem("level_values_transposed")
    lv_copied, lv_added = sem("level_values_copied"), sem("level_added")
    sg_ready, branch_taken = sem("merge_gate_ready"), sem("branch_taken")
    tk_pe, tk_act, tk_dve = sem("topk_tensor_stage"), sem("topk_scalar_stage"), sem("topk_vector_stage")
    hot_ready, gm_done, gm_taken = sem("one_hots_ready"), sem("gate_map_ready"), sem("gate_map_taken")
    gelu_done, ez_hi = sem("gelu_done"), sem("gated_expert_hi")
    s_y = sem("y_stored")

    NCH = CH["end"]

    ZB = {"sc": 0, "ffn0": KD, "ffn1": KD + NF, "merge": KD + 2 * NF, "peer": 2 * KD + 2 * NF}
    HB = {"moba": 0, "sb": 16, "nsa": 24, "end": 40}
    MB = {b: b - 8 * (b > HB["sb"]) for b in HB.values()}
    TC = {"qkv": 0, "p_split": 24, "p_tok": 40, "p_feat": 46, "pq": 62}

    def bank(par, sub):
        return ps[:, 4 + 2 * par + sub // 2, (sub % 2) * T:(sub % 2) * T + T]

    def stream_all(sp):
        def one(st):
            r = st.mod(RING)
            if st.s >= RING:
                sp.wait_ge(lo_done[r], lo_count(st, 1, 0) - 2)
            sp.dma_start(raw[:, r, :], stream[st.lin(1), :, :]).then_inc(ring_full[r], 16)
            if st.s == RING - 1:
                sp.dma_start(cons[:, :], con).then_inc(s_con, 16)

        steps(sp, None, 0, NCH, RING, one, first=RING)

    def split_hi(act, st, a, b):
        if st.i is None and a * st.s + b >= NCH:
            return
        r = st.mod(RING, a, b)
        v = 16 * ((a * st.s + b) // RING + 1)
        act.wait_ge(ring_full[r], v if st.i is None else st.i * (16 * (a * st.stride // RING)) + v)
        nc.scalar.activation(w_hi[:, r, :], raw[:, r, :], ACT.Copy).then_inc(hi_done, 1)

    def lo_count(st, a, b):
        v = 2 * ((a * st.s + b) // RING + 1)
        return v if st.i is None else st.i * (2 * (a * st.stride // RING)) + v

    def split_lo(eng, ops, st, a, b):
        if st.i is None and a * st.s + b >= NCH:
            return
        r = st.mod(RING, a, b)
        cut = CUT_PEER if a * st.s + b >= UP0 else CUT
        cols = slice(cut, D) if ops is nc.gpsimd else slice(0, cut)
        eng.wait_ge(hi_done, st.lin(a, b + 1))
        ops.tensor_tensor(w_lo[:, r, cols], raw[:, r, cols], w_hi[:, r, cols].bitcast(F32), ALU.subtract)\
            .then_inc(lo_done[r], 1)

    def walk_act(act, st, a, b):
        act.wait_ge(chunk_done, st.lin(a, b + 1))
        split_hi(act, st, a, b + RING)

    def walk_dve(dve, st, a, b):
        split_lo(dve, nc.vector, st, a, b + RING)

    def range_act(act, lo, hi):
        steps(act, None, lo, hi, RING, lambda st: walk_act(act, st, 1, 0), first=lo + 1)

    def range_dve(dve, lo, hi):
        steps(dve, None, lo, hi, RING, lambda st: walk_dve(dve, st, 1, 0))

    def range_pool(pool, lo, hi):
        steps(pool, None, lo, hi, RING, lambda st: split_lo(pool, nc.gpsimd, st, 1, 0))

    def arrived(pe, st, a, b):
        r = st.mod(RING, a, b)
        pe.wait_ge(lo_done[r], lo_count(st, a, b))
        return r

    def exact(out, lhs, rhs, start, stop, **kw):
        nc.tensor.matmul(out, lhs[0], rhs[0], start=start, stop=False, **kw)
        nc.tensor.matmul(out, lhs[0], rhs[1], start=False, stop=False, **kw)
        return nc.tensor.matmul(out, lhs[1], rhs[0], start=False, stop=stop, **kw)

    def transposed(out, v, unit):
        return nc.tensor.matmul(out, v, unit, start=True, stop=True)

    def wt(r, k):
        return w_hi[:, r, k * P:k * P + P], w_lo[:, r, k * P:k * P + P]

    def up(pe, slot, out, k0=0, nk=KD, rhs=(h_hi, h_lo), r0=0, inc=True, hwait=None):
        for k in range(nk):
            if hwait is not None and k % 2 == 0:
                pe.wait_ge(h_part, hwait + k // 2 + 1)
            ins = exact(out, wt(slot, k0 + k), (rhs[0][:, r0 + k, :], rhs[1][:, r0 + k, :]), k == 0, k == nk - 1)
        if inc:
            ins.then_inc(chunk_done, 1)

    def down(pe, slot, src, first, final):
        for o in range(KD):
            ins = exact(acc[:, o // 2, (o % 2) * T:(o % 2) * T + T], wt(slot, o), src, first and o % 2 == 0,
                        final, skip_group_check=True)
        ins.then_inc(chunk_done, 1)

    def up_at(name, per, j, u):
        return per, CH[name] + u - (1 if j > 0 else 0)

    def down_at(name, per, n, j):
        return per, CH[name] + (per - 2 if j < n else -1)

    def norm_pe(pe, parts):
        for k in range(4):
            pe.wait_ge(sq_part, parts + k + 1)
            for j in (2 * k, 2 * k + 1):
                ins = nc.tensor.matmul(ps[:, 7, 0:T], ones[:, 0:P], sq[:, j, :], start=(j == 0), stop=(j == 7))
        ins.then_inc(sum_ready, 1)

    def gated_pe(pe, name, n, ups, body, free, free_base, hb):
        def one(st):
            if st.s < n:
                if st.s >= 2:
                    pe.wait_ge(free, st.lin(1, free_base - 1))
                for u in range(ups):
                    up(pe, arrived(pe, st, *up_at(name, ups + 1, st.s, u)), bank(st.mod(2), u),
                       hwait=hb if st.s == 0 and u == 0 else None)
            if st.s >= 1:
                pe.wait_ge(z_ready, st.lin(1, ZB[name]))
                r = arrived(pe, st, *down_at(name, ups + 1, n, st.s))
                down(pe, r, (z_hi, z_lo), st.s == 1, st.s == n)

        steps(pe, None, 0, n, body, one, first=2)
        one(Step(n))

    def residual_dve(dve, dc):
        for k in range(4):
            nc.vector.tensor_tensor(x[:, 2 * k:2 * k + 2, :], x[:, 2 * k:2 * k + 2, :],
                                    acc[:, k, :].rearrange("p (a t) -> p a t", a=2), ALU.add).then_inc(x_part, 1)

    def norm_act(act, n, source, base, hb=None, counts="part", first_chunks=0):
        for k in range(4):
            act.wait_ge(source, base + {"x": 0, "part": k + 1, "tile": 2 * k + 2}[counts])
            nc.scalar.activation(sq[:, 2 * k:2 * k + 2, :], x[:, 2 * k:2 * k + 2, :], ACT.Square).then_inc(sq_part, 1)
        for c in range(first_chunks):
            split_hi(act, Step(c), 1, 0)
        act.wait_ge(recip_ready, n + 1)
        nc.scalar.activation(rstd[:, :], norm_t[:, :], ACT.Sqrt).then_inc(rstd_ready, 1)
        if hb is not None:
            for k in range(4):
                act.wait_ge(h_tile, 2 * (hb + k + 1))
                nc.scalar.activation(h_hi[:, 2 * k:2 * k + 2, :], h_f[:, 2 * k:2 * k + 2, :], ACT.Copy)\
                    .then_inc(hi_part, 1)

    def norm_dve(dve, dc, n, weight, hb=None):
        dve.wait_ge(sum_ready, n + 1)
        dc.link(nc.vector.tensor_scalar(norm_t[:, :], ps[:, 7, 0:T], 1.0 / D, EPS, ALU.mult, ALU.add))
        nc.vector.reciprocal(norm_t[:, :], norm_t[:, :]).then_inc(recip_ready, 1)
        dve.wait_ge(rstd_ready, n + 1)
        dst = x if hb is None else h_f
        if hb:
            dve.wait_ge(h_part, hb)
        for k in range(KD):
            ins = nc.vector.scalar_tensor_tensor(dst[:, k, :], x[:, k, :], par_(weight, k), rstd[:, :],
                                                 ALU.mult, ALU.mult)
            ins.then_inc(h_tile if hb is not None else x_normed, 1)
        if hb is None:
            dve.wait_ge(x_normed, KD if n < 7 else 2 * KD)
            return
        for k in range(4):
            dve.wait_ge(hi_part, hb + k + 1)
            nc.vector.tensor_tensor(h_lo[:, 2 * k:2 * k + 2, :], h_f[:, 2 * k:2 * k + 2, :],
                                    h_hi[:, 2 * k:2 * k + 2, :].bitcast(F32), ALU.subtract).then_inc(h_part, 1)
        dve.wait_ge(h_part, hb + 4)

    def split_z(dve, dc, st, name, per, n):
        dve.wait_ge(z_full, st.lin(1, ZB[name] + 1))
        if st.s >= 1:
            a, b = down_at(name, per, n, st.s)
            dve.wait_ge(chunk_done, st.lin(a, b + 1))
        dc.link(nc.vector.tensor_copy(z_hi, z_f))
        nc.vector.tensor_tensor(z_lo, z_f, z_hi.bitcast(F32), ALU.subtract).then_inc(z_ready, 1)
        if st.s >= 1:
            walk_dve(dve, st, a, b)

    def last_down_dve(dve, name, per, n):
        dve.wait_ge(chunk_done, CH[name] + per * n)
        walk_dve(dve, Step(n), *down_at(name, per, n, n))

    def conv(dve, dc, dst, src, wname, tap0):
        yield nc.vector.tensor_scalar(dst, src, par_(wname, tap0 + 2), None, ALU.mult)
        yield nc.vector.scalar_tensor_tensor(dst[:, 1:T], src[:, 0:T - 1], par_(wname, tap0 + 1), dst[:, 1:T],
                                             ALU.mult, ALU.add)
        yield nc.vector.scalar_tensor_tensor(dst[:, 2:T], src[:, 0:T - 2], par_(wname, tap0), dst[:, 2:T],
                                             ALU.mult, ALU.add)

    def ffn_dve(dve, dc, name, wname, sems0):
        n = NF

        def one(st):
            for u in range(2):
                a, b = up_at(name, 3, st.s, u)
                walk_dve(dve, st, a, b)
            dve.wait_ge(chunk_done, st.lin(a, b + 1))
            if st.s >= 1:
                dve.wait_ge(z_ready, st.lin(1, ZB[name]))
            par = st.mod(2)
            cg = conv(dve, dc, conv_g, bank(par, 0), wname, st.lin(3, 0))
            cu = conv(dve, dc, conv_u, bank(par, 1), wname, st.lin(3, NF * 3))
            g1, u1 = dc.mark(next(cg)), dc.mark(next(cu))
            dc.need(g1)
            g2 = dc.mark(next(cg))
            dc.need(u1)
            u2 = dc.mark(next(cu))
            dc.need(g2)
            next(cg).then_inc(conv_g_done, 1)
            dc.need(u2)
            next(cu).then_inc(conv_u_done, 1)
            dve.wait_ge(conv_u_done, st.lin(1, sems0 + 1))
            dve.wait_ge(silu_done, st.lin(1, sems0 + 1))
            nc.vector.tensor_tensor(z_f, silu_o, conv_u, ALU.mult).then_inc(z_full, 1)
            split_z(dve, dc, st, name, 3, n)

        steps(dve, dc, 0, n, 2, one, first=2, per=5)
        last_down_dve(dve, name, 3, n)

    def ffn_act(act, name, sems0):
        def one(st):
            for u in range(2):
                walk_act(act, st, *up_at(name, 3, st.s, u))
            act.wait_ge(conv_g_done, st.lin(1, sems0 + 1))
            nc.scalar.activation(silu_o, conv_g, ACT.Silu).then_inc(silu_done, 1)
            if st.s >= 1:
                walk_act(act, st, *down_at(name, 3, NF, st.s))

        steps(act, None, 0, NF, 2, one, first=2)
        walk_act(act, Step(NF), *down_at(name, 3, NF, NF))

    def sc_dve(dve, dc):
        def one(st):
            par = st.mod(2)
            for u in range(3):
                a, b = up_at("sc", 4, st.s, u)
                walk_dve(dve, st, a, b)
            dve.wait_ge(chunk_done, st.lin(a, b + 1))
            dve.wait_ge(c_copied, st.lin(1, 1))
            if st.s >= 1:
                dve.wait_ge(z_ready, st.lin(1))
            dc.link(nc.vector.tensor_tensor(conv_u, silu_o, bank(par, 2), ALU.mult))
            for ins in conv(dve, dc, conv_g, conv_u, "sconv", st.lin(3)):
                dc.link(ins)
            nc.vector.tensor_tensor(z_f, conv_g, bank(par, 0), ALU.mult).then_inc(z_full, 1)
            split_z(dve, dc, st, "sc", 4, KD)

        steps(dve, dc, 0, KD, 6, one)
        last_down_dve(dve, "sc", 4, KD)

    def sc_act(act):
        def one(st):
            for u in range(2):
                walk_act(act, st, *up_at("sc", 4, st.s, u))
            if st.s >= 1:
                act.wait_ge(z_ready, st.lin(1))
            nc.scalar.activation(silu_o, bank(st.mod(2), 1), ACT.Copy).then_inc(c_copied, 1)
            walk_act(act, st, *up_at("sc", 4, st.s, 2))
            if st.s >= 1:
                walk_act(act, st, *down_at("sc", 4, KD, st.s))

        steps(act, None, 0, KD, 6, one)
        walk_act(act, Step(KD), *down_at("sc", 4, KD, KD))

    def project_pe(pe, name, n, hb=None):
        def one(st):
            g = TC[name]
            if g + st.s >= 2:
                pe.wait_ge(tile_copied, st.lin(1, g - 1))
            up(pe, arrived(pe, st, 1, CH[name]), bank(st.mod(2, 1, g), 0), hwait=hb if st.s == 0 else None)

        steps(pe, None, 0, n, 6, one, first=1 if hb is not None else 0)

    def tokens_pe(pe, name, n, skip=0):
        g = TC[name] + skip
        for i in range(n // 2):
            pe.wait_ge(tile_copied, g - 1 + i if i < 2 else g - 2 + 2 * i)
            for u in range(2):
                r = arrived(pe, Step(skip + 2 * i + u), 1, CH[name])
                for c in range(2):
                    for k in range(4):
                        hk = tuple(h[:, 4 * u + k, c * P:c * P + P] for h in (h_hi, h_lo))
                        wk = tuple(w[:, r, k * T:k * T + T] for w in (w_hi, w_lo))
                        ins = exact(ps[:, 4 + 2 * (i % 2), c * T:c * T + T], hk, wk, u == 0 and c == 0 and k == 0,
                                    u == 1 and k == 3, skip_group_check=True)
                ins.then_inc(chunk_done, 1)

    def tokens_act(act, name, n, skip=0):
        for i in range(n // 2):
            for u in range(2):
                act.wait_ge(chunk_done, CH[name] + skip + 2 * i + u + 1)
                if u == 1:
                    for c in range(2):
                        nc.scalar.activation(vtok[:, c, i * T:i * T + T], ps[:, 4 + 2 * (i % 2), c * T:c * T + T],
                                             ACT.Copy).then_inc(tile_copied, 1)
                split_hi(act, Step(skip + 2 * i + u), 1, CH[name] + RING)

    def copy_heads(act, ac, st, g, dst):
        src = bank(st.mod(2, 1, g), 0)
        nc.scalar.activation(dst[:, st.lin(2), :], src[0:HD, :], ACT.Copy)
        return nc.scalar.activation(dst[:, st.lin(2, 1), :], src[HD:P, :], ACT.Copy)

    def copy_feat(act, ac, st, g, dst):
        return nc.scalar.activation(dst[:, st.lin(1), :], bank(st.mod(2, 1, g), 0), ACT.Copy)

    def project_act(act, ac, name, n, copy, *args):
        def one(st):
            act.wait_ge(chunk_done, st.lin(1, CH[name] + 1))
            copy(act, ac, st, TC[name], *args).then_inc(tile_copied, 1)
            split_hi(act, st, 1, CH[name] + RING)

        steps(act, None, 0, n, 6, one)

    def qk_pe(pe):
        def swap(st):
            pe.wait_ge(tile_copied, st.lin(1))
            if st.s >= 3:
                pe.wait_ge(rope_done, st.lin(1, -2))
            nc.tensor.matmul(bank(st.mod(2, 1, 1), 2), con_("swap"), copied[:, st.mod(2, 1, 1), :],
                             start=True, stop=True).then_inc(rot_ready, 1)

        def one(st):
            if st.s >= 2:
                pe.wait_ge(tile_copied, st.lin(1, -1))
            up(pe, arrived(pe, st, 1, CH["qkv"]), bank(st.mod(2), 0), hwait=8 if st.s == 0 else None)
            if st.s >= 1:
                swap(st)

        steps(pe, None, 0, 16, 6, one, first=4)
        swap(Step(16))

    def qk_act(act):
        def one(st):
            act.wait_ge(chunk_done, st.lin(1, CH["qkv"] + 1))
            if st.s >= 2:
                act.wait_ge(rope_done, st.lin(1, -1))
            nc.scalar.activation(copied[:, st.mod(2), :], bank(st.mod(2), 0), ACT.Copy).then_inc(tile_copied, 1)
            split_hi(act, st, 1, CH["qkv"] + RING)

        steps(act, None, 0, 16, 6, one, first=4)

    def qk_dve(dve, dc):
        def one(st):
            walk_dve(dve, st, 1, CH["qkv"])
            dve.wait_ge(rot_ready, st.lin(1, 1))
            if st.s >= 1:
                dve.wait_ge(rope_done, st.lin(1))
            dc.mark(nc.vector.tensor_tensor(rope_a, copied[:, st.mod(2), :], con_("cos"), ALU.mult))
            dc.link(nc.vector.tensor_tensor(rope_b, bank(st.mod(2), 2), con_("sin"), ALU.mult))
            nc.vector.tensor_tensor(heads[:, st.lin(2), :], rope_a[0:HD], rope_b[0:HD], ALU.add)
            nc.vector.tensor_tensor(heads[:, st.lin(2, 1), :], rope_a[HD:P], rope_b[HD:P],
                                    ALU.add).then_inc(rope_done, 1)

        steps(dve, dc, 0, 16, 6, one, first=4, per=2)

    def heads_pool(pool, base, n, q):
        def one(st):
            if base + st.s >= 2:
                pool.wait_ge(s_ready, st.lin(1, base - 1))
            nc.gpsimd.tensor_copy(a_q[:, st.mod(2), :], q(st)).then_inc(q_staged, 1)

        steps(pool, None, 0, n, 2, one, first=2)

    def prev(st, n=1):
        return Step(st.s - n, st.stride, st.i)

    def head_stages_pe(pe, base, k, v, q=None):
        def scores(st):
            if q is None:
                pe.wait_ge(q_staged, st.lin(1, base + 1))
            if base + st.s >= 2:
                pe.wait_ge(s_read, st.lin(1, base - 1))
            p = st.mod(2)
            qs = a_q[:, p, :] if q is None else q(st)
            nc.tensor.matmul(ps[:, 4 + p, 0:P], qs[:, 0:P], k(st)[:, 0:P], start=True, stop=True)
            nc.tensor.matmul(ps[:, 4 + p, P:SC3], qs[:, P:T], k(st), start=True, stop=True).then_inc(s_ready, 1)

        def turn(st):
            pe.wait_ge(e_ready, st.lin(1, base + 1))
            if base + st.s >= 2:
                pe.wait_ge(et_copied, st.lin(1, base - 1))
            p = st.mod(2)
            for b in range(3):
                ins = transposed(ps[:, 6 + p, b * P:b * P + P], a_e[:, p, b * P:b * P + P], ident)
            ins.then_inc(et_ready, 1)

        def values(st):
            pe.wait_ge(et_copied, st.lin(1, base + 1))
            if base + st.s >= 2:
                pe.wait_ge(o_read, st.lin(1, base - 1))
            p = st.mod(2)
            nc.tensor.matmul(ps[:, p, 0:HD], a_t[:, p, 0:P], v(st, 0), start=True, stop=True)
            nc.tensor.matmul(ps[:, p, HD:2 * HD], a_t[:, p, P:2 * P], v(st, 0), start=True, stop=False)
            nc.tensor.matmul(ps[:, p, HD:2 * HD], a_t[:, p, 2 * P:SC3], v(st, 1), start=False,
                             stop=True).then_inc(pv_ready, 1)

        return scores, turn, values

    def heads_pe(pe, base, n, k, v, q=None):
        scores, turn, values = head_stages_pe(pe, base, k, v, q)

        def one(st):
            if st.s < n:
                scores(st)
            if 2 <= st.s <= n + 1:
                turn(prev(st, 2))
            if st.s >= 3:
                values(prev(st, 3))

        steps(pe, None, 0, n, 2, one, first=n if q else 4)
        for j in range(n, n + 3):
            one(Step(j))

    def copy_weights(act, base, st):
        act.wait_ge(et_ready, st.lin(1, base + 1))
        if base + st.s >= 2:
            act.wait_ge(pv_ready, st.lin(1, base - 1))
        nc.scalar.activation(a_t[:, st.mod(2), :], ps[:, 6 + st.mod(2), 0:SC3], ACT.Copy).then_inc(et_copied, 1)

    def soft_act(act, base, n, loop=True):
        def one(st):
            p = st.mod(2)
            if st.s < n:
                act.wait_ge(max_ready, st.lin(1, MB[base] + 1))
                if base + st.s >= 2:
                    act.wait_ge(et_ready, st.lin(1, base - 1))
                for c, (lo, hi) in enumerate(((0, P), (P, SC3))):
                    ins = nc.scalar.activation(a_e[:, p, lo:hi], a_s[:, p, lo:hi], ACT.Exp,
                                               bias=a_max[:, p, c:c + 1],
                                               accum_out=a_sum[:, st.lin(1, base), c:c + 1])
                ins.then_inc(e_ready, 1)
            if st.s >= 2:
                copy_weights(act, base, prev(st, 2))

        steps(act, None, 0, n, 2, one, first=2 if loop else n)
        one(Step(n))
        one(Step(n + 1))

    def soft_dve(dve, dc, base, n, bias, out, loop=True):
        def score(st):
            p = st.mod(2)
            dve.wait_ge(s_ready, st.lin(1, base + 1))
            if base + st.s >= 2:
                dve.wait_ge(e_ready, st.lin(1, base - 1))
            nc.vector.scalar_tensor_tensor(a_s[:, p, :], ps[:, 4 + p, 0:SC3], SCALE, bias(st), ALU.mult, ALU.add).then_inc(s_read, 1)
            dve.wait_ge(s_read, st.lin(1, base + 1))
            nc.vector.tensor_reduce(a_max[:, p, 0:1], a_s[:, p, 0:P], AX.X, ALU.max, negate=True)
            nc.vector.tensor_reduce(a_max[:, p, 1:2], a_s[:, p, P:SC3], AX.X, ALU.max,
                                    negate=True).then_inc(max_ready, 1)

        def rows(st):
            dve.wait_ge(pv_ready, st.lin(1, base + 1))
            if base + st.s >= 1:
                dve.wait_ge(o_read, st.lin(1, base))
            dc.link(nc.vector.reciprocal(a_r[:, 0, :], a_sum[:, st.lin(1, base), :]))
            out(st, ps[:, st.mod(2), 0:2 * HD].rearrange("p (c d) -> p c d", c=2)).then_inc(o_read, 1)

        def one(st):
            if st.s < n:
                score(st)
            if st.s >= 3:
                rows(prev(st, 3))

        steps(dve, dc, 0, n, 2, one, first=4 if loop else n, per=1)
        for j in range(n, n + 3):
            one(Step(j))

    def stick_pe(pe, base, n, q, k, v):
        scores, turn, values = head_stages_pe(pe, base, k, v, q)
        for j in range(n):
            scores(Step(j))
        turn(Step(0))

        def one(st):
            turn(st)
            values(prev(st))

        steps(pe, None, 1, n, 2, one, first=2)
        values(Step(n - 1))

    def stick_act(act, ac, base, n):
        def soft(st):
            l = st_l[:, st.lin(1), :]
            act.wait_ge(s_read, st.lin(1, base + 1))
            ac.link(nc.scalar.activation(l, st_s[:, st.lin(1), :], ACT.Abs))
            ac.mark(nc.scalar.activation(l, l, ACT.Exp, scale=-1.0))

        def log(st):
            l = st_l[:, st.lin(1), :]
            nc.scalar.activation(l, l, ACT.Ln, bias=1.0).then_inc(soft_ready, 1)

        def weight(st):
            act.wait_ge(logit_ready, st.lin(1, 1))
            if base + st.s >= 2:
                act.wait_ge(et_ready, st.lin(1, base - 1))
            nc.scalar.activation(a_e[:, st.mod(2), :], st_l[:, st.lin(1), :], ACT.Exp).then_inc(e_ready, 1)

        def one(st):
            weight(st)
            copy_weights(act, base, prev(st))

        for j in range(n):
            soft(Step(j))
        ac.need()
        for j in range(n):
            log(Step(j))
        weight(Step(0))
        for j in range(1, n):
            one(Step(j))
        copy_weights(act, base, Step(n - 1))

    def stick_dve(dve, dc, base, n, out):
        def mask(st):
            dve.wait_ge(s_ready, st.lin(1, base + 1))
            nc.vector.scalar_tensor_tensor(st_s[:, st.lin(1), :], ps[:, 4 + st.mod(2), 0:SC3], SCALE, con_("strict"),
                                           ALU.mult, ALU.add).then_inc(s_read, 1)

        def logit(st):
            dve.wait_ge(soft_ready, st.lin(1, 1))
            if st.s >= 1:
                dve.wait_ge(logit_ready, st.lin(1))
            l = st_l[:, st.lin(1), :]
            dc.link(nc.vector.scalar_tensor_tensor(l, st_s[:, st.lin(1), :], 0.0, l, ALU.max, ALU.add))
            for lo, hi in ((0, P), (P, SC3)):
                rev = slice(hi - 1, lo - 1 if lo else None, -1)
                dc.mark(nc.vector.tensor_tensor_scan(a_c[:, rev], ones[:, 0:hi - lo], l[:, rev], 0.0,
                                                     ALU.mult, ALU.add))
            dc.need()
            nc.vector.tensor_tensor(l, st_s[:, st.lin(1), :], a_c, ALU.subtract).then_inc(logit_ready, 1)

        def rows(st):
            dve.wait_ge(pv_ready, st.lin(1, base + 1))
            out(st, ps[:, st.mod(2), 0:2 * HD].rearrange("p (c d) -> p c d", c=2)).then_inc(o_read, 1)

        def one(st):
            logit(st)
            rows(Step(st.s - 2, st.stride, st.i))

        steps(dve, None, 0, n, 2, mask)
        dve.wait_ge(s_read, base + n)
        for j in range(2):
            logit(Step(j))
        for j in range(2, n):
            one(Step(j))
        for j in (n - 2, n - 1):
            rows(Step(j))

    def head_cols(st, o=0):
        return otok[:, :, bass.ds(st.lin(HD, o), HD)]

    def rows_soft(st, o):
        dst = head_cols(st)
        nc.vector.tensor_scalar(dst[:, 0, :], o[:, 0, :], a_r[:, 0, 0:1], None, ALU.mult)
        return nc.vector.tensor_scalar(dst[:, 1, :], o[:, 1, :], a_r[:, 0, 1:2], None, ALU.mult)

    def turn_out_pe(pe, base):
        for g in range(4):
            for b in range(4):
                j, c = 2 * g + b // 2, b % 2
                ins = transposed(ps[:, 4 + g, b * P:b * P + P], otok[:, c, j * P:j * P + P], ident)
            ins.then_inc(ot_ready, 1)

    def turn_out_act(act, base):
        for g in range(4):
            act.wait_ge(ot_ready, base + g + 1)
            nc.scalar.activation(oT_hi[:, 2 * g:2 * g + 2, :], ps[:, 4 + g, :].rearrange("p (a t) -> p a t", a=2),
                                 ACT.Copy).then_inc(ot_copied, 1)

    def turn_out_dve(dve, base):
        for g in range(4):
            dve.wait_ge(ot_copied, base + g + 1)
            nc.vector.tensor_tensor(oT_lo[:, 2 * g:2 * g + 2, :], ps[:, 4 + g, :].rearrange("p (a t) -> p a t", a=2),
                                    oT_hi[:, 2 * g:2 * g + 2, :].bitcast(F32), ALU.subtract).then_inc(ot_split, 1)

    def wo_pe(pe):
        for j in range(KD):
            pe.wait_ge(ot_split, j // 2 + 1)
            down(pe, arrived(pe, Step(j), 1, CH["wo"]), (oT_hi[:, j, :], oT_lo[:, j, :]), j == 0, j == KD - 1)

    def gates_pe(pe):
        pe.wait_ge(s_small, 16 * 1)
        pe.wait_ge(h_tile, 2 * 20)
        for c in range(2):
            for k in range(KD):
                ins = nc.tensor.matmul(ps[:, 0, c * 24:c * 24 + 24], h_f[:, k, c * P:c * P + P], wg_s[:, k, :],
                                       start=(k == 0), stop=(k == KD - 1))
        ins.then_inc(gate_ready, 1)

    def gates_act(act):
        act.wait_ge(gate_ready, 1)
        nc.scalar.activation(gates, ps[:, 0, 0:48].rearrange("p (c g) -> p c g", c=2), ACT.Sigmoid)\
            .then_inc(gate_copied, 1)

    def feat_pe(pe, lo, hi):
        for n in range(lo, hi):
            pe.wait_ge(tile_copied, TC["p_feat"] + n - 1)
            up(pe, arrived(pe, Step(n), 1, CH["p_feat"]), ps[:, n % 2, 0:T])

    def feat_act(act, lo, hi):
        for n in range(lo, hi):
            act.wait_ge(chunk_done, CH["p_feat"] + n + 1)
            nc.scalar.activation(hfeat[:, n, :], ps[:, n % 2, 0:T], ACT.Copy).then_inc(tile_copied, 1)
            split_hi(act, Step(n), 1, CH["p_feat"] + RING)

    def feat_dve(dve, lo, hi):
        for n in range(lo, hi):
            walk_dve(dve, Step(n), 1, CH["p_feat"])

    def cmp_dve(dve, dc):
        dve.wait_ge(s_cmp, 16 * 4)
        dve.wait_ge(tile_copied, TC["p_tok"])
        dc.mark(nc.vector.memset(blk_k, 0.0))
        dc.link(nc.vector.memset(blk_v, 0.0))
        for dst, hd in ((blk_k, 24), (blk_v, 26)):
            src = heads[:, hd:hd + 2, :].rearrange("p g (c l) -> p l g c", l=16)
            for half in range(2):
                ins = nc.vector.tensor_tensor(
                    dst[half * HD:half * HD + HD, :, :, 0:15], src[:, :, :, half:half + 15],
                    pe_s[:, 16 * half:16 * half + 16].unsqueeze(2).unsqueeze(3).broadcast_to([HD, 16, 2, 15]), ALU.add)
        ins.then_inc(cmp_dve_s, 1)
        feat_dve(dve, 0, 4)
        dve.wait_ge(cmp_pe_s, 2)
        nc.vector.scalar_tensor_tensor(ce, ps[:, 2, 0:256], SCALE, con_("cmpbias"), ALU.mult, ALU.add)\
            .then_inc(cmp_dve_s, 1)
        dve.wait_ge(cmp_dve_s, 2)
        ce3 = ce.rearrange("p (r c) -> p r c", c=CMP)
        dc.link(nc.vector.tensor_reduce(cm, ce3, AX.X, ALU.max))
        nc.vector.tensor_tensor(ce3, ce3, cm.unsqueeze(2).broadcast_to([P, 16, CMP]), ALU.subtract)\
            .then_inc(cmp_dve_s, 1)
        feat_dve(dve, 4, 7)
        dve.wait_ge(cmp_act_s, 2)
        dve.wait_ge(gate_copied, 1)
        dc.link(nc.vector.tensor_reduce(cm, ce3, AX.X, ALU.add))
        dc.link(nc.vector.reciprocal(cm, cm))
        g = gates.rearrange("p c (h b) -> p h c b", b=3)[:, :, :, 0]
        cm2 = cm.rearrange("p (h c) -> p h c", c=2)
        dc.link(nc.vector.tensor_tensor(cm2, cm2, g, ALU.mult))
        dc.link(nc.vector.tensor_tensor(cm2, cm2, con_("rowok").unsqueeze(1).broadcast_to([P, 8, 2]), ALU.mult))
        nc.vector.tensor_tensor(ce3, ce3, cm.unsqueeze(2).broadcast_to([P, 16, CMP]), ALU.mult)\
            .then_inc(cmp_dve_s, 1)
        feat_dve(dve, 7, 11)
        dve.wait_ge(cmp_pe_s, 4)
        for b in range(2):
            src = ps[:, 2 + b, :].rearrange("p (h c d) -> p h c d", h=4, c=2)
            for c in range(2):
                ins = nc.vector.tensor_copy(
                    otok[:, c, 512 + b * 256:512 + b * 256 + 256].rearrange("p (h d) -> p h d", h=4), src[:, :, c, :])
        ins.then_inc(cmp_dve_s, 1)
        dve.wait_ge(cmp_dve_s, 5)
        feat_dve(dve, 11, 12)
        dve.wait_ge(hg_act_s, 1)
        dc.link(nc.vector.scalar_tensor_tensor(h_lf, hf, 0.0, h_tmp, ALU.min, ALU.subtract))
        nc.vector.tensor_tensor(h_tmp, h_lf, hf, ALU.subtract).then_inc(hg_dve_s, 1)
        feat_dve(dve, 12, 16)

    def cmp_pe(pe):
        pe.wait_ge(gate_copied, 1)
        feat_pe(pe, 0, 2)
        pe.wait_ge(s_cmp, 16 * 4)
        pe.wait_ge(cmp_dve_s, 1)
        for l in range(16):
            nc.tensor.matmul(ps[0:HD, 2, 0:32], wk_s[:, l, :], blk_k[:, l, :, :].rearrange("p g c -> p (g c)"),
                             start=(l == 0), stop=(l == 15))
        for l in range(16):
            ins = nc.tensor.matmul(ps[0:HD, 3, 0:HD], blk_v[:, l, :, :].rearrange("p g c -> p (g c)"), wv_s[:, l, :],
                                   start=(l == 0), stop=(l == 15))
        ins.then_inc(cmp_pe_s, 1)
        feat_pe(pe, 2, 4)
        pe.wait_ge(cmp_act_s, 1)
        for hd in range(8):
            for c in range(2):
                r = 2 * hd + c
                ins = nc.tensor.matmul(ps[:, 2, r * CMP:r * CMP + CMP], heads[:, 16 + hd, c * P:c * P + P],
                                       kc[:, hd // 4, :], start=True, stop=True)
        ins.then_inc(cmp_pe_s, 1)
        feat_pe(pe, 4, 9)
        pe.wait_ge(cmp_dve_s, 4)
        for r in range(16):
            ins = transposed(ps[0:CMP, 4 + r // 4, (r % 4) * P:(r % 4) * P + P],
                                      ce[:, r * CMP:r * CMP + CMP], ident)
        ins.then_inc(cmp_pe_s, 1)
        feat_pe(pe, 9, 11)
        pe.wait_ge(cmp_act_s, 3)
        for r in range(16):
            ins = nc.tensor.matmul(ps[:, 2 + r // 8, (r % 8) * HD:(r % 8) * HD + HD], ceT[:, r, :], vc[:, r // 8, :],
                                   start=True, stop=True)
        ins.then_inc(cmp_pe_s, 1)
        feat_pe(pe, 11, 16)

    def cmp_act(act, ac):
        feat_act(act, 0, 2)
        act.wait_ge(cmp_pe_s, 1)
        nc.scalar.activation(kc.rearrange("p g c -> p (g c)"), ps[0:HD, 2, 0:32], ACT.Copy)
        nc.scalar.activation(vc[:, 0, :], ps[0:CMP, 3, 0:HD], ACT.Copy)
        nc.scalar.activation(vc[:, 1, :], ps[32:32 + CMP, 3, 0:HD], ACT.Copy).then_inc(cmp_act_s, 1)
        feat_act(act, 2, 6)
        act.wait_ge(cmp_dve_s, 3)
        nc.scalar.activation(ce, ce, ACT.Exp).then_inc(cmp_act_s, 1)
        feat_act(act, 6, 10)
        act.wait_ge(cmp_pe_s, 3)
        nc.scalar.activation(ceT.rearrange("p r t -> p (r t)"), ps[0:CMP, 4:8, :].rearrange("p b t -> p (b t)"),
                             ACT.Copy).then_inc(cmp_act_s, 1)
        feat_act(act, 10, 12)
        act.wait_ge(tile_copied, TC["p_feat"] + 12)
        ac.link(nc.scalar.activation(h_tmp, hf, ACT.Abs))
        ac.link(nc.scalar.activation(h_tmp, h_tmp, ACT.Exp, scale=-1.0))
        nc.scalar.activation(h_tmp, h_tmp, ACT.Ln, bias=1.0).then_inc(hg_act_s, 1)
        nc.scalar.activation(hq, hq, ACT.Silu)
        feat_act(act, 12, 16)
        act.wait_ge(hg_dve_s, 1)
        nc.scalar.activation(h_k, h_tmp, ACT.Exp).then_inc(hg_act_s, 1)
        act.wait_ge(hg_act_s, 2)

    def rows_stick(st, o):
        return nc.vector.tensor_copy(head_cols(st), o)

    def rows_nsa(dc):
        def out(st, o):
            g0, branch, _, _ = NSA[st.s // 4]
            h = g0 + st.s % 4
            gh = gates.rearrange("p c (h b) -> p b h c", b=3)[:, branch, h, :]
            dst = otok[:, :, 512 + h * HD:512 + h * HD + HD]
            dc.link(nc.vector.tensor_tensor(a_r[:, 0, :], a_r[:, 0, :], gh, ALU.mult))
            nc.vector.scalar_tensor_tensor(dst[:, 0, :], o[:, 0, :], a_r[:, 0, 0:1], dst[:, 0, :], ALU.mult, ALU.add)
            return nc.vector.scalar_tensor_tensor(dst[:, 1, :], o[:, 1, :], a_r[:, 0, 1:2], dst[:, 1, :],
                                                  ALU.mult, ALU.add)
        return out

    NSA = [(0, 2, 30, 640), (0, 1, 28, 512), (4, 2, 31, 704), (4, 1, 29, 576)]

    def halves(v, lv, a=None):
        v = v.rearrange("p a t -> p (a t)") if a is None else v[:, a, :]
        v = v.rearrange("p (m s u) -> p m s u", s=2, u=LEVELS[lv])
        return v[:, :, 0, :], v[:, :, 1, :]

    def compact(v, lv):
        return v.rearrange("p (m u) -> p m u", u=LEVELS[lv])

    o_acc = ps[:, 0:2, :].rearrange("p a t -> p (a t)").rearrange("p (a t) -> p a t", a=4)

    def hg_act(act):
        for lv, L in enumerate(LEVELS):
            p = lv % 2
            if lv == 0:
                act.wait_ge(r_zeroed, 1)
            else:
                act.wait_ge(lv_widened, lv)
            if lv >= 2:
                act.wait_ge(lv_scored, lv - 1)
            nc.scalar.activation(compact(lv_q[:, p, :], lv), halves(h_c, lv)[1], ACT.Exp)
            nc.scalar.activation(compact(lv_k[:, p, :], lv), halves(h_r, lv)[0], ACT.Exp).then_inc(lv_exp, 1)
            act.wait_ge(lv_turned, lv + 1)
            if lv >= 2:
                act.wait_ge(lv_added, lv - 1)
            nc.scalar.activation(lv_i[:, p, :], ps[:, 4 + p, :], ACT.Copy).then_inc(lv_copied, 1)
        act.wait_ge(tile_copied, TC["p_feat"] + 16)
        nc.scalar.activation(hg, hg, ACT.Silu).then_inc(hg_act_s, 1)
        act.wait_ge(lv_added, len(LEVELS))
        nc.scalar.activation(h_tmp, o_acc, ACT.Square).then_inc(hg_act_s, 1)
        act.wait_ge(hg_dve_s, 4)
        nc.scalar.activation(h_tmp, h_tmp, ACT.Sqrt).then_inc(hg_act_s, 1)

    def hg_pool(pool):
        pool.wait_ge(o_read, HB["end"])
        nc.gpsimd.memset(h_r, 0.0).then_inc(r_zeroed, 1)
        for lv in range(len(LEVELS)):
            if lv >= 2:
                pool.wait_ge(lv_turned, lv - 1)
            nc.gpsimd.tensor_copy(compact(lv_v[:, lv % 2, :], lv), halves(hi, lv)[0]).then_inc(lv_values, 1)

    def hg_dve(dve, dc):
        def widen(lv):
            dve.wait_ge(lv_exp, lv)
            for_c, for_r = halves(h_c, lv - 1), halves(h_r, lv - 1)
            L = LEVELS[lv - 1]
            shape = [P, 4 * P // L, L]
            dc.link(nc.vector.tensor_tensor(for_r[0], for_r[0], for_c[1][:, :, L - 1:L].broadcast_to(shape), ALU.add))
            nc.vector.tensor_tensor(for_c[1], for_c[1], for_c[0][:, :, L - 1:L].broadcast_to(shape), ALU.add)\
                .then_inc(lv_widened, 1)
            dve.wait_ge(lv_widened, lv)

        def decay(lv):
            p = lv % 2
            dve.wait_ge(lv_exp, lv + 1)
            q, k = compact(lv_q[:, p, :], lv), compact(lv_k[:, p, :], lv)
            nc.vector.tensor_tensor(q, q, halves(hq, lv)[1], ALU.mult)
            nc.vector.tensor_tensor(k, k, halves(h_k, lv)[0], ALU.mult).then_inc(lv_ready, 1)

        def mask(lv):
            p = lv % 2
            dve.wait_ge(lv_scored, lv + 1)
            if lv >= 2:
                dve.wait_ge(lv_added, lv - 1)
            src = ps[:, 2 + p, :].rearrange("p (a t) -> p a t", a=4)
            if lv < len(LEVELS) - 1:
                m = con_("pairs")[:, lv * P - P:lv * P] if lv else ident
                m = m.unsqueeze(1).broadcast_to([P, 4, P])
                ins = nc.vector.tensor_tensor(lv_a[:, p], src, m, ALU.mult)
            else:
                ins = nc.vector.tensor_copy(lv_a[:, p], src)
            ins.then_inc(lv_masked, 1)

        dve.wait_ge(hg_dve_s, 1)
        dve.wait_ge(hg_act_s, 2)
        nc.vector.tensor_tensor(h_o, hq, h_k, ALU.mult).then_inc(hg_dve_s, 1)
        dve.wait_ge(hg_pe_s, 1)
        nc.vector.tensor_tensor(h_o.rearrange("p a t -> p (a t)"), ps[:, 6:8, :].rearrange("p a t -> p (a t)"),
                                hi.rearrange("p a t -> p (a t)"), ALU.mult).then_inc(hg_dve_s, 1)
        for lv in range(len(LEVELS) + 1):
            if lv + 1 < len(LEVELS):
                widen(lv + 1)
            if lv < len(LEVELS):
                decay(lv)
            if lv >= 1:
                mask(lv - 1)
        tmp2 = h_tmp.rearrange("p a t -> p (a t)")
        dve.wait_ge(hg_pe_s, 2)
        dc.link(nc.vector.tensor_scalar(tmp2, ps[:, 6:8, :].rearrange("p a t -> p (a t)"), 1.0 / P, EPS,
                                        ALU.mult, ALU.add))
        nc.vector.reciprocal(tmp2, tmp2).then_inc(hg_dve_s, 1)
        dve.wait_ge(hg_act_s, 5)
        dc.link(nc.vector.tensor_tensor(h_o, o_acc, h_tmp, ALU.mult))
        for a in range(4):
            dc.mark(nc.vector.scalar_tensor_tensor(h_o[:, a, :], h_o[:, a, :], par_("hnorm", a), hg[:, a, :],
                                                   ALU.mult, ALU.mult))
        dc.need()
        dc.link(nc.vector.tensor_copy(oT_hi[:, 8:12, :], h_o))
        nc.vector.tensor_tensor(oT_lo[:, 8:12, :], h_o, oT_hi[:, 8:12, :].bitcast(F32), ALU.subtract)\
            .then_inc(hg_dve_s, 1)

    def hg_pe(pe):
        pe.wait_ge(o_read, HB["end"])
        pe.wait_ge(ot_split, 8)
        pe.wait_ge(hg_dve_s, 2)
        o2 = h_o.rearrange("p a t -> p (a t)")
        for b in range(2):
            ins = nc.tensor.matmul(ps[:, 6 + b, :], ones[:, 0:P], o2[:, b * 512:b * 512 + 512], start=True, stop=True)
        ins.then_inc(hg_pe_s, 1)

        def added(lv):
            p, L = lv % 2, LEVELS[lv]
            pe.wait_ge(lv_masked, lv + 1)
            pe.wait_ge(lv_copied, lv + 1)
            for a in range(4):
                ins = nc.tensor.matmul(halves(o_acc, lv, a)[1], lv_i[:, p, a * P:a * P + P],
                                       compact(lv_a[:, p, a, :], lv), start=False, stop=lv == len(LEVELS) - 1,
                                       skip_group_check=True)
            ins.then_inc(lv_added, 1)

        for lv in range(len(LEVELS)):
            p = lv % 2
            if lv >= 2:
                pe.wait_ge(lv_copied, lv - 1)
            pe.wait_ge(lv_values, lv + 1)
            for a in range(4):
                ins = transposed(ps[:, 4 + p, a * P:a * P + P], lv_v[:, p, a * P:a * P + P], ident)
            ins.then_inc(lv_turned, 1)
            pe.wait_ge(lv_ready, lv + 1)
            if lv >= 2:
                pe.wait_ge(lv_masked, lv - 1)
            for a in range(4):
                ins = nc.tensor.matmul(ps[:, 2 + p, a * P:a * P + P], lv_k[:, p, a * P:a * P + P],
                                       lv_q[:, p, a * P:a * P + P], start=True, stop=True)
            ins.then_inc(lv_scored, 1)
            if lv == 0:
                pe.wait_ge(hg_dve_s, 3)
                for b in range(2):
                    nc.tensor.matmul(ps[:, b, :], ident, o2[:, b * 512:b * 512 + 512], start=True, stop=False,
                                     skip_group_check=True)
            else:
                added(lv - 1)
        added(len(LEVELS) - 1)
        pe.wait_ge(hg_act_s, 4)
        tmp2 = h_tmp.rearrange("p a t -> p (a t)")
        for b in range(2):
            ins = nc.tensor.matmul(ps[:, 6 + b, :], ones[:, 0:P], tmp2[:, b * 512:b * 512 + 512], start=True, stop=True)
        ins.then_inc(hg_pe_s, 1)

    def merge_at(j, k):
        return 6, CH["merge"] + k - (1 if j > 0 else 0)

    def merge_pe(pe):
        n = KD

        def one(st):
            if st.s < n:
                def gate(i, k):
                    if st.s >= 1:
                        pe.wait_ge(branch_taken, st.lin(3, i - 2))
                    up(pe, arrived(pe, st, *merge_at(st.s, k)), ps[:, 4 + i, 0:T])

                gate(0, 0)
                gate(1, 1)
                r = arrived(pe, st, *merge_at(st.s, 2))
                up(pe, r, ps[:, 4, T:2 * T], 0, 4, (oT_hi, oT_lo), 0, inc=False)
                up(pe, r, ps[:, 5, T:2 * T], 4, 4, (oT_hi, oT_lo), 4)
                if st.s == 0:
                    pe.wait_ge(hg_dve_s, 5)
                gate(2, 3)
                up(pe, arrived(pe, st, *merge_at(st.s, 4)), ps[:, 6, T:2 * T], 0, 4, (oT_hi, oT_lo), 8)
            if st.s >= 1:
                pe.wait_ge(z_ready, st.lin(1, ZB["merge"]))
                down(pe, arrived(pe, st, 6, CH["merge"] + (4 if st.s < n else -1)), (z_hi, z_lo),
                     st.s == 1, st.s == n)

        steps(pe, None, 0, n, 1, one, first=2)
        one(Step(n))

    def merge_act(act):
        def one(st):
            for k in (0, 1, 2):
                walk_act(act, st, *merge_at(st.s, k))
            for i in range(3):
                if i == 2:
                    walk_act(act, st, *merge_at(st.s, 3))
                    walk_act(act, st, *merge_at(st.s, 4))
                if st.s >= 1:
                    act.wait_ge(branch_taken, st.lin(3, i - 2))
                nc.scalar.activation(sg[:, i, :], ps[:, 4 + i, 0:T], ACT.Sigmoid).then_inc(sg_ready, 1)
            if st.s >= 1:
                walk_act(act, st, *down_at("merge", 6, KD, st.s))

        steps(act, None, 0, KD, 1, one, first=2)
        walk_act(act, Step(KD), *down_at("merge", 6, KD, KD))

    def merge_dve(dve, dc):
        def one(st):
            if st.s >= 1:
                dve.wait_ge(z_ready, st.lin(1, ZB["merge"]))
            for k in (0, 1, 2):
                walk_dve(dve, st, *merge_at(st.s, k))
            for i in range(3):
                if i == 2:
                    walk_dve(dve, st, *merge_at(st.s, 3))
                    walk_dve(dve, st, *merge_at(st.s, 4))
                    dc.link(nc.vector.tensor_tensor(conv_g, conv_g, conv_u, ALU.add))
                dve.wait_ge(sg_ready, st.lin(3, i + 1))
                nc.vector.tensor_tensor(conv_u if i else conv_g, sg[:, i, :], ps[:, 4 + i, T:2 * T], ALU.mult)\
                    .then_inc(branch_taken, 1)
                dve.wait_ge(branch_taken, st.lin(3, i + 1))
            nc.vector.tensor_tensor(z_f, conv_g, conv_u, ALU.add).then_inc(z_full, 1)
            split_z(dve, dc, st, "merge", 6, KD)

        steps(dve, dc, 0, KD, 1, one, first=2, per=2)
        last_down_dve(dve, "merge", 6, KD)

    def peer_turn_pe(pe):
        pe.wait_ge(tk_dve, 2)
        for i in range(3):
            for c in range(2):
                ins = transposed(ps[:, i, c * P:c * P + P], t_key[:, i, c, :], ident)
        ins.then_inc(tk_pe, 1)

    def peer_scores_pe(pe):
        pe.wait_ge(tile_copied, TC["pq"] + KD)
        pe.wait_ge(s_keys, 32)
        for c in range(2):
            for a in range(PH):
                ins = nc.tensor.matmul(ps[:, 4 * c + a // 2, (a % 2) * T:(a % 2) * T + T], t_q[:, a, c * P:c * P + P],
                                       keys_s, start=True, stop=True)
                if a % 2:
                    ins.then_inc(tk_pe, 1)

    def peer_top_act(act):
        for b in range(8):
            act.wait_ge(tk_pe, b + 1)
            nc.scalar.activation(t_s[:, 4 * b:4 * b + 4, :], ps[:, b, :].rearrange("p (r k) -> p r k", r=4),
                                 ACT.Copy).then_inc(tk_act, 1)

    def top16(dc, rows, src, best, where, us):
        for lo in range(0, rows, 8):
            rs = range(lo, min(lo + 8, rows))
            for at0 in (0, 8):
                for r in rs:
                    dc.mark(nc.vector.max(best[:, r, at0:at0 + 8], src[:, r, :]))
                    yield us
                dc.need()
                for r in rs:
                    dc.mark(nc.vector.max_index(where[:, r, at0:at0 + 8], best[:, r, at0:at0 + 8], src[:, r, :]))
                    yield us
                dc.need()
                for r in rs if at0 == 0 else ():
                    dc.mark(nc.vector.match_replace(src[:, r, :], best[:, r, 0:8], src[:, r, :], -3e38))
                    yield us
                dc.need()

    def peer_top(dve, dc):
        dve.wait_ge(tk_act, 8)
        yield from top16(dc, 32, t_s, t_b, t_i, 0.22)
        dc.link(nc.vector.tensor_copy(t_if, t_i))
        yield 0.6
        for c in range(2):
            b = t_b.rearrange("p (c a h) k -> p c a h k", c=2, h=2)[:, c]
            dc.mark(nc.vector.tensor_tensor(
                t_c[:, 8 * c:8 * c + 8, :].rearrange("p a (i j) -> p a i j", i=TOPK),
                b[:, :, 0, :].unsqueeze(3).broadcast_to([P, PH, TOPK, TOPK]),
                b[:, :, 1, :].unsqueeze(2).broadcast_to([P, PH, TOPK, TOPK]), ALU.add))
            yield 2.2
        dc.need()
        yield from top16(dc, 16, t_c, t_g, t_w, 0.36)
        dc.mark(nc.vector.tensor_scalar(t_wi, t_w, 4, None, ALU.logical_shift_right))
        dc.link(nc.vector.tensor_scalar(t_wj, t_w, 15, None, ALU.bitwise_and))
        dc.mark(nc.vector.tensor_copy(t_wf[:, 0], t_wi))
        dc.mark(nc.vector.tensor_copy(t_wf[:, 1], t_wj))
        dc.mark(nc.vector.tensor_copy(t_m, t_g[:, :, 0:1]))
        dc.need()
        nc.vector.tensor_tensor(t_g, t_g, t_m.broadcast_to([P, 16, TOPK]), ALU.subtract).then_inc(tk_dve, 1)
        yield 2.0
        for half in range(2):
            for c in range(2):
                w = t_wf[:, half, 8 * c:8 * c + 8, :].rearrange("p a k -> p (a k)")
                dc.link(nc.vector.tensor_tensor(t_1, con_("iota16").unsqueeze(1).broadcast_to([P, P, TOPK]),
                                                w.unsqueeze(2).broadcast_to([P, P, TOPK]), ALU.is_equal))
                yield 2.2
                t14 = t_1.rearrange("p (a k) i -> p a k i", a=PH)
                f = t_if.rearrange("p (c a h) k -> p c h a k", c=2, h=2)[:, c, half]
                dc.link(nc.vector.tensor_tensor(t14, t14, f.unsqueeze(2).broadcast_to([P, PH, TOPK, TOPK]), ALU.mult))
                yield 2.2
                dc.link(nc.vector.tensor_reduce(t_key[:, half, c, :], t_1, AX.X, ALU.add))
                yield 2.2
        dve.wait_ge(tk_act, 9)
        dc.link(nc.vector.tensor_reduce(t_m, t_g, AX.X, ALU.add))
        dc.link(nc.vector.reciprocal(t_m, t_m))
        nc.vector.tensor_tensor(t_key[:, 2, :, :].rearrange("p c (a k) -> p (c a) k", a=PH), t_g,
                                t_m.broadcast_to([P, 16, TOPK]), ALU.mult).then_inc(tk_dve, 1)
        yield 1.0

    def emap_of(half, st):
        v = emap[:, half * HALF:half * HALF + HALF, bass.ds(st.lin(GT), GT)]
        return v.rearrange("p a t -> p t a")

    NB = T // GT

    def hots(dve, dc, half, st):
        if half or st.s >= 1:
            dve.wait_ge(gm_done, st.lin(1, NB * half))
        tok = bass.ds(st.lin(GT), GT)
        sa, sb_ = [P, GT, HALF], [P, GT, P]
        iota = iota_b
        dc.mark(nc.vector.tensor_tensor(hot_a[:, 2], iota[:, half * HALF:half * HALF + HALF].unsqueeze(1).broadcast_to(sa),
                                        idx[:, 0, tok].unsqueeze(2).broadcast_to(sa), ALU.is_equal))
        nc.vector.tensor_tensor(hot_b, iota.unsqueeze(1).broadcast_to(sb_),
                                idx[:, 1, tok].unsqueeze(2).broadcast_to(sb_), ALU.is_equal)
        dc.need()
        for i in range(3):
            ins = nc.vector.tensor_tensor(hot_a[:, i], hot_a[:, 2],
                                          gate_part[:, i, tok].unsqueeze(2).broadcast_to(sa), ALU.mult)
            if i == 1:
                dc.link(ins)
        ins.then_inc(hot_ready, 1)

    def take_gates(dve, half, st):
        dve.wait_ge(gm_done, st.lin(1, NB * half + 1))
        v = emap_of(half, st)
        nc.vector.tensor_tensor(v, v, ps[:, 6 + st.mod(2), :].rearrange("p (t a) -> p t a", t=GT), ALU.mult)\
            .then_inc(gm_taken, 1)

    def gates_of_batch_pe(pe, half, st):
        pe.wait_ge(hot_ready, st.lin(1, NB * half + 1))
        if half or st.s >= 2:
            pe.wait_ge(gm_taken, st.lin(1, NB * half - 1))
        for q in range(GT):
            out = ps[:, 6 + st.mod(2), q * HALF:q * HALF + HALF]
            for i in range(3):
                ins = nc.tensor.matmul(out, hot_b[:, q, :], hot_a[:, i, q, :], start=i == 0, stop=i == 2)
        ins.then_inc(gm_done, 1)

    def expert_up_pe(pe, st, a, b):
        if a * st.s + b >= 2:
            pe.wait_ge(gelu_done, st.lin(a, b - 1))
        up(pe, arrived(pe, st, a, b + UP0), ps[:, 4 + st.mod(2, a, b), 0:T])

    def expert_down_pe(pe, st, a, b):
        pe.wait_ge(z_ready, st.lin(a, b + ZB["peer"] + 1))
        n = a * st.s + b
        down(pe, arrived(pe, st, a, b + DOWN0), ez[st.mod(2, a, b)], n == 0, n == NKEY - 1)

    def peer_pe(pe):
        pe.wait_ge(tk_act, 8)
        steps(pe, None, 0, HALF, 6, lambda st: expert_up_pe(pe, st, 1, 0), first=2)
        peer_turn_pe(pe)

        def second(st):
            for u in range(2):
                expert_up_pe(pe, st, 2, HALF + u)
            gates_of_batch_pe(pe, 0, st)

        steps(pe, None, 0, NB, 6, second, first=2)

        def third(st):
            for u in range(2):
                expert_down_pe(pe, st, 2, u)
            gates_of_batch_pe(pe, 1, st)

        steps(pe, None, 0, NB, 6, third, first=2)
        steps(pe, None, HALF, NKEY - 1, 6, lambda st: expert_down_pe(pe, st, 1, 0))
        expert_down_pe(pe, Step(NKEY - 1), 1, 0)

    def peer_act(act):
        def one(st):
            act.wait_ge(chunk_done, st.lin(1, UP0 + 1))
            nc.scalar.activation(emap[:, st.lin(1), :], ps[:, 4 + st.mod(2), 0:T], ACT.Gelu).then_inc(gelu_done, 1)
            split_hi(act, st, 1, UP0 + RING)

        steps(act, None, 0, 48, 6, one)
        act.wait_ge(tk_dve, 1)
        nc.scalar.activation(t_g, t_g, ACT.Exp).then_inc(tk_act, 1)
        steps(act, None, 48, HALF, 6, one)
        act.wait_ge(tk_pe, 9)
        nc.scalar.activation(iota_b, con_("iota"), ACT.Copy)
        nc.scalar.activation(idx, ps[:, 0:2, 0:T], ACT.Copy)
        nc.scalar.activation(gate_part[:, 0], ps[:, 2, 0:T], ACT.Copy).then_inc(tk_act, 1)
        steps(act, None, HALF, NKEY, 6, one)

        def z(st, gates=None):
            if st.s >= 2:
                walk_act(act, st, 1, DOWN0 - 2)
            if gates is not None:
                act.wait_ge(gm_taken, gates)
            nc.scalar.activation(ez[st.mod(2)][0], emap[:, st.lin(1), :], ACT.Copy).then_inc(ez_hi, 1)

        z(Step(0), NB)
        steps(act, None, 1, HALF, 6, z, first=2)
        z(Step(HALF), 2 * NB)
        steps(act, None, HALF + 1, NKEY - RING, 6, z)
        for n in range(NKEY - RING, NKEY):
            z(Step(n))
        for n in (NKEY, NKEY + 1):
            walk_act(act, Step(n), 1, DOWN0 - 2)

    def peer_dve(dve, dc):
        done, us = 0, 0.0
        for price in peer_top(dve, dc):
            us += price
            while done < HALF and us >= 1.8 * (done + 1):
                walk_dve(dve, Step(done), 1, UP0)
                done += 1
        range_dve(dve, UP0 + done, UP0 + HALF)
        dve.wait_ge(tk_act, 10)
        dc.link(nc.vector.tensor_tensor(gate_left[:, 0], ps[:, 2, 0:T], gate_part[:, 0], ALU.subtract))
        dc.link(nc.vector.tensor_copy(gate_part[:, 1], gate_left[:, 0]))
        dc.link(nc.vector.tensor_tensor(gate_part[:, 2], gate_left[:, 0], gate_part[:, 1], ALU.subtract))

        def second(st):
            hots(dve, dc, 0, st)
            for u in range(2):
                walk_dve(dve, st, 2, UP0 + HALF + u - 1) if st.s or u else None
            if st.s >= 1:
                take_gates(dve, 0, prev(st))

        steps(dve, dc, 0, NB, 6, second, first=1, per=2)
        walk_dve(dve, Step(NKEY - 1), 1, UP0)
        take_gates(dve, 0, Step(NB - 1))

        def z_rest(st, a, b):
            p = st.mod(2, a, b)
            dve.wait_ge(ez_hi, st.lin(a, b + 1))
            nc.vector.tensor_tensor(ez[p][1], emap[:, st.lin(a, b), :], ez[p][0].bitcast(F32), ALU.subtract)\
                .then_inc(z_ready, 1)

        z_rest(Step(0), 1, 0)

        def third(st, last=False):
            z_rest(st, 2, 1)
            hots(dve, dc, 1, st)
            if st.s >= 1:
                walk_dve(dve, st, 2, DOWN0 - 1)
            if not last:
                z_rest(st, 2, 2)
            walk_dve(dve, st, 2, DOWN0)
            if st.s >= 1:
                take_gates(dve, 1, prev(st))

        steps(dve, dc, 0, NB - 1, 6, third, first=1, per=2)
        third(Step(NB - 1), last=True)
        take_gates(dve, 1, Step(NB - 1))

        def fourth(st):
            z_rest(st, 1, 0)
            walk_dve(dve, st, 1, DOWN0 - 1)

        steps(dve, None, HALF, NKEY - RING, 6, fourth)
        for n in range(NKEY - RING, NKEY):
            fourth(Step(n))
        dve.wait_ge(chunk_done, NCH)

    HP = {0: 0, 1: 4, 2: 8, 3: 12, 5: 16, 6: 20}

    with nc.Block() as block:
        @block.sync
        def _(sp):
            sp.dma_start(x[:, :, :], xT).then_inc(s_x, 16)
            sp.dma_start(tabs[:, :], par).then_inc(s_par, 16)
            stream_all(sp)
            for k in range(0, KD, 2):
                sp.wait_ge(x_normed, KD + k + 2)
                sp.dma_start(y[:, k:k + 2, :], x[:, k:k + 2, :]).then_inc(s_y, 16)
            sp.wait_ge(s_y, 16 * KD // 2)

        @block.gpsimd
        def _(pool):
            nc.gpsimd.memset(ones[:, :], 1.0).then_inc(s_ones, 1)
            pool.dma_start(wg_s, wg).then_inc(s_small, 16)
            range_pool(pool, 0, CH["wo"] + RING)
            pool.wait_ge(rope_done, 16)
            heads_pool(pool, HB["moba"], 16, lambda st: heads[:, st.lin(1), :])
            range_pool(pool, CH["wo"] + RING, CH["ffn1"] + RING)
            pool.wait_ge(chunk_done, CH["ffn1"])
            pool.dma_start(wk_s, wcmpk).then_inc(s_cmp, 16)
            pool.dma_start(wv_s, wcmpv).then_inc(s_cmp, 16)
            pool.dma_start(pe_s, peT).then_inc(s_cmp, 16)
            pool.dma_start(alibi, alibi_t).then_inc(s_cmp, 16)
            range_pool(pool, CH["ffn1"] + RING, CH["merge"] + RING)
            hg_pool(pool)
            range_pool(pool, CH["merge"] + RING, CH["pq"] + RING)
            pool.wait_ge(chunk_done, CH["pq"])
            nc.gpsimd.memset(keys_s, 0.0).then_inc(keys_zeroed, 1)
            pool.wait_ge(keys_zeroed, 1)
            pool.dma_start(keys_s[0:HD, 0:NKEY], subk[0, :, :]).then_inc(s_keys, 16)
            pool.dma_start(keys_s[HD:P, NKEY:2 * NKEY], subk[1, :, :]).then_inc(s_keys, 16)
            range_pool(pool, CH["pq"] + RING, UP0)
            range_pool(pool, UP0, NCH)

        @block.tensor
        def _(pe):
            pe.wait_ge(s_ones, 1)
            norm_pe(pe, 0)
            gated_pe(pe, "sc", KD, 3, 6, z_full, 0, HP[0])
            norm_pe(pe, 4)
            gated_pe(pe, "ffn0", NF, 2, 2, conv_u_done, 0, HP[1])
            norm_pe(pe, 8)
            pe.wait_ge(s_con, 16)
            qk_pe(pe)
            tokens_pe(pe, "qkv", 8, skip=16)
            pe.wait_ge(tile_copied, 24)
            heads_pe(pe, HB["moba"], 16, lambda st: heads[:, st.lin(1, 16), :],
                     lambda st, c: vtok[:, c, bass.ds(st.lin(HD), HD)])
            pe.wait_ge(o_read, 16)
            turn_out_pe(pe, 0)
            wo_pe(pe)
            norm_pe(pe, 12)
            gated_pe(pe, "ffn1", NF, 2, 2, conv_u_done, NF, HP[3])
            norm_pe(pe, 16)
            norm_pe(pe, 20)
            gates_pe(pe)
            project_pe(pe, "p_split", 16, hb=HP[5])
            tokens_pe(pe, "p_tok", 6)
            cmp_pe(pe)
            pe.wait_ge(cmp_dve_s, 5)
            pe.wait_ge(tile_copied, TC["p_feat"] + 16)
            stick_pe(pe, HB["sb"], 8, lambda st: heads[:, st.s, :], lambda st: heads[:, st.lin(1, 8), :],
                     lambda st, c: vtok[:, c, bass.ds(st.lin(HD), HD)])
            heads_pe(pe, HB["nsa"], 16, lambda st: heads[:, NSA[st.s // 4][2], :],
                     lambda st, c: vtok[:, c, NSA[st.s // 4][3]:NSA[st.s // 4][3] + HD],
                     q=lambda st: heads[:, 16 + NSA[st.s // 4][0] + st.s % 4, :])
            pe.wait_ge(o_read, HB["end"])
            turn_out_pe(pe, 4)
            hg_pe(pe)
            merge_pe(pe)
            norm_pe(pe, 24)
            project_pe(pe, "pq", KD, hb=HP[6])
            peer_scores_pe(pe)
            peer_pe(pe)
            norm_pe(pe, 28)

        @block.scalar
        def _(act):
            ac = Chain(act, act_c)
            norm_act(act, 0, s_x, 16, HP[0], "x", first_chunks=RING)
            sc_act(act)
            norm_act(act, 1, x_part, 0, HP[1])
            ffn_act(act, "ffn0", 0)
            norm_act(act, 2, x_part, 4, HP[2])
            qk_act(act)
            tokens_act(act, "qkv", 8, skip=16)
            soft_act(act, HB["moba"], 16)
            turn_out_act(act, 0)
            range_act(act, CH["wo"], CH["ffn1"])
            norm_act(act, 3, x_part, 8, HP[3])
            ffn_act(act, "ffn1", NF)
            norm_act(act, 4, x_part, 12)
            norm_act(act, 5, x_normed, 0, HP[5], "tile")
            gates_act(act)
            project_act(act, ac, "p_split", 16, copy_heads, heads)
            tokens_act(act, "p_tok", 6)
            cmp_act(act, ac)
            stick_act(act, ac, HB["sb"], 8)
            soft_act(act, HB["nsa"], 16, loop=False)
            turn_out_act(act, 4)
            hg_act(act)
            merge_act(act)
            norm_act(act, 6, x_part, 16, HP[6])
            project_act(act, ac, "pq", KD, copy_feat, t_q)
            peer_top_act(act)
            peer_act(act)
            norm_act(act, 7, x_part, 20)

        @block.vector
        def _(dve):
            dc = Chain(dve, dve_c)
            for c in range(RING):
                split_lo(dve, nc.vector, Step(c), 1, 0)
            dve.wait_ge(s_par, 16)
            norm_dve(dve, dc, 0, "mix0", HP[0])
            sc_dve(dve, dc)
            residual_dve(dve, dc)
            norm_dve(dve, dc, 1, "ffn0", HP[1])
            ffn_dve(dve, dc, "ffn0", "fconv0", 0)
            residual_dve(dve, dc)
            norm_dve(dve, dc, 2, "mix1", HP[2])
            dve.wait_ge(s_con, 16)
            qk_dve(dve, dc)
            range_dve(dve, CH["qkv"] + 16, CH["wo"])
            soft_dve(dve, dc, HB["moba"], 16, lambda st: con_("causal"), rows_soft)
            turn_out_dve(dve, 0)
            range_dve(dve, CH["wo"], CH["ffn1"])
            dve.wait_ge(chunk_done, CH["ffn1"])
            residual_dve(dve, dc)
            norm_dve(dve, dc, 3, "ffn1", HP[3])
            ffn_dve(dve, dc, "ffn1", "fconv1", NF)
            residual_dve(dve, dc)
            norm_dve(dve, dc, 4, "fin1")
            norm_dve(dve, dc, 5, "mix2", HP[5])
            range_dve(dve, CH["p_split"], CH["p_feat"])
            cmp_dve(dve, dc)
            stick_dve(dve, dc, HB["sb"], 8, rows_stick)
            dve.wait_ge(o_read, HB["nsa"])
            soft_dve(dve, dc, HB["nsa"], 16, lambda st: alibi[:, NSA[st.s // 4][0] + st.s % 4, :], rows_nsa(dc),
                     loop=False)
            turn_out_dve(dve, 4)
            hg_dve(dve, dc)
            merge_dve(dve, dc)
            residual_dve(dve, dc)
            norm_dve(dve, dc, 6, "ffn2", HP[6])
            range_dve(dve, CH["pq"], UP0 - RING)
            range_dve(dve, UP0 - RING, UP0)
            peer_dve(dve, dc)
            residual_dve(dve, dc)
            norm_dve(dve, dc, 7, "fin2")


def constants():
    c = np.zeros((P, NCON), np.float32)

    def put(name, a):
        a = np.asarray(a, np.float32).reshape(P, -1)
        c[:, COFF[name]:COFF[name] + a.shape[1]] = a

    p = np.arange(P)
    put("ident", np.eye(P))
    swap = np.zeros((P, P))
    swap[p ^ 32, p] = 1.0
    put("swap", swap)
    half = HD // 2
    inv = (10000.0 ** (-np.arange(half, dtype=np.float32) / np.float32(half))).astype(np.float32)
    ang = inv[p % half][:, None] * np.arange(T, dtype=np.float32)[None, :]
    ang = ang.astype(np.float32)
    put("cos", np.cos(ang))
    put("sin", np.sin(ang) * np.where(p % HD < half, -1.0, 1.0)[:, None])
    t = np.concatenate([np.broadcast_to(p[:, None], (P, P)), np.broadcast_to(p[:, None] + P, (P, T))], 1)
    k = np.concatenate([np.broadcast_to(np.arange(P)[None], (P, P)), np.broadcast_to(np.arange(T)[None], (P, T))], 1)
    put("causal", np.where(k <= t, 0.0, NEG))
    put("strict", np.where(k < t, 0.0, NEG))
    slopes = 2.0 ** (-(np.arange(8) + 1.0))
    tok = p[:, None, None, None] + P * np.arange(2)[None, None, :, None]
    dist = tok - (16 * np.arange(CMP)[None, None, None, :] + 31)
    ok = (dist >= 0) & (np.arange(CMP) < CMP - 1)
    put("cmpbias", np.where(ok, -slopes[None, :, None, None] * dist, NEG))
    put("rowok", (p[:, None] + P * np.arange(2)[None] >= 31) * 1.0)
    put("pairs", np.stack([p[:, None] // L == p[None] // L for L in LEVELS[1:-1]], 1) * 1.0)
    put("iota", np.broadcast_to(np.arange(P), (P, P)))
    put("iota16", np.broadcast_to(np.arange(TOPK), (P, TOPK)))
    alibi = np.stack([np.where(k <= t, -s * (t - k), NEG) for s in slopes], 1).astype(np.float32)
    return c, alibi


def up_chunks(w, cols):
    w = w[:, cols] if not isinstance(cols, slice) or cols != slice(None) else w
    n = w.shape[1] // P
    return w.reshape(KD, P, n, P).transpose(2, 1, 0, 3).reshape(n, P, D)


def token_chunks(w):
    n = w.shape[1] // T
    return w.reshape(2, 4, P, n, T).transpose(3, 0, 2, 1, 4).reshape(2 * n, P, D)


def interleave(ups, downs):
    out = []
    for j in range(len(ups)):
        out += list(ups[j])
        if j:
            out.append(downs[j - 1])
    return out + [downs[-1]]


def lay_out(a):
    w = {k: np.asarray(v) for k, v in a.items()}
    s = []
    b = up_chunks(w["sc_w_in"][0], slice(None))
    s += interleave([(b[j], b[KD + j], b[2 * KD + j]) for j in range(KD)], w["sc_w_out"][0].reshape(KD, P, D))

    def ffn(i):
        b = up_chunks(w["ffn_w_up"][i], slice(None))
        return interleave([(b[j], b[NF + j]) for j in range(NF)], w["ffn_w_down"][i].reshape(NF, P, D))

    s += ffn(0)
    s += list(up_chunks(w["moba_w_qkv"][0], slice(0, 2 * D)))
    s += list(token_chunks(w["moba_w_qkv"][0][:, 2 * D:]))
    s += list(w["moba_w_o"][0].reshape(KD, P, D))
    s += ffn(1)
    win = w["w_in_2"][0]
    kv = 2048
    hg = kv + 768 + 24
    s += list(up_chunks(win[:, 0:1024], slice(None)))
    s += list(up_chunks(win[:, 1536:2048], slice(None)))
    for i in (0, 1, 2, 4):
        s += list(up_chunks(win[:, kv + i * P:kv + i * P + P], slice(None)))
    s += list(token_chunks(win[:, 1024:1536]))
    s += list(token_chunks(np.concatenate([win[:, kv + i * P:kv + i * P + P] for i in (3, 5)], 1)))
    s += list(up_chunks(win[:, hg:hg + 2048], slice(None)))
    gm = up_chunks(win[:, hg + 2048:], slice(None))
    br = [w[n][0].reshape(4, P, KD, P).transpose(2, 1, 0, 3).reshape(KD, P, 4 * P)
          for n in ("w_branch_sb_2", "w_branch_nsa_2", "w_branch_hgrn_2")]
    pad = np.zeros((P, 4 * P), np.float32)
    s += interleave([(gm[j], gm[KD + j], np.concatenate([br[0][j], br[1][j]], 1), gm[2 * KD + j],
                      np.concatenate([br[2][j], pad], 1)) for j in range(KD)],
                    w["w_out_2"][0].reshape(KD, P, D))
    s += list(up_chunks(w["peer_w_q_2"][0], slice(None)))
    u = w["peer_u_2"][0].reshape(NKEY, NKEY, KD, P).transpose(0, 3, 2, 1).reshape(NKEY, P, D)
    v = w["peer_v_2"][0].reshape(NKEY, NKEY, D)
    s += list(u) + list(v)
    stream = np.empty((len(s), P, D), np.float32)
    for i, c in enumerate(s):
        stream[i] = c
    par = np.zeros((P, NPAR), np.float32)

    def put(name, a):
        a = a.reshape(P, -1)
        par[:, POFF[name]:POFF[name] + a.shape[1]] = a

    def vec(v):
        return v.reshape(-1, P).T

    def taps(v):
        return v.reshape(3, -1, P).transpose(2, 1, 0)

    for name, v in (("mix0", w["mix_norm"][0]), ("mix1", w["mix_norm"][1]), ("ffn0", w["ffn_norm"][0]),
                    ("ffn1", w["ffn_norm"][1]), ("fin1", w["final_norm"]), ("mix2", w["norm_mix_2"][0]),
                    ("ffn2", w["norm_ffn_2"][0]), ("fin2", w["norm_final_2"]), ("hnorm", w["hgrn_norm_2"][0])):
        put(name, vec(v))
    put("sconv", taps(w["sc_w_conv"][0]))
    put("fconv0", taps(w["ffn_w_conv"][0]))
    put("fconv1", taps(w["ffn_w_conv"][1]))
    return {
        "stream": stream,
        "xT": w["x"][0].T.reshape(KD, P, T).transpose(1, 0, 2),
        "par": par,
        "con": constants()[0],
        "alibi_t": constants()[1],
        "wg": win[:, kv + 768:hg].reshape(KD, P, 24).transpose(1, 0, 2),
        "wcmpk": w["nsa_w_cmp_k_2"][0].reshape(2, 16, HD, HD).transpose(0, 2, 1, 3).reshape(P, 16, HD),
        "wcmpv": w["nsa_w_cmp_v_2"][0].reshape(2, 16, HD, HD).transpose(0, 2, 1, 3).reshape(P, 16, HD),
        "peT": w["nsa_cmp_pe_2"][0].T,
        "subk": w["peer_sub_keys_2"][0].transpose(0, 2, 1),
    }


def kernel(**inputs):
    import concourse.bacc as bacc
    from concourse.bass_utils import run_bass_kernel_spmd as run

    nc = bacc.Bacc("TRN2", target_bir_lowering=False, num_devices=1)
    arrays, args = {}, []
    for name, a in lay_out(inputs).items():
        a = np.ascontiguousarray(a)
        arrays[name] = a
        args.append(nc.dram_tensor(name, a.shape, F32, kind="ExternalInput").ap())
    y = nc.dram_tensor("y", (P, KD, T), F32, kind="ExternalOutput").ap()
    build(nc, *args, y)
    r = run(nc, [arrays], core_ids=[0])
    return r.results[0]["y"].transpose(2, 1, 0).reshape(1, T, D)
```
